# Optimizing a Trainium2 kernel written in Bass

```python
import jax, jax.numpy as jnp
from jax import lax
import numpy as np

D_MODEL = 1024
BATCH = 1
SEQ = 1024
DEPTH = 2
DEC_BATCH = 1
DEC_SEQ = 512
PAST_LEN = 128

GRID_W = 64
Q_BLOCK = 128
EPS = 1e-6
ROPE_THETA = 10000.0
NEG_INF = -1e30
A_HEADS = 8
A_HEAD_DIM = 64
DILATED_CONFIGS = ((128, 1), (512, 4), (2048, 16))
MLA_HEADS = 8
MLA_Q_RANK = 256
MLA_KV_RANK = 128
MLA_NOPE_DIM = 64
MLA_ROPE_DIM = 32
MLA_V_DIM = 64
C_HEADS = 16
C_KV_HEADS = 4
C_HEAD_DIM = 64
A_WIDTH = A_HEADS * A_HEAD_DIM
B_WIDTH = MLA_HEADS * MLA_V_DIM
AB_WIDTH = A_WIDTH + B_WIDTH
SPLIT_AB = list(np.cumsum([A_WIDTH, A_WIDTH, A_WIDTH, MLA_Q_RANK, MLA_KV_RANK, MLA_ROPE_DIM]))
IN_AB = 3 * A_WIDTH + MLA_Q_RANK + MLA_KV_RANK + MLA_ROPE_DIM + AB_WIDTH
C_WIDTH = C_HEADS * C_HEAD_DIM
C_KV_WIDTH = C_KV_HEADS * C_HEAD_DIM
SPLIT_C = list(np.cumsum([C_WIDTH, C_KV_WIDTH, C_KV_WIDTH]))
IN_C = C_WIDTH + 2 * C_KV_WIDTH + C_WIDTH
N_EVEN_LAYERS = (DEPTH + 1) // 2
N_ODD_LAYERS = DEPTH // 2

kernel_name = "hybrid_dilated_mla_axial_gqa_encoder"

def rms_norm(x, g):
    xf = x.astype(jnp.float32)
    y = xf * lax.rsqrt(jnp.mean(xf * xf, axis=-1, keepdims=True) + EPS)
    return (y * g.astype(jnp.float32)).astype(x.dtype)

def rope(x, pos):
    half = x.shape[-1] // 2
    freqs = ROPE_THETA ** (-jnp.arange(half, dtype=jnp.float32) / half)
    ang = pos[:, None] * freqs[None, :]
    cos = jnp.cos(ang)[:, None, :].astype(x.dtype)
    sin = jnp.sin(ang)[:, None, :].astype(x.dtype)
    x1, x2 = x[..., :half], x[..., half:]
    return jnp.concatenate([x1 * cos - x2 * sin, x2 * cos + x1 * sin], axis=-1)

def alibi_slopes(n):
    return 2.0 ** (-8.0 * jnp.arange(1, n + 1, dtype=jnp.float32) / n)

def dilated_window_branch(q, k, v, slopes, window, dilation):
    B, T, H, C = q.shape
    d = dilation
    R = window // (2 * d)
    U = T // d
    nb = -(-U // R)
    Up = nb * R

    def to_classes(x):
        x = x.reshape(B, U, d, H, C)
        return jnp.pad(x, ((0, 0), (0, Up - U), (0, 0), (0, 0), (0, 0)))

    def band(x):
        xp = jnp.pad(to_classes(x), ((0, 0), (R, R), (0, 0), (0, 0), (0, 0)))
        xp = xp.reshape(B, nb + 2, R, d, H, C)
        return jnp.concatenate([xp[:, :-2], xp[:, 1:-1], xp[:, 2:]], axis=2)

    qc = to_classes(q).reshape(B, nb, R, d, H, C)
    kb, vb = band(k), band(v)
    s = jnp.einsum('bnqrhc,bnkrhc->bnrhqk', qc, kb).astype(jnp.float32)
    qi = jnp.arange(R)[:, None]
    ki = jnp.arange(3 * R)[None, :]
    diff = ki - R - qi
    u_key = (jnp.arange(nb)[:, None, None] - 1) * R + ki[None]
    valid = (jnp.abs(diff)[None] <= R) & (u_key >= 0) & (u_key < U)
    dist = (d * jnp.abs(diff)).astype(jnp.float32)
    s = s - slopes[:, None, None] * dist[None]
    s = jnp.where(valid[None, :, None, None], s, NEG_INF)
    m = jnp.max(s, axis=-1)
    p = jnp.exp(s - m[..., None])
    z = jnp.sum(p, axis=-1)
    o = jnp.einsum('bnrhqk,bnkrhc->bnqrhc', p, vb.astype(jnp.float32))
    m = jnp.transpose(m, (0, 1, 4, 2, 3)).reshape(B, Up * d, H)[:, :T]
    z = jnp.transpose(z, (0, 1, 4, 2, 3)).reshape(B, Up * d, H)[:, :T]
    o = o.reshape(B, Up * d, H, C)[:, :T]
    return m, z, o

def block_attention(q, k, v, scale):
    B, T, KH, G, C = q.shape
    nq = T // Q_BLOCK
    qb = jnp.moveaxis(q.reshape(B, nq, Q_BLOCK, KH, G, C), 1, 0)

    def one(qblk):
        s = jnp.einsum('bqhgc,bkhc->bhgqk', qblk, k).astype(jnp.float32) * scale
        p = jax.nn.softmax(s, axis=-1).astype(v.dtype)
        return jnp.einsum('bhgqk,bkhc->bqhgc', p, v)

    o = lax.map(one, qb)
    return jnp.moveaxis(o, 0, 1).reshape(B, T, KH * G, v.shape[-1])

def even_layer(x, g_pre, g_post, w_in, q_a_norm, w_uq, kv_a_norm, w_ukv, w_out):
    B, T, _ = x.shape
    h = rms_norm(x, g_pre)
    proj = jnp.einsum('btd,de->bte', h, w_in)
    qa, ka, va, cq, ckv, kr, gate = jnp.split(proj, SPLIT_AB, axis=-1)
    shp = (B, T, A_HEADS, A_HEAD_DIM)
    qa = qa.reshape(shp) * (A_HEAD_DIM ** -0.5)
    ka = ka.reshape(shp)
    va = va.reshape(shp)
    slopes = alibi_slopes(A_HEADS)
    stats = [dilated_window_branch(qa, ka, va, slopes, wdw, dil) for wdw, dil in DILATED_CONFIGS]
    m_all = jnp.stack([st[0] for st in stats])
    z_all = jnp.stack([st[1] for st in stats])
    o_all = jnp.stack([st[2] for st in stats])
    wts = jnp.exp(m_all - jnp.max(m_all, axis=0, keepdims=True))
    z = jnp.sum(z_all * wts, axis=0)
    o_a = jnp.sum(o_all * wts[..., None], axis=0) / z[..., None]
    out_a = o_a.astype(x.dtype).reshape(B, T, A_WIDTH)
    pos = jnp.arange(T, dtype=jnp.float32)
    cq = rms_norm(cq, q_a_norm)
    qb = jnp.einsum('btr,re->bte', cq, w_uq).reshape(B, T, MLA_HEADS, MLA_NOPE_DIM + MLA_ROPE_DIM)
    q_nope, q_rope = qb[..., :MLA_NOPE_DIM], qb[..., MLA_NOPE_DIM:]
    q_b = jnp.concatenate([q_nope, rope(q_rope, pos)], axis=-1)
    ckv = rms_norm(ckv, kv_a_norm)
    kv = jnp.einsum('btr,re->bte', ckv, w_ukv).reshape(B, T, MLA_HEADS, MLA_NOPE_DIM + MLA_V_DIM)
    k_nope, v_b = kv[..., :MLA_NOPE_DIM], kv[..., MLA_NOPE_DIM:]
    k_rope = jnp.broadcast_to(rope(kr[:, :, None, :], pos), (B, T, MLA_HEADS, MLA_ROPE_DIM))
    k_b = jnp.concatenate([k_nope, k_rope], axis=-1)
    out_b = block_attention(q_b[:, :, :, None, :], k_b, v_b,
                            (MLA_NOPE_DIM + MLA_ROPE_DIM) ** -0.5).reshape(B, T, B_WIDTH)
    y = jnp.concatenate([out_a, out_b], axis=-1) * jax.nn.silu(gate)
    y = jnp.einsum('bte,ed->btd', y, w_out)
    return x + rms_norm(y, g_post)

def odd_layer(x, g_pre, g_post, w_in, q_norm, k_norm, w_out):
    B, T, _ = x.shape
    n_rows = T // GRID_W
    rows = jnp.repeat(jnp.arange(n_rows, dtype=jnp.float32), GRID_W)
    cols = jnp.tile(jnp.arange(GRID_W, dtype=jnp.float32), n_rows)
    half = C_HEAD_DIM // 2
    h = rms_norm(x, g_pre)
    proj = jnp.einsum('btd,de->bte', h, w_in)
    q, k, v, gate = jnp.split(proj, SPLIT_C, axis=-1)
    q = rms_norm(q.reshape(B, T, C_HEADS, C_HEAD_DIM), q_norm)
    k = rms_norm(k.reshape(B, T, C_KV_HEADS, C_HEAD_DIM), k_norm)
    v = v.reshape(B, T, C_KV_HEADS, C_HEAD_DIM)
    q = jnp.concatenate([rope(q[..., :half], rows), rope(q[..., half:], cols)], axis=-1)
    k = jnp.concatenate([rope(k[..., :half], rows), rope(k[..., half:], cols)], axis=-1)
    q = q.reshape(B, T, C_KV_HEADS, C_HEADS // C_KV_HEADS, C_HEAD_DIM)
    o = block_attention(q, k, v, C_HEAD_DIM ** -0.5).reshape(B, T, C_WIDTH)
    y = jnp.einsum('bte,ed->btd', o * jax.nn.silu(gate), w_out)
    return x + rms_norm(y, g_post)

def trunk(x, norm_pre, norm_post, w_in_ab, mla_q_norm, w_uq, mla_kv_norm, w_ukv, w_out_ab,
          w_in_c, c_q_norm, c_k_norm, w_out_c):
    for layer in range(DEPTH):
        i = layer // 2
        if layer % 2 == 0:
            x = even_layer(x, norm_pre[layer], norm_post[layer], w_in_ab[i], mla_q_norm[i], w_uq[i],
                           mla_kv_norm[i], w_ukv[i], w_out_ab[i])
        else:
            x = odd_layer(x, norm_pre[layer], norm_post[layer], w_in_c[i], c_q_norm[i], c_k_norm[i], w_out_c[i])
    return x

def setup_inputs(seed: int = 0) -> dict:
    key = jax.random.key(seed)
    ks = jax.random.split(key, 16)

    def w(k, shape, fan_in):
        return jax.random.normal(k, shape, jnp.float32) * (fan_in ** -0.5)

    def gain(k, shape):
        return 1.0 + 0.05 * jax.random.normal(k, shape, jnp.float32)

    return {
        "x_prompt": jax.random.normal(ks[0], (BATCH, SEQ, D_MODEL), jnp.float32),
        "x_sample": jax.random.normal(ks[1], (DEC_BATCH, DEC_SEQ, D_MODEL), jnp.float32),
        "norm_pre": gain(ks[2], (DEPTH, D_MODEL)),
        "norm_post": gain(ks[3], (DEPTH, D_MODEL)),
        "w_in_ab": w(ks[4], (N_EVEN_LAYERS, D_MODEL, IN_AB), D_MODEL),
        "mla_q_norm": gain(ks[5], (N_EVEN_LAYERS, MLA_Q_RANK)),
        "w_uq": w(ks[6], (N_EVEN_LAYERS, MLA_Q_RANK, MLA_HEADS * (MLA_NOPE_DIM + MLA_ROPE_DIM)), MLA_Q_RANK),
        "mla_kv_norm": gain(ks[7], (N_EVEN_LAYERS, MLA_KV_RANK)),
        "w_ukv": w(ks[8], (N_EVEN_LAYERS, MLA_KV_RANK, MLA_HEADS * (MLA_NOPE_DIM + MLA_V_DIM)), MLA_KV_RANK),
        "w_out_ab": w(ks[9], (N_EVEN_LAYERS, AB_WIDTH, D_MODEL), AB_WIDTH),
        "w_in_c": w(ks[10], (N_ODD_LAYERS, D_MODEL, IN_C), D_MODEL),
        "c_q_norm": gain(ks[11], (N_ODD_LAYERS, C_HEAD_DIM)),
        "c_k_norm": gain(ks[12], (N_ODD_LAYERS, C_HEAD_DIM)),
        "w_out_c": w(ks[13], (N_ODD_LAYERS, C_WIDTH, D_MODEL), C_WIDTH),
    }

def reference(x_prompt, x_sample, norm_pre, norm_post, w_in_ab, mla_q_norm, w_uq, mla_kv_norm, w_ukv,
              w_out_ab, w_in_c, c_q_norm, c_k_norm, w_out_c):
    y_prompt = trunk(x_prompt, norm_pre, norm_post, w_in_ab, mla_q_norm, w_uq, mla_kv_norm, w_ukv,
                     w_out_ab, w_in_c, c_q_norm, c_k_norm, w_out_c)
    y_sample = trunk(x_sample, norm_pre, norm_post, w_in_ab, mla_q_norm, w_uq, mla_kv_norm, w_ukv,
                     w_out_ab, w_in_c, c_q_norm, c_k_norm, w_out_c)
    return (y_prompt, y_sample)


_drawn_inputs = setup_inputs


def setup_inputs(seed=0):
    import zlib

    import numpy as np

    out = dict(_drawn_inputs(seed))
    spreads = {}
    factors = {'mla_q_norm': 3.33}
    for name, (base, spread) in spreads.items():
        noise = np.random.default_rng([zlib.crc32(name.encode()), seed]).standard_normal(out[name].shape)
        drawn = base * np.exp(spread * noise) if base else spread * noise
        out[name] = __import__('jax').numpy.asarray(drawn.astype(out[name].dtype))
    for name, factor in factors.items():
        out[name] = (out[name] * factor).astype(out[name].dtype)
    return out
```

```python
from contextlib import ExitStack

import concourse.bass as bass
from concourse import mybir

F32 = mybir.dt.float32
F32R = mybir.dt.float32r
ALU = mybir.AluOpType
ACT = mybir.ActivationFunctionType
AX_X = mybir.AxisListType.X

P = 128
D = 1024
KT = D // P
SEQ, DEC = 1024, 512
T = SEQ + DEC
CH = 512
NC = T // CH
TT = T // P
EPS = 1e-6
HD = 64
ROPE = 32
BW = 1920
AUG = 8
SWAP16 = [(i + 16) % 32 for i in range(32)]


def ds(start, size):
    return bass.ds(start, size)


def wait_count(eng, sem, value):
    if isinstance(value, int) and value <= 0:
        return
    eng.wait_ge(sem, value)


def wait_apart(eng, sem, value, seen):
    eng.wait_ge(sem, value)
    eng.sem_inc(seen, 1)


def steps(eng, count, body):
    body(0, True, count == 1)
    if count > 2:
        with eng.Fori(1, count - 1) as i:
            body(i, False, False)
    if count > 1:
        body(count - 1, False, True)


class Arena:

    def __init__(self, nc):
        self.nc, self.sems = nc, []

    def sem(self, name):
        self.sems.append(self.nc.alloc_semaphore(name=name))
        return self.sems[-1]

    def recycle(self):
        self.nc.clear_and_free_semaphores(self.sems)
        self.nc.all_engine_barrier()
        self.sems = []

    def scope(self):
        return Scope(self.nc)


class Scope(ExitStack):
    def __init__(self, nc):
        super().__init__()
        self.nc = nc

    def sb(self, name, shape, dtype=F32):
        return self.enter_context(self.nc.sbuf_tensor(name, shape, dtype))

    def banks(self, name, count):
        return self.enter_context(self.nc.psum_tensor(name, [P, count * CH], F32))



def normalise_and_split(nc, ar, tag, Y, XH, XL, ones, epst, src=None):
    loaded = [ar.sem(f"{tag}_loaded{c}") for c in range(NC)]
    sq_ready, sum_ready, sd_ready = ar.sem(f"{tag}_sq"), ar.sem(f"{tag}_sum"), ar.sem(f"{tag}_sd")
    rstd_ready, h_ready = ar.sem(f"{tag}_rstd"), ar.sem(f"{tag}_h")
    hi_ready, lo_ready = ar.sem(f"{tag}_hi"), ar.sem(f"{tag}_lo")
    with ar.scope() as sc:
        sq = [sc.sb(f"{tag}_sqt{i}", [P, CH]) for i in range(2)]
        h = [sc.sb(f"{tag}_ht{i}", [P, CH]) for i in range(2)]
        sd = sc.sb(f"{tag}_sdt", [P, CH])
        rstd = sc.sb(f"{tag}_rstdt", [P, CH])
        ss = sc.banks(f"{tag}_ss", 1)
        block = sc.enter_context(nc.Block())

        @block.sync
        def _(sp):
            if src is not None:
                for c in range(NC):
                    sp.dma_start(Y[:, :, c * CH:(c + 1) * CH],
                                 src.rearrange("(k p) t -> p k t", p=P)[:, :, c * CH:(c + 1) * CH]
                                 ).then_inc(loaded[c], 16)

        @block.scalar
        def _(act):
            for c in range(NC):
                if src is not None:
                    act.wait_ge(loaded[c], 16)
                for k in range(KT):
                    n = c * KT + k
                    wait_count(act, sum_ready, n - 1)
                    nc.scalar.activation(sq[n % 2][:], Y[:, k, c * CH:(c + 1) * CH], ACT.Square
                                         ).then_inc(sq_ready, 1)
                act.wait_ge(sum_ready, (c + 1) * KT)
                wait_count(act, rstd_ready, c)
                nc.scalar.activation(sd[:], ss[:], ACT.Sqrt, bias=epst[:], scale=1.0 / D).then_inc(sd_ready, 1)
                for k in range(KT):
                    n = c * KT + k
                    act.wait_ge(h_ready, n + 1)
                    nc.scalar.activation(XH[:, k, c * CH:(c + 1) * CH], h[n % 2][:], ACT.Copy
                                         ).then_inc(hi_ready, 1)

        @block.tensor
        def _(pe):
            for c in range(NC):
                wait_count(pe, sd_ready, c)
                for k in range(KT):
                    pe.wait_ge(sq_ready, c * KT + k + 1)
                    nc.tensor.matmul(ss[:], ones[:], sq[(c * KT + k) % 2][:], start=(k == 0), stop=(k == KT - 1)
                                     ).then_inc(sum_ready, 1)

        @block.vector
        def _(dve):
            for c in range(NC):
                if src is not None:
                    dve.wait_ge(loaded[c], 16)
                dve.wait_ge(sd_ready, c + 1)
                wait_count(dve, h_ready, c * KT)
                nc.vector.reciprocal(rstd[:], sd[:]).then_inc(rstd_ready, 1)
                dve.wait_ge(rstd_ready, c + 1)
                for k in range(KT):
                    n = c * KT + k
                    wait_count(dve, lo_ready, n - 1)
                    nc.vector.tensor_tensor(h[n % 2][:], Y[:, k, c * CH:(c + 1) * CH], rstd[:], ALU.mult
                                            ).then_inc(h_ready, 1)

        @block.gpsimd
        def _(pool):
            for n in range(NC * KT):
                c, k = n // KT, n % KT
                pool.wait_ge(hi_ready, n + 1)
                nc.gpsimd.tensor_tensor(XL[:, k, c * CH:(c + 1) * CH], h[n % 2][:],
                                        XH[:, k, c * CH:(c + 1) * CH].bitcast(F32), ALU.subtract
                                        ).then_inc(lo_ready, 1)



def project(nc, ar, tag, XH, XL, tiles, gain, groups, values=None, Yout=None, sel=None, epst=None, before=None):
    NT = sum(g[2] for g in groups)
    raw_in = [ar.sem(f"{tag}_w_in{i}") for i in range(2)]
    w_scaled, w_hi, w_ready = ar.sem(f"{tag}_w_scaled"), ar.sem(f"{tag}_w_hi"), ar.sem(f"{tag}_w_ready")
    acc_ready = ar.sem(f"{tag}_acc_ready")
    acc_read = {g[1]: ar.sem(f"{tag}_acc_read{g[1]}") for g in groups}
    if values:
        acc_read[NT] = ar.sem(f"{tag}_acc_read_v")
    v_used = ar.sem(f"{tag}_v_used")
    hi_ready = ar.sem(f"{tag}_hi_ready")
    stored = [ar.sem(f"{tag}_stored{i}") for i in range(3)]
    g_exp, g_one, g_rcp = ar.sem(f"{tag}_g_exp"), ar.sem(f"{tag}_g_one"), ar.sem(f"{tag}_g_rcp")
    has_qk = any(g[0] == "qk" for g in groups)
    if has_qk:
        q_raw, q_sum, q_sd, q_rstd = (ar.sem(f"{tag}_q_{x}") for x in ("raw", "sum", "sd", "rstd"))
        q_sw, q_cos, q_sin, q_rot, q_done, q_lo, q_seen = (
            ar.sem(f"{tag}_q_{x}") for x in ("sw", "cos", "sin", "rot", "done", "lo", "seen"))
    hi0, qk0, nh, nq = {}, {}, 0, 0
    for kind, t0, nt, _ in groups:
        hi0[t0], qk0[t0] = nh, nq
        nh += 3 * nt if kind in ("split", "qk") else 0
        nq += 3 * nt if kind == "qk" else 0
    vhi0 = nh
    VU = KT if values else 0

    with ar.scope() as sc:
        raw = [sc.sb(f"{tag}_raw{i}", [P, D]) for i in range(2)]
        wg = sc.sb(f"{tag}_wg", [P, D])
        wh = [sc.sb(f"{tag}_wh{i}", [P, D], F32R) for i in range(2)]
        wl = [sc.sb(f"{tag}_wl{i}", [P, D], F32R) for i in range(2)]
        sh = [sc.sb(f"{tag}_sh{i}", [P, CH]) for i in range(3)] if Yout is None else None
        if Yout is None:
            sl = [sc.sb(f"{tag}_sl{i}", [P, CH]) for i in range(3)]
            ta = [sc.sb(f"{tag}_ta{i}", [P, CH]) for i in range(3)]
            tb = [sc.sb(f"{tag}_tb{i}", [P, CH]) for i in range(3)]
        if has_qk:
            tsq = [sc.sb(f"{tag}_tsq{i}", [P, CH]) for i in range(2)]
            tsd = [sc.sb(f"{tag}_tsd{i}", [P, CH]) for i in range(2)]
        acc = sc.banks(f"{tag}_acc", 6)
        ssb = sc.banks(f"{tag}_ssb", 2)
        bank = [acc[:, i * CH:(i + 1) * CH] for i in range(6)]
        sums = [ssb[:, i * CH:(i + 1) * CH] for i in range(2)]
        block = sc.enter_context(nc.Block())

        def cols(c):
            return slice(c * CH, (c + 1) * CH)

        @block.sync
        def _(sp):
            def load(t, b):
                wait_count(sp, w_ready, t - 1)
                sp.dma_start(raw[b][:], tiles[ds(t, 1), :, :].rearrange("a p n -> p (a n)")
                             ).then_inc(raw_in[b], 16)

            load(0, 0)
            load(1, 1)
            for kind, t0, nt, opt in groups:
                final = t0 + nt == NT

                def pair(i, first, last):
                    for b in range(2):
                        tl = i * 2 + b
                        t = tl + t0
                        if not (final and last):
                            load(t + 2, b)
                        for c in range(NC):
                            rows = ds(tl * P, P)
                            if kind == "qk":
                                sp.wait_ge(q_lo, tl * 3 + (qk0[t0] + c + 1))
                            elif kind != "keep":
                                sp.wait_ge(acc_read[t0], tl * 3 + (c + 1))
                            if kind in ("split", "qk"):
                                sp.dma_start(opt["hi"][rows, cols(c)], sh[c][:]).then_inc(stored[c], 16)
                                sp.dma_start(opt["lo"][rows, cols(c)], sl[c][:]).then_inc(stored[c], 16)
                            elif kind in ("raw", "gate"):
                                sp.dma_start(opt["out"][rows, cols(c)], sh[c][:]).then_inc(stored[c], 32)
                steps(sp, nt // 2, pair)
            if values:
                W = values["w"].shape[2]
                nhd = values["heads"]

                def store_half(half):
                    for i in range(6 * half, 6 * half + 6):
                        sp.wait_ge(acc_read[NT], i + 1)
                        for part, stage in (("hi", sh), ("lo", sl)):
                            sp.dma_start(values[part].rearrange("h p i d -> p h i d")[:, :, i, :],
                                         stage[i % 3][:, 0:nhd * HD].rearrange("p (h d) -> p h d", d=HD)
                                         ).then_inc(stored[i % 3], 16)

                for u in range(VU):
                    b = (NT + u) % 2
                    sp.wait_ge(w_ready, NT + u - 1)
                    sp.dma_start(raw[b][:, 0:W], values["w"][u % (VU // 2)]).then_inc(raw_in[b], 16)
                    if u == VU // 2 + 1:
                        store_half(0)
                store_half(1)
            if Yout is None:
                for c in range(3):
                    sp.wait_ge(stored[c], 32 * (NT + (TT // 3 if values else 0)))

        @block.gpsimd
        def _(pool):
            def split(t, b, w, g, counts, free_sem=acc_ready):
                def v(x):
                    return x[:, 0:w].rearrange("p (k n) -> p k n", k=g.shape[1])
                gb = g.unsqueeze(2).to_broadcast([P, g.shape[1], w // g.shape[1]])
                pool.wait_ge(raw_in[b], counts[1])
                wait_count(pool, free_sem, counts[0])
                nc.gpsimd.tensor_tensor(v(wh[b]), v(raw[b]), gb, ALU.mult).then_inc(w_hi, 1)
                wait_count(pool, w_ready, t)
                nc.gpsimd.tensor_tensor(v(wg), v(raw[b]), gb, ALU.mult).then_inc(w_scaled, 1)
                pool.wait_ge(w_hi, t + 1)
                pool.wait_ge(w_scaled, t + 1)
                nc.gpsimd.tensor_tensor(wl[b][:, 0:w], wg[:, 0:w], wh[b][:, 0:w].bitcast(F32), ALU.subtract
                                        ).then_inc(w_ready, 1)

            split(0, 0, D, gain[:, 0:KT], (0, 16))
            for kind, t0, nt, opt in groups:
                final = t0 + nt == NT

                def pair(i, first, last):
                    for b in range(2):
                        tl = i * 2 + b
                        if not (final and last and b == 1):
                            split(tl + (t0 + 1), 1 - b, D, gain[:, 0:KT],
                                  (tl * 3 + 3 * t0, i * 16 + (16 * (t0 // 2 + b) + 16)))
                        for c in range(NC if kind == "qk" else 0):
                            m = tl * 3 + (qk0[t0] + c)
                            pc = slice((c * CH) % SEQ, (c * CH) % SEQ + CH)
                            pool.wait_ge(q_sw, m + 1)
                            nc.gpsimd.tensor_tensor(ta[c][:], ta[c][:], opt["cos"][:, pc], ALU.mult
                                                    ).then_inc(q_cos, 1)
                            nc.gpsimd.tensor_tensor(tb[c][:], tb[c][:], opt["sin"][:, pc], ALU.mult
                                                    ).then_inc(q_sin, 1)
                steps(pool, nt // 2, pair)
            for u in range(VU):
                W = values["w"].shape[2]
                if u < 2:
                    free = (acc_ready, 3 * (NT + u) - 3)
                elif (u - 2) % (VU // 2) == VU // 2 - 1:
                    free = (acc_ready, 3 * NT + 6 * ((u - 2) // (VU // 2) + 1))
                else:
                    free = (v_used, u - 1 - (u - 2) // (VU // 2))
                ku = 2 * (u % (VU // 2))
                split(NT + u, (NT + u) % 2, W, gain[:, ku:ku + 2], (free[1], 16 * ((NT + u) // 2) + 16), free[0])

        @block.tensor
        def _(pe):
            if before is not None:
                before(pe)

            def bank_free(t0, n):
                if isinstance(n, int) and n < 6:
                    before = [g for g in groups if g[1] < t0]
                    if before:
                        pe.wait_ge(acc_read[before[-1][1]], 3 * before[-1][2] + n - 5)
                else:
                    pe.wait_ge(acc_read[t0], n - 5)

            def head_sums(m, slot, t0, n_read):
                pe.wait_ge(acc_read[t0], n_read)
                wait_count(pe, q_sd, m - 1)
                nc.tensor.matmul(sums[slot], sel[:], tsq[slot][:], start=True, stop=True).then_inc(q_sum, 1)

            for kind, t0, nt, opt in groups:
                def pair(i, first, last):
                    for b in range(2):
                        tl = i * 2 + b
                        t = tl + t0
                        pe.wait_ge(w_ready, t + 1)
                        for c in range(NC):
                            bank_free(t0, tl * 3 + c)
                            out = bank[3 * b + c]
                            for k in range(KT):
                                ks = slice(k * P, (k + 1) * P)
                                for j, (w, x) in enumerate(((wh[b], XH), (wh[b], XL), (wl[b], XH))):
                                    last_mm = nc.tensor.matmul(out, w[:, ks], x[:, k, cols(c)],
                                                               start=(k == 0 and j == 0),
                                                               stop=(k == KT - 1 and j == 2))
                            last_mm.then_inc(acc_ready, 1)
                            if kind == "qk" and not (first and b == 0 and c == 0):
                                head_sums(tl * 3 + (qk0[t0] + c - 1), (3 * b + c - 1) % 2, t0, tl * 3 + c)
                    if kind == "qk" and last:
                        head_sums(qk0[t0] + 3 * nt - 1, 1, t0, 3 * nt)
                assert t0 % 2 == 0 and nt % 2 == 0
                steps(pe, nt // 2, pair)
            if values:
                W = values["w"].shape[2] // 2
                for u in range(VU):
                    half, ku = u // (VU // 2), 2 * (u % (VU // 2))
                    b = (NT + u) % 2
                    pe.wait_ge(w_ready, NT + u + 1)
                    for i in range(6):
                        if ku == 0:
                            bank_free(NT, 6 * half + i)
                        tok = slice((6 * half + i) * P, (6 * half + i + 1) * P)
                        for kk in range(2):
                            ws = slice(kk * W, (kk + 1) * W)
                            for j, (x, w) in enumerate(((XH, wh[b]), (XL, wh[b]), (XH, wl[b]))):
                                last_mm = nc.tensor.matmul(bank[i][:, 0:W], x[:, ku + kk, tok], w[:, ws],
                                                           start=(ku + kk + j == 0),
                                                           stop=(ku + kk == KT - 1 and j == 2))
                        if ku == KT - 2:
                            last_mm.then_inc(acc_ready, 1)
                    if ku != KT - 2:
                        last_mm.then_inc(v_used, 1)

        @block.scalar
        def _(act):
            for kind, t0, nt, opt in groups:
                scale = opt.get("scale", 1.0)
                if kind == "gate" and nq:
                    act.wait_ge(q_lo, nq)

                def sd(m, slot):
                    act.wait_ge(q_sum, m + 1)
                    wait_count(act, q_done, m - 1)
                    nc.scalar.activation(tsd[slot][:], sums[slot], ACT.Sqrt, bias=epst[:], scale=1.0 / HD
                                         ).then_inc(q_sd, 1)

                def hi(m, c, uses, nhi):
                    act.wait_ge(q_done, m + 1)
                    wait_count(act, stored[c], uses)
                    nc.scalar.activation(sh[c][:].bitcast(F32R), ta[c][:], ACT.Copy).then_inc(hi_ready, 1)

                def pair(i, first, last):
                    for b in range(2):
                        tl = i * 2 + b
                        t = tl + t0
                        for c in range(NC):
                            src = bank[3 * b + c]
                            act.wait_ge(acc_ready, t * 3 + (c + 1))
                            m = tl * 3 + (qk0[t0] + c)
                            if kind == "keep":
                                nc.scalar.activation(Yout[:, ds(t, 1), cols(c)].rearrange("p a n -> p (a n)"), src,
                                                     ACT.Copy).then_inc(acc_read[t0], 1)
                            elif kind == "raw":
                                wait_count(act, stored[c], t * 32)
                                nc.scalar.activation(sh[c][:], src, ACT.Copy).then_inc(acc_read[t0], 1)
                            elif kind == "split":
                                wait_count(act, stored[c], t * 32)
                                nc.scalar.activation(sh[c][:].bitcast(F32R), src, ACT.Copy, scale=scale
                                                     ).then_inc(hi_ready, 1)
                            elif kind == "gate":
                                wait_count(act, g_rcp, tl * 3 + (c - 2))
                                nc.scalar.activation(ta[c][:], src, ACT.Exp, scale=-1.0).then_inc(g_exp, 1)
                            elif kind == "qk":
                                wait_count(act, q_lo, m - 2)
                                nc.scalar.activation(ta[c][:], src, ACT.Copy).then_inc(q_raw, 1)
                                wait_count(act, q_sum, m - 1)
                                nc.scalar.activation(tsq[(3 * b + c) % 2][:], src, ACT.Square
                                                     ).then_inc(acc_read[t0], 1)
                                lag = 3 * b + c
                                if not (first and lag < 1):
                                    sd(m - 1, (lag - 1) % 2)
                                if not (first and lag < 2):
                                    hi(m - 2, (c - 2) % 3, (t if c >= 2 else t - 1) * 32, m - 2)
                    if kind == "qk" and last:
                        mm = qk0[t0] + 3 * nt
                        sd(mm - 1, 1)
                        hi(mm - 2, 1, (t0 + nt - 1) * 32, mm - 2)
                        hi(mm - 1, 2, (t0 + nt - 1) * 32, mm - 1)
                steps(act, nt // 2, pair)
            if values:
                for i in range(TT):
                    W = values["w"].shape[2] // 2
                    act.wait_ge(acc_ready, 3 * NT + i + 1)
                    act.wait_ge(stored[i % 3], 32 * (NT + i // 3))
                    nc.scalar.activation(sh[i % 3][:, 0:W].bitcast(F32R), bank[i % 6][:, 0:W], ACT.Copy
                                         ).then_inc(hi_ready, 1)

        @block.vector
        def _(dve):
            for kind, t0, nt, opt in groups:
                scale = opt.get("scale", 1.0)

                def norm_rope(m, c, slot):
                    dve.wait_ge(q_sd, m + 1)
                    nc.vector.reciprocal(tsd[slot][:], tsd[slot][:]).then_inc(q_rstd, 1)
                    dve.wait_ge(q_sin, m + 1)
                    dve.wait_ge(q_cos, m + 1)
                    nc.vector.tensor_tensor(ta[c][:], ta[c][:], tb[c][:], ALU.add).then_inc(q_rot, 1)
                    dve.wait_ge(q_rot, m + 1)
                    dve.wait_ge(q_rstd, m + 1)
                    nc.vector.tensor_tensor(ta[c][:], ta[c][:], tsd[slot][:], ALU.mult).then_inc(q_done, 1)

                def lo(m, c):
                    dve.wait_ge(hi_ready, hi0[t0] - qk0[t0] + m + 1)
                    dve.wait_ge(q_done, m + 1)
                    nc.vector.tensor_tensor(sl[c][:].bitcast(F32R), ta[c][:], sh[c][:], ALU.subtract
                                            ).then_inc(q_lo, 1)

                def pair(i, first, last):
                    for b in range(2):
                        tl = i * 2 + b
                        t = tl + t0
                        for c in range(NC):
                            src = bank[3 * b + c]
                            m = tl * 3 + (qk0[t0] + c)
                            if kind == "split":
                                dve.wait_ge(hi_ready, tl * 3 + (hi0[t0] + c + 1))
                                nc.vector.scalar_tensor_tensor(out=sl[c][:].bitcast(F32R), in0=src, scalar=scale,
                                                               in1=sh[c][:], op0=ALU.mult, op1=ALU.subtract
                                                               ).then_inc(acc_read[t0], 1)
                            elif kind == "gate":
                                g = tl * 3 + (c + 1)
                                dve.wait_ge(g_exp, g)
                                nc.vector.tensor_scalar(ta[c][:], ta[c][:], 1.0, None, ALU.add).then_inc(g_one, 1)
                                dve.wait_ge(g_one, g)
                                nc.vector.reciprocal(tb[c][:], ta[c][:]).then_inc(g_rcp, 1)
                                dve.wait_ge(g_rcp, g)
                                wait_count(dve, stored[c], t * 32)
                                nc.vector.tensor_tensor(sh[c][:], src, tb[c][:], ALU.mult).then_inc(acc_read[t0], 1)
                            elif kind == "qk":
                                lag = 3 * b + c
                                wait_apart(dve, q_raw, m + 1, q_seen)
                                nc.vector.stream_shuffle(tb[c][:], ta[c][:], SWAP16).then_inc(q_sw, 1)
                                if not (first and lag < 2):
                                    lo(m - 2, (c - 2) % 3)
                                if not (first and lag < 1):
                                    norm_rope(m - 1, (c - 1) % 3, (lag - 1) % 2)
                    if kind == "qk" and last:
                        mm = qk0[t0] + 3 * nt
                        norm_rope(mm - 1, 2, 1)
                        lo(mm - 2, 1)
                        lo(mm - 1, 2)
                if kind in ("split", "gate", "qk"):
                    steps(dve, nt // 2, pair)
            if values:
                for i in range(TT):
                    W = values["w"].shape[2] // 2
                    dve.wait_ge(hi_ready, vhi0 + i + 1)
                    nc.vector.tensor_tensor(sl[i % 3][:, 0:W].bitcast(F32R), bank[i % 6][:, 0:W],
                                            sh[i % 3][:, 0:W], ALU.subtract).then_inc(acc_read[NT], 1)


def latent_projections(nc, ar, S, A, ones, epst):
    scale = float(HD + ROPE) ** -0.5
    W3 = [("q", h, c) for h in range(8) for c in range(NC)] + [("k", j, c) for j in range(4) for c in range(NC)] \
        + [("v", i, 0) for i in range(TT)]
    units = [("r", 0, c) for c in range(NC)] + W3
    lat_in = [ar.sem(f"l_in{c}") for c in range(NC)]
    w_in, tab_in = ar.sem("l_w_in"), ar.sem("l_tab_in")
    sq_ready, sum_ready, sd_ready, rstd_ready = (ar.sem(f"l_{x}") for x in ("sq", "sum", "sd", "rstd"))
    n_ready, n_hi, n_lo = ar.sem("l_n"), ar.sem("l_n_hi"), ar.sem("l_n_lo")
    w_mul, w_hi, w_lo = ar.sem("l_w_mul"), ar.sem("l_w_hi"), ar.sem("l_w_lo")
    mm_done, u_raw, u_sw, u_cos, u_sin, u_rot, u_hi, u_lo = (
        ar.sem(f"l_u_{x}") for x in ("mm", "raw", "sw", "cos", "sin", "rot", "hi", "lo"))
    stored = [ar.sem(f"l_stored{i}") for i in range(3)]
    roped = {u: sum(x[0] in "qr" for x in units[:u]) for u in range(len(units) + 1)}
    with ar.scope() as sc:
        L = sc.sb("l_L", [P, 4, T])
        CH_ = sc.sb("l_ch", [P, 3, T], F32R)
        CL_ = sc.sb("l_cl", [P, 3, T], F32R)
        wr = sc.sb("l_wr", [P, 2560])
        wh = sc.sb("l_wh", [P, 2560], F32R)
        wl = sc.sb("l_wl", [P, 2560], F32R)
        g = sc.sb("l_g", [P, 3])
        cos, sin = sc.sb("l_cos", [P, SEQ]), sc.sb("l_sin", [P, SEQ])
        sq = [sc.sb(f"l_sq{i}", [P, CH]) for i in range(2)]
        sd = sc.sb("l_sd", [P, 2, CH])
        nt_ = [sc.sb(f"l_nt{i}", [P, CH]) for i in range(2)]
        ta = [sc.sb(f"l_ta{i}", [P, CH]) for i in range(3)]
        tb = [sc.sb(f"l_tb{i}", [P, CH]) for i in range(3)]
        sh = [sc.sb(f"l_sh{i}", [P, CH]) for i in range(3)]
        sl = [sc.sb(f"l_sl{i}", [P, CH]) for i in range(3)]
        acc = sc.banks("l_acc", 6)
        ssb = sc.banks("l_ssb", 2)
        bank = [acc[:, i * CH:(i + 1) * CH] for i in range(6)]
        sums = [ssb[:, i * CH:(i + 1) * CH] for i in range(2)]
        block = sc.enter_context(nc.Block())

        def cols(c):
            return slice(c * CH, (c + 1) * CH)

        def rows(kind):
            return {"q": slice(0, 96), "k": slice(0, P), "v": slice(0, P), "r": slice(64, 96)}[kind]

        @block.sync
        def _(sp):
            for c in range(NC):
                sp.dma_start(L[:, :, cols(c)], S["latent"].rearrange("(k p) t -> p k t", p=P)[:, :, cols(c)]
                             ).then_inc(lat_in[c], 16)
            sp.dma_start(wr[:, 0:1536].rearrange("p (k n) -> p k n", k=2),
                         A["w_uq"].rearrange("(k p) n -> p k n", p=P)).then_inc(w_in, 16)
            sp.dma_start(wr[:, 1536:2560], A["w_ukv"]).then_inc(w_in, 16)
            sp.dma_start(g[:], A["g_lat"]).then_inc(w_in, 16)
            sp.dma_start(cos[:], A["cosB"]).then_inc(tab_in, 16)
            sp.dma_start(sin[:], A["sinB"]).then_inc(tab_in, 16)
            for u, (kind, j, c) in enumerate(units):
                sp.wait_ge(u_lo, u + 1)
                s = u % 3
                for part, st in (("hi", sh), ("lo", sl)):
                    if kind == "q":
                        dst, src = S["qB", part][j * 96:(j + 1) * 96, cols(c)], st[s][0:96, :]
                    elif kind == "k":
                        dst, src = S["kB", part][j * P:(j + 1) * P, cols(c)], st[s][:]
                    elif kind == "r":
                        dst, src = S["krB", part][:, cols(c)], st[s][64:96, :]
                    else:
                        dst = S["vB", part].rearrange("h p i d -> p h i d")[:, :, j, :]
                        src = st[s][:].rearrange("p (h d) -> p h d", d=HD)
                    sp.dma_start(dst, src).then_inc(stored[s], 16)
            for s in range(3):
                sp.wait_ge(stored[s], 32 * len(range(s, len(units), 3)))

        parts = ((0, 2), (2, 1))

        @block.gpsimd
        def _(pool):
            pool.wait_ge(w_in, 48)
            gb = g[:, 0:2].unsqueeze(2).to_broadcast([P, 2, 768])
            for out in (wh, wr):
                nc.gpsimd.tensor_tensor(out[:, 0:1536].rearrange("p (k n) -> p k n", k=2),
                                        wr[:, 0:1536].rearrange("p (k n) -> p k n", k=2), gb, ALU.mult
                                        ).then_inc(w_mul, 1)
                nc.gpsimd.tensor_tensor(out[:, 1536:2560], wr[:, 1536:2560], g[:, 2:3].to_broadcast([P, 1024]),
                                        ALU.mult).then_inc(w_mul, 1)
            pool.wait_ge(w_mul, 4)
            nc.gpsimd.tensor_tensor(wl[:], wr[:], wh[:].bitcast(F32), ALU.subtract).then_inc(w_lo, 1)
            pool.wait_ge(w_lo, 1)
            pool.wait_ge(tab_in, 32)
            for u, (kind, j, c) in enumerate(units):
                if kind in "qr":
                    s, k = u % 3, roped[u]
                    pc = slice((c * CH) % SEQ, (c * CH) % SEQ + CH)
                    pool.wait_ge(u_sw, k + 1)
                    nc.gpsimd.tensor_tensor(ta[s][64:96, :], ta[s][64:96, :], cos[64:96, pc], ALU.mult
                                            ).then_inc(u_cos, 1)
                    nc.gpsimd.tensor_tensor(tb[s][64:96, :], tb[s][64:96, :], sin[64:96, pc], ALU.mult
                                            ).then_inc(u_sin, 1)

        @block.tensor
        def _(pe):
            n = 0
            for c in range(NC):
                for q, (k0, nk) in enumerate(parts):
                    x = 2 * c + q
                    wait_count(pe, sd_ready, x - 1)
                    for k in range(nk):
                        pe.wait_ge(sq_ready, n + 1)
                        nc.tensor.matmul(sums[q], ones[:], sq[n % 2][:], start=(k == 0), stop=(k == nk - 1)
                                         ).then_inc(sum_ready, 1)
                        n += 1
            pe.wait_ge(w_lo, 1)
            pe.wait_ge(n_lo, 9)
            for w, (kind, j, c) in enumerate(W3):
                u = w + 3
                wait_count(pe, u_raw, u - 5)
                b = bank[w % 6]
                if kind == "q":
                    for k in range(2):
                        ws = slice(k * 768 + j * 96, k * 768 + (j + 1) * 96)
                        for i, (a, x) in enumerate(((wh, CH_), (wh, CL_), (wl, CH_))):
                            mm = nc.tensor.matmul(b[0:96, :], a[:, ws], x[:, k, cols(c)],
                                                  start=(k == 0 and i == 0), stop=(k == 1 and i == 2))
                elif kind == "k":
                    ws = slice(1536 + j * P, 1536 + (j + 1) * P)
                    for i, (a, x) in enumerate(((wh, CH_), (wh, CL_), (wl, CH_))):
                        mm = nc.tensor.matmul(b, a[:, ws], x[:, 2, cols(c)], start=(i == 0), stop=(i == 2))
                else:
                    tok = slice(j * P, (j + 1) * P)
                    for i, (x, a) in enumerate(((CH_, wh), (CL_, wh), (CH_, wl))):
                        mm = nc.tensor.matmul(b, x[:, 2, tok], a[:, 2048:2560], start=(i == 0), stop=(i == 2))
                mm.then_inc(mm_done, 1)

        @block.scalar
        def _(act):
            n = m = 0
            for c in range(NC):
                act.wait_ge(lat_in[c], 16)
                for q, (k0, nk) in enumerate(parts):
                    for k in range(k0, k0 + nk):
                        wait_count(act, sum_ready, n - 1)
                        nc.scalar.activation(sq[n % 2][:], L[:, k, cols(c)], ACT.Square).then_inc(sq_ready, 1)
                        n += 1
                for q, (k0, nk) in enumerate(parts):
                    act.wait_ge(sum_ready, 3 * c + k0 + nk)
                    wait_count(act, n_ready, 3 * c)
                    nc.scalar.activation(sd[:, q, :], sums[q], ACT.Sqrt, bias=epst[:], scale=1.0 / (nk * P)
                                         ).then_inc(sd_ready, 1)
                for k in range(3):
                    act.wait_ge(n_ready, m + 1)
                    nc.scalar.activation(CH_[:, k, cols(c)], nt_[m % 2][:], ACT.Copy).then_inc(n_hi, 1)
                    m += 1

            def hi(u):
                kind, s = units[u][0], u % 3
                if kind in "qr":
                    act.wait_ge(u_rot, roped[u] + 1)
                wait_count(act, stored[s], 32 * (u // 3))
                act.wait_ge(u_raw, u + 1)
                nc.scalar.activation(sh[s][rows(kind), :].bitcast(F32R), ta[s][rows(kind), :], ACT.Copy
                                     ).then_inc(u_hi, 1)

            for u, (kind, j, c) in enumerate(units):
                s = u % 3
                wait_count(act, u_lo, u - 2)
                if kind == "r":
                    nc.scalar.activation(ta[s][64:96, :], L[64:96, 3, cols(c)], ACT.Copy).then_inc(u_raw, 1)
                else:
                    act.wait_ge(mm_done, u - 2)
                    nc.scalar.activation(ta[s][rows(kind), :], bank[(u - 3) % 6][rows(kind), :], ACT.Copy,
                                         scale=scale if kind == "q" else 1.0).then_inc(u_raw, 1)
                if u >= 2:
                    hi(u - 2)
            hi(len(units) - 2)
            hi(len(units) - 1)

        @block.vector
        def _(dve):
            m = 0
            for c in range(NC):
                dve.wait_ge(lat_in[c], 16)
                dve.wait_ge(sd_ready, 2 * c + 2)
                nc.vector.reciprocal(sd[:, 0, :], sd[:, 0, :]).then_inc(rstd_ready, 1)
                nc.vector.reciprocal(sd[:, 1, :], sd[:, 1, :]).then_inc(rstd_ready, 1)
                dve.wait_ge(rstd_ready, 2 * c + 2)
                for k in range(3):
                    wait_count(dve, n_lo, m - 1)
                    nc.vector.tensor_tensor(nt_[m % 2][:], L[:, k, cols(c)], sd[:, k // 2, :], ALU.mult
                                            ).then_inc(n_ready, 1)
                    dve.wait_ge(n_hi, m + 1)
                    dve.wait_ge(n_ready, m + 1)
                    nc.vector.tensor_tensor(CL_[:, k, cols(c)], nt_[m % 2][:], CH_[:, k, cols(c)].bitcast(F32),
                                            ALU.subtract).then_inc(n_lo, 1)
                    m += 1

            def rot(u):
                kind, s = units[u][0], u % 3
                if kind in "qr":
                    dve.wait_ge(u_cos, roped[u] + 1)
                    dve.wait_ge(u_sin, roped[u] + 1)
                    nc.vector.tensor_tensor(ta[s][64:96, :], ta[s][64:96, :], tb[s][64:96, :], ALU.add
                                            ).then_inc(u_rot, 1)

            def lo(u):
                kind, s = units[u][0], u % 3
                dve.wait_ge(u_hi, u + 1)
                if kind in "qr":
                    dve.wait_ge(u_rot, roped[u] + 1)
                r = rows(kind)
                nc.vector.tensor_tensor(sl[s][r, :].bitcast(F32R), ta[s][r, :], sh[s][r, :], ALU.subtract
                                        ).then_inc(u_lo, 1)

            for u, (kind, j, c) in enumerate(units):
                if kind in "qr":
                    dve.wait_ge(u_raw, u + 1)
                    nc.vector.stream_shuffle(tb[u % 3][64:96, :], ta[u % 3][64:96, :], SWAP16).then_inc(u_sw, 1)
                if u >= 1:
                    rot(u - 1)
                if u >= 2:
                    lo(u - 2)
            rot(len(units) - 1)
            lo(len(units) - 2)
            lo(len(units) - 1)



def attention(nc, ar, tag, A, heads, unroll, load_a, load_b, n_a, n_b, KQ, o_head0, S, biased=False):
    stacked = KQ == HD
    KA = KQ + AUG
    NP, NS = SEQ // P, DEC // P
    LAG = 3
    NU = 2 * NP + NS
    MAXES = {3: (0, 1), 4: (2, 3), 5: (4, 5, 6), 6: (7, 8, 9), 7: (10, 11, 12), 8: (13, 14, 15),
             9: (16, 17, 18, 19)}
    HI_V = [0, 1, 2]
    HI_S = [s for s in range(10) if s not in HI_V]
    LO_P = [1, 3, 5, 7, 8, 9]
    LO_V = [s for s in range(10) if s not in LO_P]
    in_a = [ar.sem(f"{tag}_in_a{i}") for i in range(2)]
    in_b = [ar.sem(f"{tag}_in_b{i}") for i in range(2)]
    const_in, const_set = ar.sem(f"{tag}_const_in"), ar.sem(f"{tag}_const_set")
    s_ready = ar.sem(f"{tag}_s_ready")
    e_done = ar.sem(f"{tag}_e_done")
    p_hi_v, p_hi_s = ar.sem(f"{tag}_p_hi_v"), ar.sem(f"{tag}_p_hi_s")
    p_lo_v, p_lo_p = ar.sem(f"{tag}_p_lo_v"), ar.sem(f"{tag}_p_lo_p")
    pv_done = ar.sem(f"{tag}_pv_done")
    m_ready, m_done = ar.sem(f"{tag}_m_ready"), ar.sem(f"{tag}_m_done")
    m_both = ar.sem(f"{tag}_m_both")
    mt_ready, aug_done = ar.sem(f"{tag}_mt"), ar.sem(f"{tag}_aug")
    o_prompt, o_sample = ar.sem(f"{tag}_o_prompt"), ar.sem(f"{tag}_o_sample")
    o_stored = [ar.sem(f"{tag}_o_stored{i}") for i in range(2)]
    if biased:
        b_hi, b_sum, b_lo = ar.sem(f"{tag}_b_hi"), ar.sem(f"{tag}_b_sum"), ar.sem(f"{tag}_b_lo")
        m_seen = ar.sem(f"{tag}_m_seen")
    with ar.scope() as sc:
        KS = P if stacked else KQ
        Q1 = [sc.sb(f"{tag}_Q1{i}", [P, T], F32R) for i in range(2)]
        K2 = [sc.sb(f"{tag}_K2{i}", [P, T], F32R) for i in range(2)]
        Q3 = [sc.sb(f"{tag}_Q3{i}", [P, T], F32R) for i in range(2)]
        K3 = [sc.sb(f"{tag}_K3{i}", [P, T], F32R) for i in range(2)]
        VH = [sc.sb(f"{tag}_VH{i}", [P, TT, HD + 2], F32R) for i in range(2)]
        VL = [sc.sb(f"{tag}_VL{i}", [P, TT, HD + 2], F32R) for i in range(2)]
        PF = [sc.sb(f"{tag}_PF{i}", [P, 2 * CH]) for i in range(4)]
        PH = [sc.sb(f"{tag}_PH{i}", [P, 2 * CH], F32R) for i in range(4)]
        PL = [sc.sb(f"{tag}_PL{i}", [P, 2 * CH], F32R) for i in range(4)]
        OB = [sc.sb(f"{tag}_OB{i}", [HD + 1, T]) for i in range(2)]
        MH = sc.sb(f"{tag}_MH", [P, NP, 2])
        M = sc.sb(f"{tag}_M", [P, 2 * AUG])
        ident = sc.sb(f"{tag}_ident", [P, P])
        negsel = sc.sb(f"{tag}_negsel", [AUG, AUG, P])
        if biased:
            identr = sc.sb(f"{tag}_identr", [P, P], F32R)
            BD, BL_ = sc.sb(f"{tag}_BD", [P, BW]), sc.sb(f"{tag}_BL", [P, BW])
            slope = sc.sb(f"{tag}_slope", [P, 8])
            BF = sc.sb(f"{tag}_BF", [P, BW])
            BS = sc.sb(f"{tag}_BS", [P, 2 * CH])
            Bhi = [sc.sb(f"{tag}_Bhi{i}", [P, BW], F32R) for i in range(2)]
            Blo = [sc.sb(f"{tag}_Blo{i}", [P, BW], F32R) for i in range(2)]
        SA = sc.banks(f"{tag}_SA", 2)
        SM = sc.banks(f"{tag}_SM", 2)
        OP = sc.banks(f"{tag}_OP", 2)
        OS = sc.banks(f"{tag}_OS", 1)
        MT = sc.banks(f"{tag}_MT", 1)
        block = sc.enter_context(nc.Block())
        bufs = [dict(Q1=Q1[i], K2=K2[i], Q3=Q3[i], K3=K3[i], VH=VH[i], VL=VL[i]) for i in range(2)]
        NIT = heads // unroll
        n_const = 5 if biased else 2
        n_set = 8 if biased else 7

        def head_of(i, j):
            return i * unroll + j, j % 2, i * (unroll // 2) + j // 2

        def hi_count(h, s):
            a, sem_ = (HI_V, p_hi_v) if s in HI_V else (HI_S, p_hi_s)
            return sem_, h * len(a) + (a.index(s) + 1)

        def lo_count(h, s):
            a, sem_ = (LO_V, p_lo_v) if s in LO_V else (LO_P, p_lo_p)
            return sem_, h * len(a) + (a.index(s) + 1)

        @block.sync
        def _(sp):
            for dst, src in [(ident[:], A["ident"]), (negsel[:], A["negsel"])] + (
                    [(BD[:], A["bias_dist"]), (BL_[:], A["bias_count"]), (slope[:], A["slopes"])] if biased else []):
                sp.dma_start(dst, src).then_inc(const_in, 16)

            def load(h, b, i, j):
                wait_count(sp, s_ready, h * 10 - 10)
                wait_count(sp, m_done, h * NU - NU)
                for dst, src in load_a(h, i, j, bufs[b]):
                    sp.dma_start(dst.bitcast(F32), src).then_inc(in_a[b], 16)
                wait_count(sp, pv_done, h * 10 - 10)
                for dst, src in load_b(h, i, j, bufs[b]):
                    sp.dma_start(dst.bitcast(F32), src).then_inc(in_b[b], 16)

            load(0, 0, 0, 0)
            load(1, 1, 0, 1)

            def body(i, first, last):
                for j in range(unroll):
                    h, b, _ = head_of(i, j)
                    if not (last and j >= unroll - 2):
                        load(h + 2, b, i + (j + 2) // unroll, (j + 2) % unroll)
                    sp.wait_ge(o_sample, h + 1)
                    sp.dma_start(S["O"][ds(h * HD + o_head0 * HD, HD), :], OB[b][0:HD, :]).then_inc(o_stored[b], 16)
                    sp.dma_start(S["Z"][ds(h + o_head0, 1), :], OB[b][HD:HD + 1, :]).then_inc(o_stored[b], 16)
            steps(sp, NIT, body)
            for b in range(2):
                sp.wait_ge(o_stored[b], 32 * (heads // 2))

        @block.tensor
        def _(pe):
            def max_unit(h, b, fills, u):
                if u == 0:
                    pe.wait_ge(in_a[b], fills * 16 * n_a + 16 * n_a)
                wait_count(pe, m_done, h * NU + (u - 1))
                q, k = (Q1[b][:], K2[b][:]) if stacked else (Q1[b][0:KQ, :], K3[b][0:KQ, :])
                if u < 2 * NP:
                    q0, k0 = (u // 2) * P, (u % 2) * CH
                else:
                    q0, k0 = SEQ + (u - 2 * NP) * P, SEQ
                nc.tensor.matmul(SM[:, (u % 2) * CH:(u % 2 + 1) * CH], q[:, q0:q0 + P], k[:, k0:k0 + CH],
                                 start=True, stop=True).then_inc(m_ready, 1)

            def transpose_max(h, sample):
                if sample:
                    pe.wait_ge(m_done, h * NU + NU)
                else:
                    pe.wait_ge(m_both, h + 1)
                wait_count(pe, aug_done, h * 2 + sample)
                nc.tensor.matmul(MT[0:AUG, 0:P], M[:, sample * AUG:(sample + 1) * AUG], ident[:],
                                 start=True, stop=True).then_inc(mt_ready, 1)

            def scores(h, b, fills, s, g):
                if s == 0:
                    pe.wait_ge(in_b[b], fills * 16 * n_b + 16 * n_b)
                    pe.wait_ge(aug_done, h * 2 + 1)
                    if biased:
                        pe.wait_ge(b_lo, h + 1)
                if s == NP:
                    pe.wait_ge(aug_done, h * 2 + 2)
                wait_count(pe, e_done, g)
                for x in range(2):
                    out = SA[:, x * CH:(x + 1) * CH]
                    if s < NP:
                        q0, k0, base = x * CH, s * P, 0
                    else:
                        q0, k0, base = SEQ, SEQ + (2 * (s - NP) + x) * P, SEQ
                    qs, ks = slice(q0, q0 + CH), slice(k0, k0 + P)
                    mms = [(K2[b][0:KS, ks], Q1[b][0:KS, qs], None), (K3[b][0:KA, ks], Q3[b][0:KA, qs], None)]
                    if not stacked:
                        mms.insert(0, (K3[b][0:KQ, ks], Q1[b][0:KQ, qs], None))
                    if biased:
                        off = q0 - k0 + BW - SEQ
                        mms.insert(1, (identr[:], Bhi[b][:, off:off + CH], None))
                        n0, n1 = max(0, k0 - q0 - 256), min(CH, k0 - q0 + P + 256)
                        if n0 < n1:
                            mms.insert(2, (identr[:], Blo[b][:, off + n0:off + n1], (n0, n1)))
                    for i, (w, y, part) in enumerate(mms):
                        o = out if part is None else out[:, part[0]:part[1]]
                        mm = nc.tensor.matmul(o, w, y, start=(i == 0), stop=(i == len(mms) - 1),
                                              skip_group_check=biased)
                mm.then_inc(s_ready, 1)

            def pv(h, b, s, g, p, between=None):
                if s == 0:
                    wait_count(pe, o_prompt, h)
                if s == NP:
                    wait_count(pe, o_sample, h)
                pe.wait_ge(*hi_count(h, s))
                pe.wait_ge(*lo_count(h, s))
                for x in range(2):
                    pc = slice(x * CH, (x + 1) * CH)
                    if s < NP:
                        kt, out, st, en = s, OP[0:HD + 1, pc], s == 0, s == NP - 1
                    else:
                        kt, out = NP + 2 * (s - NP) + x, OS[0:HD + 1, :]
                        st, en = (s == NP and x == 0), (s == NP + 1 and x == 1)
                    for i, (w, y) in enumerate(((VH, PH), (VL, PH), (VH, PL))):
                        mm = nc.tensor.matmul(out, w[b][:, kt, 0:HD + 1], y[p][:, pc],
                                              start=(st and i == 0), stop=(en and i == 2))
                    if x == 0 and between is not None:
                        max_unit(*between)
                mm.then_inc(pv_done, 1)

            pe.wait_ge(const_in, 16 * n_const)
            pe.wait_ge(const_set, n_set)
            for u in range(NU):
                max_unit(0, 0, 0, u)
            transpose_max(0, 0)

            def body(i, first, last):
                for j in range(unroll):
                    h, b, fills = head_of(i, j)
                    hn, bn, fn = head_of(i, j + 1)
                    final = last and j == unroll - 1
                    for s in range(10):
                        scores(h, b, fills, s, h * 10 + s)
                        if s == 0:
                            transpose_max(h, 1)
                        if s == 9 and not final:
                            transpose_max(hn, 0)
                        units = MAXES.get(s, ()) if not final else ()
                        lead = len(units) - 2
                        for u in units[:max(lead, 0)]:
                            max_unit(hn, bn, fn, u)
                        between = (hn, bn, fn, units[max(lead, 0)]) if units else None
                        if s >= LAG:
                            pv(h, b, s - LAG, h * 10 + s - LAG, (j * 10 + s - LAG) % 4, between)
                        elif not (first and j == 0):
                            pv(h - 1, 1 - b, s + 10 - LAG, h * 10 + s - LAG, (j * 10 + s - LAG) % 4)
                        for u in units[max(lead, 0) + 1:]:
                            max_unit(hn, bn, fn, u)
                if last:
                    for s in range(10 - LAG, 10):
                        pv(h, b, s, h * 10 + s, (j * 10 + s) % 4)
            steps(pe, NIT, body)

        @block.scalar
        def _(act):
            if biased:
                act.wait_ge(const_in, 16 * n_const)
                nc.scalar.activation(identr[:], ident[:], ACT.Copy).then_inc(const_set, 1)

            def evac_prompt(h, b, fills):
                wait_count(act, o_stored[b], fills * 32)
                act.wait_ge(pv_done, h * 10 + NP)
                nc.scalar.activation(OB[b][:, 0:SEQ], OP[0:HD + 1, :], ACT.Copy).then_inc(o_prompt, 1)

            def evac_sample(h, b):
                act.wait_ge(pv_done, h * 10 + 10)
                act.wait_ge(o_prompt, h + 1)
                nc.scalar.activation(OB[b][:, SEQ:T], OS[0:HD + 1, :], ACT.Copy).then_inc(o_sample, 1)

            def body(i, first, last):
                for j in range(unroll):
                    h, b, fills = head_of(i, j)
                    for s in range(10):
                        g, p = h * 10 + s, (j * 10 + s) % 4
                        act.wait_ge(s_ready, g + 1)
                        wait_count(act, pv_done, g - 3)
                        nc.scalar.activation(PF[p][:], SA[:], ACT.Exp).then_inc(e_done, 1)
                        if s in HI_S:
                            act.wait_ge(e_done, g + 1)
                            nc.scalar.activation(PH[p][:], PF[p][:], ACT.Copy).then_inc(p_hi_s, 1)
                        if s == 1 and not (first and j == 0):
                            evac_prompt(h - 1, 1 - b, i * (unroll // 2) + (j - 1) // 2)
                        if s == 3 and not (first and j == 0):
                            evac_sample(h - 1, 1 - b)
                if last:
                    evac_prompt(h, b, fills)
                    evac_sample(h, b)
            steps(act, NIT, body)

        @block.vector
        def _(dve):
            for b in range(2):
                nc.vector.memset(K3[b][KQ:KA, :].bitcast(F32), 1.0).then_inc(const_set, 1)
                nc.vector.memset(VH[b][:, :, HD:HD + 1].bitcast(F32), 1.0).then_inc(const_set, 1)
                nc.vector.memset(VL[b][:, :, HD:HD + 1].bitcast(F32), 0.0).then_inc(const_set, 1)
            nc.vector.memset(M[:], 0.0).then_inc(const_set, 1)
            dve.wait_ge(const_in, 16 * n_const)
            dve.wait_ge(const_set, n_set)

            def bias(h, b):
                wait_count(dve, s_ready, h * 10 - 10)
                sl = slope[:, ds(h, 1)]
                nc.vector.scalar_tensor_tensor(out=Bhi[b][:], in0=BD[:], scalar=sl, in1=BL_[:],
                                               op0=ALU.mult, op1=ALU.add).then_inc(b_hi, 1)
                wait_count(dve, b_lo, h)
                nc.vector.scalar_tensor_tensor(out=BF[:], in0=BD[:], scalar=sl, in1=BL_[:],
                                               op0=ALU.mult, op1=ALU.add).then_inc(b_sum, 1)

            def maximum(h, b, u):
                x = u % 2
                src = SM[:, x * CH:(x + 1) * CH]
                qi = u // 2 if u < 2 * NP else u - 2 * NP
                dst = MH[:, qi, x:x + 1] if u < 2 * NP else M[:, AUG + qi:AUG + qi + 1]
                if not biased:
                    dve.wait_ge(m_ready, h * NU + (u + 1))
                    nc.vector.reduce_max(dst, src, axis=AX_X).then_inc(m_done, 1)
                else:
                    off = BW - SEQ - qi * P + (x * CH if u < 2 * NP else 0)
                    if u == 0:
                        dve.wait_ge(b_hi, h + 1)
                    wait_apart(dve, m_ready, h * NU + (u + 1), m_seen)
                    nc.vector.tensor_tensor_reduce(
                        out=BS[:, x * CH:(x + 1) * CH], in0=src, in1=Bhi[b][:, off:off + CH].bitcast(F32), scale=1.0,
                        scalar=-3.0e38, op0=ALU.add, op1=ALU.max, accum_out=dst).then_inc(m_done, 1)
                if u == 2 * NP - 1:
                    dve.wait_ge(m_done, h * NU + 2 * NP)
                    nc.vector.tensor_tensor(M[:, 0:NP], MH[:, :, 0], MH[:, :, 1], ALU.max).then_inc(m_both, 1)

            def augment(h, b, sample):
                dve.wait_ge(mt_ready, h * 2 + sample + 1)
                wait_count(dve, s_ready, h * 10 - 10)
                nt = NS if sample else NP
                t0 = SEQ if sample else 0
                nc.vector.tensor_tensor(
                    Q3[b][KQ:KA, t0:t0 + nt * P].rearrange("r (i n) -> r i n", n=P),
                    MT[0:AUG, 0:P].unsqueeze(1).to_broadcast([AUG, nt, P]), negsel[:, 0:nt, :], ALU.mult
                ).then_inc(aug_done, 1)

            def low(h, s, g, p):
                dve.wait_ge(*hi_count(h, s))
                nc.vector.tensor_tensor(PL[p][:], PF[p][:], PH[p][:].bitcast(F32), ALU.subtract).then_inc(p_lo_v, 1)

            if biased:
                bias(0, 0)
            for u in range(NU):
                maximum(0, 0, u)
            augment(0, 0, 0)

            def body(i, first, last):
                for j in range(unroll):
                    h, b, fills = head_of(i, j)
                    hn, bn, _ = head_of(i, j + 1)
                    final = last and j == unroll - 1
                    for s in range(10):
                        g, p = h * 10 + s, (j * 10 + s) % 4
                        if s == 0:
                            augment(h, b, 1)
                        if s in HI_V:
                            dve.wait_ge(e_done, g + 1)
                            nc.vector.tensor_copy(PH[p][:], PF[p][:]).then_inc(p_hi_v, 1)
                        if s == 1 and biased and not final:
                            bias(hn, bn)
                        if s == 9 and not final:
                            augment(hn, bn, 0)
                        units = MAXES.get(s, ()) if not final else ()
                        for u in units[0:1]:
                            maximum(hn, bn, u)
                        if s - 1 in LO_V:
                            low(h, s - 1, g - 1, (p - 1) % 4)
                        for u in units[1:]:
                            maximum(hn, bn, u)
            steps(dve, NIT, body)

        @block.gpsimd
        def _(pool):
            def bias_low(h, b):
                pool.wait_ge(b_hi, h + 1)
                pool.wait_ge(b_sum, h + 1)
                nc.gpsimd.tensor_tensor(Blo[b][:], BF[:], Bhi[b][:].bitcast(F32), ALU.subtract).then_inc(b_lo, 1)

            if biased:
                bias_low(0, 0)

            def body(i, first, last):
                for j in range(unroll):
                    h, b, _ = head_of(i, j)
                    hn, bn, _ = head_of(i, j + 1)
                    if biased and not (last and j == unroll - 1):
                        bias_low(hn, bn)
                    for s in LO_P:
                        p = (j * 10 + s) % 4
                        pool.wait_ge(*hi_count(h, s))
                        nc.gpsimd.tensor_tensor(PL[p][:], PF[p][:], PH[p][:].bitcast(F32), ALU.subtract
                                                ).then_inc(p_lo_p, 1)
            steps(pool, NIT, body)



def reciprocal_denominators(nc, ar, tag, S, row0):
    N = 16 * T // P
    z_in, z_rcp, z_out = ar.sem(f"{tag}_z_in"), ar.sem(f"{tag}_z_rcp"), ar.sem(f"{tag}_z_out")
    with ar.scope() as sc:
        z = sc.sb(f"{tag}_z", [P, N])
        rz = sc.sb(f"{tag}_rz", [P, N])
        block = sc.enter_context(nc.Block())

        def flat(x):
            return x[row0:row0 + 16, :].rearrange("h (a n) -> (h a) n", n=N)

        @block.sync
        def _(sp):
            sp.dma_start(z[:], flat(S["Z"])).then_inc(z_in, 16)
            sp.wait_ge(z_rcp, 1)
            sp.dma_start(flat(S["RZ"]), rz[:]).then_inc(z_out, 16)
            sp.wait_ge(z_out, 16)

        @block.vector
        def _(dve):
            dve.wait_ge(z_in, 16)
            nc.vector.reciprocal(rz[:], z[:]).then_inc(z_rcp, 1)


def gate_and_split(nc, ar, tag, S, row0, gate, XH, XL):
    o_in = [ar.sem(f"{tag}_o_in{i}") for i in range(2)]
    g1, g2, ghi, glo = (ar.sem(f"{tag}_g{x}") for x in ("1", "2", "hi", "lo"))
    with ar.scope() as sc:
        O = [sc.sb(f"{tag}_O{i}", [P, T]) for i in range(2)]
        G = [sc.sb(f"{tag}_G{i}", [P, T]) for i in range(2)]
        R = [sc.sb(f"{tag}_R{i}", [P, T]) for i in range(2)]
        block = sc.enter_context(nc.Block())

        @block.sync
        def _(sp):
            for k in range(KT):
                b = k % 2
                wait_count(sp, glo, k - 1)
                r = slice((row0 + 2 * k) * HD, (row0 + 2 * k + 2) * HD)
                sp.dma_start(O[b][:], S["O"][r, :]).then_inc(o_in[b], 16)
                sp.dma_start(G[b][:], gate[k * P:(k + 1) * P, :]).then_inc(o_in[b], 16)
                for x in range(2):
                    row = row0 + 2 * k + x
                    sp.dma_start(R[b][x * HD:(x + 1) * HD, :], S["RZ"][row:row + 1, :].to_broadcast([HD, T])
                                 ).then_inc(o_in[b], 16)

        @block.gpsimd
        def _(pool):
            for k in range(KT):
                b = k % 2
                pool.wait_ge(o_in[b], 64 * (k // 2 + 1))
                nc.gpsimd.tensor_tensor(G[b][:], G[b][:], R[b][:], ALU.mult).then_inc(g1, 1)

        @block.vector
        def _(dve):
            for k in range(KT):
                b = k % 2
                dve.wait_ge(g1, k + 1)
                nc.vector.tensor_tensor(O[b][:], O[b][:], G[b][:], ALU.mult).then_inc(g2, 1)
                dve.wait_ge(g2, k + 1)
                dve.wait_ge(ghi, k + 1)
                nc.vector.tensor_tensor(XL[:, k, :], O[b][:], XH[:, k, :].bitcast(F32), ALU.subtract
                                        ).then_inc(glo, 1)

        @block.scalar
        def _(act):
            for k in range(KT):
                act.wait_ge(g2, k + 1)
                nc.scalar.activation(XH[:, k, :], O[k % 2][:], ACT.Copy).then_inc(ghi, 1)


def post_norm_add(nc, ar, tag, Y, gpost, ones, epst, xin, xout):
    loaded = [ar.sem(f"{tag}_x_in{i}") for i in range(2)]
    sq_ready, sum_ready, sd_ready = ar.sem(f"{tag}_sq"), ar.sem(f"{tag}_sum"), ar.sem(f"{tag}_sd")
    rstd_ready, t_ready, y_ready, y_out = (ar.sem(f"{tag}_{x}") for x in ("rstd", "t", "y", "y_out"))
    with ar.scope() as sc:
        X = [sc.sb(f"{tag}_X{i}", [P, CH]) for i in range(2)]
        sq = [sc.sb(f"{tag}_sqt{i}", [P, CH]) for i in range(2)]
        tt = [sc.sb(f"{tag}_tt{i}", [P, CH]) for i in range(2)]
        sd = sc.sb(f"{tag}_sdt", [P, CH])
        rstd = sc.sb(f"{tag}_rstdt", [P, CH])
        ss = sc.banks(f"{tag}_ss", 1)
        block = sc.enter_context(nc.Block())

        def at(x, n):
            c, k = n // KT, n % KT
            return x[k * P:(k + 1) * P, c * CH:(c + 1) * CH]

        @block.sync
        def _(sp):
            for n in range(NC * KT):
                wait_count(sp, y_ready, n - 1)
                sp.dma_start(X[n % 2][:], at(xin, n)).then_inc(loaded[n % 2], 16)
                if n >= 2:
                    sp.dma_start(at(xout, n - 2), Y[:, (n - 2) % KT, (n - 2) // KT * CH:((n - 2) // KT + 1) * CH]
                                 ).then_inc(y_out, 16)
            for n in range(NC * KT - 2, NC * KT):
                sp.wait_ge(y_ready, n + 1)
                sp.dma_start(at(xout, n), Y[:, n % KT, n // KT * CH:(n // KT + 1) * CH]).then_inc(y_out, 16)
            sp.wait_ge(y_out, 16 * NC * KT)

        @block.scalar
        def _(act):
            for c in range(NC):
                for k in range(KT):
                    n = c * KT + k
                    wait_count(act, sum_ready, n - 1)
                    nc.scalar.activation(sq[n % 2][:], Y[:, k, c * CH:(c + 1) * CH], ACT.Square
                                         ).then_inc(sq_ready, 1)
                act.wait_ge(sum_ready, (c + 1) * KT)
                wait_count(act, rstd_ready, c)
                nc.scalar.activation(sd[:], ss[:], ACT.Sqrt, bias=epst[:], scale=1.0 / D).then_inc(sd_ready, 1)

        @block.tensor
        def _(pe):
            for c in range(NC):
                wait_count(pe, sd_ready, c)
                for k in range(KT):
                    pe.wait_ge(sq_ready, c * KT + k + 1)
                    nc.tensor.matmul(ss[:], ones[:], sq[(c * KT + k) % 2][:], start=(k == 0), stop=(k == KT - 1)
                                     ).then_inc(sum_ready, 1)

        @block.vector
        def _(dve):
            for c in range(NC):
                dve.wait_ge(sd_ready, c + 1)
                nc.vector.reciprocal(rstd[:], sd[:]).then_inc(rstd_ready, 1)
                dve.wait_ge(rstd_ready, c + 1)
                for k in range(KT):
                    n = c * KT + k
                    y = Y[:, k, c * CH:(c + 1) * CH]
                    nc.vector.tensor_tensor(tt[n % 2][:], y, rstd[:], ALU.mult).then_inc(t_ready, 1)
                    dve.wait_ge(t_ready, n + 1)
                    dve.wait_ge(loaded[n % 2], 16 * (n // 2 + 1))
                    nc.vector.scalar_tensor_tensor(out=y, in0=tt[n % 2][:], scalar=gpost[:, k:k + 1], in1=X[n % 2][:],
                                                   op0=ALU.mult, op1=ALU.add).then_inc(y_ready, 1)



def build_trunk(nc, A):
    ar = Arena(nc)

    def scratch(name, shape):
        return nc.dram_tensor(name, shape, F32, kind="Internal").ap()

    S = {"O": scratch("att_out", [32 * HD, T]),
         "Z": scratch("att_den", [32, T]),
         "RZ": scratch("att_rden", [32, T]),
         "X1": scratch("x_mid", [D, T]),
         "latent": scratch("latent", [4 * P, T]),
         "gate0": scratch("silu_gate0", [D, T]), "gate1": scratch("silu_gate1", [D, T])}
    for part in ("hi", "lo"):
        for name, shape in (("qA", [512, T]), ("kA", [512, T]), ("vA", [8, P, TT, HD]),
                            ("qB", [8 * 96, T]), ("kB", [512, T]), ("krB", [ROPE, T]), ("vB", [8, P, TT, HD]),
                            ("qC", [1024, T]), ("kC", [256, T]), ("vC", [4, P, TT, HD])):
            S[name, part] = scratch(f"{name}_{part}", shape)

    with ar.scope() as sc:
        ones = sc.sb("ones", [P, P])
        epst = sc.sb("epst", [P, 1])
        unit = sc.sb("unit_gain", [P, KT])
        gpre = [sc.sb(f"gpre{l}", [P, KT]) for l in range(2)]
        gpost = [sc.sb(f"gpost{l}", [P, KT]) for l in range(2)]
        set_up(nc, ar, ones, epst, unit, gpre, gpost, A)

        def rows(h, j, n, mul=1):
            return ds(h * n, n)

        with ar.scope() as s1:
            XH = s1.sb("XH0", [P, KT, T], F32R)
            XL = s1.sb("XL0", [P, KT, T], F32R)
            with ar.scope() as s2:
                normalise_and_split(nc, ar, "n0", s2.sb("X0", [P, KT, T]), XH, XL, ones, epst, src=A["xT"])
            project(nc, ar, "p0", XH, XL, A["w_tiles0"], gpre[0],
                    [("split", 0, 4, {"hi": S["qA", "hi"], "lo": S["qA", "lo"], "scale": HD ** -0.5}),
                     ("split", 4, 4, {"hi": S["kA", "hi"], "lo": S["kA", "lo"]}),
                     ("raw", 8, 4, {"out": S["latent"]}),
                     ("gate", 12, 8, {"out": S["gate0"]})],
                    values={"w": A["wv0"], "heads": 8, "hi": S["vA", "hi"], "lo": S["vA", "lo"]})
        latent_projections(nc, ar, S, A, ones, epst)

        def per_head(name, part, h, n):
            return S[name, part][ds(h * n, n), :]

        def values_of(name, part, h):
            return S[name, part][ds(h, 1), :, :, :].rearrange("a p i d -> (a p) i d")

        def load_v(name, h, B):
            return [(B["VH"][:, :, 0:HD], values_of(name, "hi", h)), (B["VL"][:, :, 0:HD], values_of(name, "lo", h))]

        attention(nc, ar, "a", A, 8, 2,
                  lambda h, i, j, B: [(B["Q1"][0:HD, :], per_head("qA", "hi", h, HD)),
                                      (B["Q1"][HD:P, :], per_head("qA", "hi", h, HD)),
                                      (B["K2"][0:HD, :], per_head("kA", "hi", h, HD)),
                                      (B["K2"][HD:P, :], per_head("kA", "lo", h, HD))],
                  lambda h, i, j, B: [(B["Q3"][0:HD, :], per_head("qA", "lo", h, HD)),
                                      (B["K3"][0:HD, :], per_head("kA", "hi", h, HD))] + load_v("vA", h, B),
                  4, 4, HD, 0, S, biased=True)
        attention(nc, ar, "b", A, 8, 2,
                  lambda h, i, j, B: [(B["Q1"][0:96, :], per_head("qB", "hi", h, 96)),
                                      (B["K3"][0:HD, :], per_head("kB", "hi", h, HD)),
                                      (B["K3"][HD:96, :], S["krB", "hi"])],
                  lambda h, i, j, B: [(B["K2"][0:HD, :], per_head("kB", "lo", h, HD)),
                                      (B["K2"][HD:96, :], S["krB", "lo"]),
                                      (B["Q3"][0:96, :], per_head("qB", "lo", h, 96))] + load_v("vB", h, B),
                  3, 5, 96, 8, S)

        ar.recycle()

        def finish_layer(l, XH, XL, Y, xin, xout):
            reciprocal_denominators(nc, ar, f"z{l}", S, 16 * l)
            gate_and_split(nc, ar, f"g{l}", S, 16 * l, S[f"gate{l}"], XH, XL)
            project(nc, ar, f"o{l}", XH, XL, A[f"w_out{l}"], unit, [("keep", 0, KT, {})], Yout=Y)
            post_norm_add(nc, ar, f"y{l}", Y, gpost[l], ones, epst, xin, xout)

        with ar.scope() as s1:
            XH = s1.sb("XH1", [P, KT, T], F32R)
            XL = s1.sb("XL1", [P, KT, T], F32R)
            with ar.scope() as s2:
                Y = s2.sb("Y0", [P, KT, T])
                finish_layer(0, XH, XL, Y, A["xT"], S["X1"])
                normalise_and_split(nc, ar, "n1", Y, XH, XL, ones, epst)
            with ar.scope() as s2:
                sel = s2.sb("headsel", [P, P])
                tabs = {x: s2.sb(f"rope_{x}", [P, SEQ]) for x in ("cq", "sq", "ck", "sk")}
                rope_tables(nc, ar, A, sel, tabs)
                project(nc, ar, "p1", XH, XL, A["w_tiles1"], gpre[1],
                        [("qk", 0, 8, {"hi": S["qC", "hi"], "lo": S["qC", "lo"], "cos": tabs["cq"], "sin": tabs["sq"]}),
                         ("qk", 8, 2, {"hi": S["kC", "hi"], "lo": S["kC", "lo"], "cos": tabs["ck"], "sin": tabs["sk"]}),
                         ("gate", 10, 8, {"out": S["gate1"]})],
                        values={"w": A["wv1"], "heads": 4, "hi": S["vC", "hi"], "lo": S["vC", "lo"]},
                        sel=sel, epst=epst)
        attention(nc, ar, "c", A, 16, 4,
                  lambda h, i, j, B: [(B["Q1"][0:HD, :], per_head("qC", "hi", h, HD)),
                                      (B["Q1"][HD:P, :], per_head("qC", "hi", h, HD)),
                                      (B["K2"][0:HD, :], per_head("kC", "hi", i, HD)),
                                      (B["K2"][HD:P, :], per_head("kC", "lo", i, HD))],
                  lambda h, i, j, B: [(B["Q3"][0:HD, :], per_head("qC", "lo", h, HD)),
                                      (B["K3"][0:HD, :], per_head("kC", "hi", i, HD))] + load_v("vC", i, B),
                  4, 4, HD, 16, S)
        with ar.scope() as s1:
            XH = s1.sb("XH2", [P, KT, T], F32R)
            XL = s1.sb("XL2", [P, KT, T], F32R)
            Y = s1.sb("Y1", [P, KT, T])
            finish_layer(1, XH, XL, Y, S["X1"], A["yT"])


def set_up(nc, ar, ones, epst, unit, gpre, gpost, A):
    g_in, c_set = ar.sem("g_in"), ar.sem("c_set")
    with nc.Block() as block:
        @block.sync
        def _(sp):
            for l in range(2):
                sp.dma_start(gpre[l][:], A["gpre"][l]).then_inc(g_in, 16)
                sp.dma_start(gpost[l][:], A["gpost"][l]).then_inc(g_in, 16)
            sp.wait_ge(g_in, 64)

        @block.vector
        def _(dve):
            nc.vector.memset(ones[:], 1.0).then_inc(c_set, 1)
            nc.vector.memset(epst[:], EPS).then_inc(c_set, 1)
            nc.vector.memset(unit[:], 1.0).then_inc(c_set, 1)
            dve.wait_ge(c_set, 3)


def rope_tables(nc, ar, A, sel, tabs):
    t_in, t_done = ar.sem("rt_in"), ar.sem("rt_done")
    with ar.scope() as sc:
        g = sc.sb("rt_gain", [P, 4])
        block = sc.enter_context(nc.Block())

        @block.sync
        def _(sp):
            sp.dma_start(g[:], A["g_heads"]).then_inc(t_in, 16)
            sp.dma_start(sel[:], A["headsel"]).then_inc(t_in, 16)
            for x, src in (("cq", "cosC"), ("sq", "sinC"), ("ck", "cosC"), ("sk", "sinC")):
                sp.dma_start(tabs[x][:], A[src]).then_inc(t_in, 16)
            sp.wait_ge(t_in, 96)

        @block.vector
        def _(dve):
            dve.wait_ge(t_in, 96)
            for n, (x, scale) in enumerate((("cq", HD ** -0.5), ("sq", HD ** -0.5), ("ck", 1.0), ("sk", 1.0))):
                nc.vector.tensor_scalar(tabs[x][:], tabs[x][:], g[:, n:n + 1], scale, ALU.mult, ALU.mult
                                        ).then_inc(t_done, 1)
            dve.wait_ge(t_done, 4)



def shape_constants():
    import numpy as np
    half = ROPE // 2
    freq = (np.float32(10000.0) ** (-np.arange(half, dtype=np.float32) / np.float32(half))).astype(np.float32)
    r = np.arange(P)
    sign = np.where(r % ROPE < half, -1.0, 1.0).astype(np.float32)[:, None]

    def tables(pos):
        ang = (pos * freq[r % half][:, None]).astype(np.float32)
        return np.cos(ang).astype(np.float32), (np.sin(ang) * sign).astype(np.float32)

    t = np.arange(SEQ, dtype=np.float32)[None, :]
    c = {}
    c["cosB"], c["sinB"] = tables(np.broadcast_to(t, (P, SEQ)))
    axial = np.where((r[:, None] // ROPE) % 2 == 0, np.floor(t / 64), t % 64).astype(np.float32)
    c["cosC"], c["sinC"] = tables(axial)
    c["headsel"] = (r[:, None] // HD == r[None, :] // HD).astype(np.float32)
    c["ident"] = np.eye(P, dtype=np.float32)
    c["negsel"] = np.ascontiguousarray(np.broadcast_to(-np.eye(AUG, dtype=np.float32)[:, :, None], (AUG, AUG, P)))
    off = np.abs(np.arange(BW)[None, :] - (BW - SEQ) - r[:, None])
    held = (off <= 64).astype(int) + ((off % 4 == 0) & (off <= 256)) + ((off % 16 == 0) & (off <= 1024))
    c["bias_dist"] = np.where(held > 0, -off.astype(np.float64), -1e30).astype(np.float32)
    c["bias_count"] = np.where(held > 0, np.log(np.maximum(held, 1).astype(np.float64)), 0.0).astype(np.float32)
    c["slopes"] = np.ascontiguousarray(np.broadcast_to(2.0 ** -np.arange(1, 9, dtype=np.float32), (P, 8)))
    return c


def kernel(x_prompt, x_sample, norm_pre, norm_post, w_in_ab, mla_q_norm, w_uq, mla_kv_norm, w_ukv,
           w_out_ab, w_in_c, c_q_norm, c_k_norm, w_out_c):
    import numpy as np
    import concourse.bacc as bacc
    from concourse.bass_utils import run_bass_kernel_spmd

    def feature_tiles(w):
        return w.reshape(KT, P, -1, P).transpose(2, 1, 0, 3).reshape(-1, P, D)

    def value_units(w):
        return w.reshape(KT // 2, 2, P, -1).transpose(0, 2, 1, 3).reshape(KT // 2, P, -1)

    def columns(g):
        return g.reshape(-1, P).T

    w0, w1 = np.asarray(w_in_ab)[0], np.asarray(w_in_c)[0]
    kr = w0[:, 1920:1952]
    cols0 = np.concatenate([w0[:, 0:1024], w0[:, 1536:1920], kr, kr, kr, kr, w0[:, 1952:2976]], axis=1)
    cols1 = np.concatenate([w1[:, 0:1280], w1[:, 1536:2560]], axis=1)
    wk = np.asarray(w_ukv)[0].reshape(P, 8, 2, HD)
    gq, gk = np.asarray(c_q_norm)[0], np.asarray(c_k_norm)[0]
    swap = np.arange(HD) // 32 * 32 + (np.arange(HD) + 16) % 32
    arrays = {
        "xT": np.concatenate([np.asarray(x_prompt)[0].T, np.asarray(x_sample)[0].T], axis=1),
        "w_tiles0": feature_tiles(cols0), "wv0": value_units(w0[:, 1024:1536]),
        "w_tiles1": feature_tiles(cols1), "wv1": value_units(w1[:, 1280:1536]),
        "w_out0": feature_tiles(np.asarray(w_out_ab)[0]), "w_out1": feature_tiles(np.asarray(w_out_c)[0]),
        "w_uq": np.asarray(w_uq)[0],
        "w_ukv": np.concatenate([wk[:, :, 0].reshape(P, 512), wk[:, :, 1].reshape(P, 512)], axis=1),
        "gpre": np.stack([columns(g) for g in np.asarray(norm_pre)]),
        "gpost": np.stack([columns(g) for g in np.asarray(norm_post)]),
        "g_lat": np.concatenate([columns(np.asarray(mla_q_norm)[0]), columns(np.asarray(mla_kv_norm)[0])], axis=1),
        "g_heads": np.stack([np.concatenate([g, g]) for g in (gq, gq[swap], gk, gk[swap])], axis=1),
    }
    arrays.update(shape_constants())
    arrays = {k: np.ascontiguousarray(v) for k, v in arrays.items()}
    nc = bacc.Bacc("TRN2", target_bir_lowering=False, num_devices=1)
    A = {k: nc.dram_tensor(f"in_{k}", v.shape, mybir.dt.from_np(v.dtype), kind="ExternalInput").ap()
         for k, v in arrays.items()}
    A["yT"] = nc.dram_tensor("yT", (D, T), F32, kind="ExternalOutput").ap()
    build_trunk(nc, A)
    r = run_bass_kernel_spmd(nc, [{f"in_{k}": v for k, v in arrays.items()}], core_ids=[0])
    y = r.results[0]["yT"]
    return (np.ascontiguousarray(y[:, 0:SEQ].T)[None], np.ascontiguousarray(y[:, SEQ:T].T)[None])
```

```python
from contextlib import ExitStack

import concourse.bass as bass
from concourse import mybir

F32 = mybir.dt.float32
F32R = mybir.dt.float32r
ALU = mybir.AluOpType
ACT = mybir.ActivationFunctionType
AX_X = mybir.AxisListType.X

P = 128
D = 1024
KT = D // P
SEQ, DEC = 1024, 512
T = SEQ + DEC
CH = 512
NC = T // CH
TT = T // P
EPS = 1e-6
HD = 64
ROPE = 32
BW = 1920
AUG = 8
SWAP16 = [(i + 16) % 32 for i in range(32)]


def ds(start, size):
    return bass.ds(start, size)


def wait_count(eng, sem, value):
    if isinstance(value, int) and value <= 0:
        return
    eng.wait_ge(sem, value)


def wait_apart(eng, sem, value, seen):
    eng.wait_ge(sem, value)
    eng.sem_inc(seen, 1)


def steps(eng, count, body):
    body(0, True, count == 1)
    if count > 2:
        with eng.Fori(1, count - 1) as i:
            body(i, False, False)
    if count > 1:
        body(count - 1, False, True)


class Arena:

    def __init__(self, nc):
        self.nc, self.sems = nc, []

    def sem(self, name):
        self.sems.append(self.nc.alloc_semaphore(name=name))
        return self.sems[-1]

    def recycle(self):
        self.nc.clear_and_free_semaphores(self.sems)
        self.nc.all_engine_barrier()
        self.sems = []

    def scope(self):
        return Scope(self.nc)


class Scope(ExitStack):
    def __init__(self, nc):
        super().__init__()
        self.nc = nc

    def sb(self, name, shape, dtype=F32):
        return self.enter_context(self.nc.sbuf_tensor(name, shape, dtype))

    def both(self, name, shape):
        offset = (self.nc.sbuf_base + 31) // 32 * 32
        plain = self.sb(name, shape)
        return plain, self.nc.alloc_sbuf_tensor_at(f"{name}_r", shape, F32R, offset=offset)

    def banks(self, name, count):
        return self.enter_context(self.nc.psum_tensor(name, [P, count * CH], F32))



def project(nc, ar, tag, x, rstd, tiles, gain, groups, values, consts, src=None, tabs=None):
    XH, XF, XL = x
    ones, epst, arrays = consts
    x_in = [ar.sem(f"{tag}_x_in{c}") for c in range(NC)]
    x_sq, x_sum, x_sd, x_rstd, x_h, x_hi = (ar.sem(f"{tag}_x_{n}") for n in ("sq", "sum", "sd", "rstd", "h", "hi"))
    x_lo_v, x_lo_p = ar.sem(f"{tag}_x_lo_v"), ar.sem(f"{tag}_x_lo_p")
    NT = sum(g[2] for g in groups)
    raw_in = [ar.sem(f"{tag}_w_in{i}") for i in range(2)]
    w_scaled, w_hi, w_ready = ar.sem(f"{tag}_w_scaled"), ar.sem(f"{tag}_w_hi"), ar.sem(f"{tag}_w_ready")
    acc_ready = ar.sem(f"{tag}_acc_ready")
    acc_read = {g[1]: ar.sem(f"{tag}_acc_read{g[1]}") for g in groups}
    acc_read[NT] = ar.sem(f"{tag}_acc_read_v")
    v_used = ar.sem(f"{tag}_v_used")
    hi_ready = ar.sem(f"{tag}_hi_ready")
    stored = [ar.sem(f"{tag}_stored{i}") for i in range(3)]
    g_exp, g_one, g_rcp = ar.sem(f"{tag}_g_exp"), ar.sem(f"{tag}_g_one"), ar.sem(f"{tag}_g_rcp")
    has_qk = any(g[0] == "qk" for g in groups)
    if has_qk:
        q_raw, q_sum, q_sd, q_rstd = (ar.sem(f"{tag}_q_{x}") for x in ("raw", "sum", "sd", "rstd"))
        q_sw, q_cos, q_sin, q_rot, q_done, q_lo, q_seen = (
            ar.sem(f"{tag}_q_{x}") for x in ("sw", "cos", "sin", "rot", "done", "lo", "seen"))
    hi0, qk0, nh, nq = {}, {}, 0, 0
    for kind, t0, nt, _ in groups:
        hi0[t0], qk0[t0] = nh, nq
        nh += 3 * nt if kind in ("split", "qk") else 0
        nq += 3 * nt if kind == "qk" else 0
    vhi0 = nh
    VU = KT

    with ar.scope() as sc:
        raw = [sc.sb(f"{tag}_raw{i}", [P, D]) for i in range(2)]
        wg = sc.sb(f"{tag}_wg", [P, D])
        wh = [sc.sb(f"{tag}_wh{i}", [P, D], F32R) for i in range(2)]
        wl = [sc.sb(f"{tag}_wl{i}", [P, D], F32R) for i in range(2)]
        sh, sl, ta, tb = ([sc.sb(f"{tag}_{n}{i}", [P, CH]) for i in range(3)] for n in ("sh", "sl", "ta", "tb"))
        if src is not None:
            xsq = [sc.sb(f"{tag}_xsq{i}", [P, CH]) for i in range(2)]
        if tabs:
            t_in, t_done = ar.sem(f"{tag}_t_in"), ar.sem(f"{tag}_t_done")
            sel = sc.sb(f"{tag}_headsel", [P, P])
            hg = sc.sb(f"{tag}_head_gain", [P, 4])
            for n in tabs:
                tabs[n][1] = sc.sb(f"{tag}_rope_{n}", [P, SEQ])
        if has_qk:
            tsq = [sc.sb(f"{tag}_tsq{i}", [P, CH]) for i in range(2)]
            tsd = [sc.sb(f"{tag}_tsd{i}", [P, CH]) for i in range(2)]
        acc = sc.banks(f"{tag}_acc", 6)
        ssb = sc.banks(f"{tag}_ssb", 2)
        bank = [acc[:, i * CH:(i + 1) * CH] for i in range(6)]
        sums = [ssb[:, i * CH:(i + 1) * CH] for i in range(2)]
        block = sc.enter_context(nc.Block())

        def cols(c):
            return slice(c * CH, (c + 1) * CH)

        def x_split(eng, sem_, engine, parity):
            def tile(c, k):
                eng.wait_ge(x_hi, c * KT + k + 1)
                engine.tensor_tensor(XL[:, k, cols(c)], XF[:, k, cols(c)], XH[:, k, cols(c)].bitcast(F32),
                                     ALU.subtract).then_inc(sem_, 1)
            return tile

        @block.sync
        def _(sp):
            def load(t, b):
                wait_count(sp, w_ready, t - 1)
                sp.dma_start(raw[b][:], tiles[ds(t, 1), :, :].rearrange("a p n -> p (a n)")
                             ).then_inc(raw_in[b], 16)

            load(0, 0)
            if src is not None:
                for c in range(NC):
                    sp.dma_start(XF[:, :, cols(c)], src.rearrange("(k p) t -> p k t", p=P)[:, :, cols(c)]
                                 ).then_inc(x_in[c], 16)
            load(1, 1)
            if tabs:
                sp.dma_start(hg[:], arrays["g_heads"]).then_inc(t_in, 16)
                sp.dma_start(sel[:], arrays["headsel"]).then_inc(t_in, 16)
                for name, (source, table) in tabs.items():
                    sp.dma_start(table[:], arrays[source]).then_inc(t_in, 16)
            for kind, t0, nt, opt in groups:
                final = t0 + nt == NT

                def pair(i, first, last):
                    for b in range(2):
                        tl = i * 2 + b
                        t = tl + t0
                        if not (final and last):
                            load(t + 2, b)
                        for c in range(NC):
                            rows = ds(tl * P, P)
                            if kind == "qk":
                                sp.wait_ge(q_lo, tl * 3 + (qk0[t0] + c + 1))
                            else:
                                sp.wait_ge(acc_read[t0], tl * 3 + (c + 1))
                            if kind in ("split", "qk"):
                                sp.dma_start(opt["hi"][rows, cols(c)], sh[c][:]).then_inc(stored[c], 16)
                                sp.dma_start(opt["lo"][rows, cols(c)], sl[c][:]).then_inc(stored[c], 16)
                            elif kind in ("raw", "gate"):
                                sp.dma_start(opt["out"][rows, cols(c)], sh[c][:]).then_inc(stored[c], 32)
                steps(sp, nt // 2, pair)
            W = values["w"].shape[2]
            nhd = values["heads"]

            def store_half(half):
                for i in range(6 * half, 6 * half + 6):
                    sp.wait_ge(acc_read[NT], i + 1)
                    for part, stage in (("hi", sh), ("lo", sl)):
                        sp.dma_start(values[part].rearrange("h p i d -> p h i d")[:, :, i, :],
                                     stage[i % 3][:, 0:nhd * HD].rearrange("p (h d) -> p h d", d=HD)
                                     ).then_inc(stored[i % 3], 16)

            for u in range(VU):
                b = (NT + u) % 2
                sp.wait_ge(w_ready, NT + u - 1)
                sp.dma_start(raw[b][:, 0:W], values["w"][u % (VU // 2)]).then_inc(raw_in[b], 16)
                if u == VU // 2 + 1:
                    store_half(0)
            store_half(1)
            for c in range(3):
                sp.wait_ge(stored[c], 32 * (NT + TT // 3))

        @block.gpsimd
        def _(pool):
            def split(t, b, w, g, counts, free_sem=acc_ready):
                def v(x):
                    return x[:, 0:w].rearrange("p (k n) -> p k n", k=g.shape[1])
                gb = g.unsqueeze(2).to_broadcast([P, g.shape[1], w // g.shape[1]])
                pool.wait_ge(raw_in[b], counts[1])
                wait_count(pool, free_sem, counts[0])
                nc.gpsimd.tensor_tensor(v(wh[b]), v(raw[b]), gb, ALU.mult).then_inc(w_hi, 1)
                wait_count(pool, w_ready, t)
                nc.gpsimd.tensor_tensor(v(wg), v(raw[b]), gb, ALU.mult).then_inc(w_scaled, 1)
                pool.wait_ge(w_hi, t + 1)
                pool.wait_ge(w_scaled, t + 1)
                nc.gpsimd.tensor_tensor(wl[b][:, 0:w], wg[:, 0:w], wh[b][:, 0:w].bitcast(F32), ALU.subtract
                                        ).then_inc(w_ready, 1)

            split(0, 0, D, gain[:, 0:KT], (0, 16))
            lo = x_split(pool, x_lo_p, nc.gpsimd, 1)
            for c in range(NC):
                for k in range(1, KT, 2):
                    lo(c, k)
            if tabs:
                pool.wait_ge(t_done, 4)
            for kind, t0, nt, opt in groups:
                final = t0 + nt == NT

                def pair(i, first, last):
                    for b in range(2):
                        tl = i * 2 + b
                        if not (final and last and b == 1):
                            split(tl + (t0 + 1), 1 - b, D, gain[:, 0:KT],
                                  (tl * 3 + 3 * t0, i * 16 + (16 * (t0 // 2 + b) + 16)))
                        for c in range(NC if kind == "qk" else 0):
                            m = tl * 3 + (qk0[t0] + c)
                            pc = slice((c * CH) % SEQ, (c * CH) % SEQ + CH)
                            pool.wait_ge(q_sw, m + 1)
                            nc.gpsimd.tensor_tensor(ta[c][:], ta[c][:], tabs[opt["cos"]][1][:, pc], ALU.mult
                                                    ).then_inc(q_cos, 1)
                            nc.gpsimd.tensor_tensor(tb[c][:], tb[c][:], tabs[opt["sin"]][1][:, pc], ALU.mult
                                                    ).then_inc(q_sin, 1)
                steps(pool, nt // 2, pair)
            for u in range(VU):
                W = values["w"].shape[2]
                if u < 2:
                    free = (acc_ready, 3 * (NT + u) - 3)
                elif (u - 2) % (VU // 2) == VU // 2 - 1:
                    free = (acc_ready, 3 * NT + 6 * ((u - 2) // (VU // 2) + 1))
                else:
                    free = (v_used, u - 1 - (u - 2) // (VU // 2))
                ku = 2 * (u % (VU // 2))
                split(NT + u, (NT + u) % 2, W, gain[:, ku:ku + 2], (free[1], 16 * ((NT + u) // 2) + 16), free[0])

        @block.tensor
        def _(pe):
            def bank_free(t0, n):
                if isinstance(n, int) and n < 6:
                    before = [g for g in groups if g[1] < t0]
                    if before:
                        pe.wait_ge(acc_read[before[-1][1]], 3 * before[-1][2] + n - 5)
                else:
                    pe.wait_ge(acc_read[t0], n - 5)

            def square_sum(c):
                wait_count(pe, x_sd, c)
                for k in range(KT):
                    pe.wait_ge(x_sq, c * KT + k + 1)
                    nc.tensor.matmul(sums[0], ones[:], xsq[k % 2][:], start=(k == 0), stop=(k == KT - 1)
                                     ).then_inc(x_sum, 1)

            def chunk_split(c):
                if src is not None:
                    for cc in range(2) if c == 0 else range(c + 1, min(c + 2, NC)):
                        square_sum(cc)
                pe.wait_ge(x_lo_v, (c + 1) * (KT // 2))
                pe.wait_ge(x_lo_p, (c + 1) * (KT // 2))

            def head_sums(m, slot, t0, n_read):
                if isinstance(m, int) and m == 0:
                    pe.wait_ge(t_done, 4)
                pe.wait_ge(acc_read[t0], n_read)
                wait_count(pe, q_sd, m - 1)
                nc.tensor.matmul(sums[slot], sel[:], tsq[slot][:], start=True, stop=True).then_inc(q_sum, 1)

            for kind, t0, nt, opt in groups:
                def pair(i, first, last):
                    for b in range(2):
                        tl = i * 2 + b
                        t = tl + t0
                        pe.wait_ge(w_ready, t + 1)
                        for c in range(NC):
                            if t0 == 0 and first and b == 0:
                                chunk_split(c)
                            bank_free(t0, tl * 3 + c)
                            out = bank[3 * b + c]
                            for k in range(KT):
                                ks = slice(k * P, (k + 1) * P)
                                for j, (w, x) in enumerate(((wh[b], XH), (wh[b], XL), (wl[b], XH))):
                                    last_mm = nc.tensor.matmul(out, w[:, ks], x[:, k, cols(c)],
                                                               start=(k == 0 and j == 0),
                                                               stop=(k == KT - 1 and j == 2))
                            last_mm.then_inc(acc_ready, 1)
                            if kind == "qk" and not (first and b == 0 and c == 0):
                                head_sums(tl * 3 + (qk0[t0] + c - 1), (3 * b + c - 1) % 2, t0, tl * 3 + c)
                    if kind == "qk" and last:
                        head_sums(qk0[t0] + 3 * nt - 1, 1, t0, 3 * nt)
                assert t0 % 2 == 0 and nt % 2 == 0
                steps(pe, nt // 2, pair)
            W = values["w"].shape[2] // 2
            for u in range(VU):
                half, ku = u // (VU // 2), 2 * (u % (VU // 2))
                b = (NT + u) % 2
                pe.wait_ge(w_ready, NT + u + 1)
                for i in range(6):
                    if ku == 0:
                        bank_free(NT, 6 * half + i)
                    tok = slice((6 * half + i) * P, (6 * half + i + 1) * P)
                    for kk in range(2):
                        ws = slice(kk * W, (kk + 1) * W)
                        for j, (x, w) in enumerate(((XH, wh[b]), (XL, wh[b]), (XH, wl[b]))):
                            last_mm = nc.tensor.matmul(bank[i][:, 0:W], x[:, ku + kk, tok], w[:, ws],
                                                       start=(ku + kk + j == 0),
                                                       stop=(ku + kk == KT - 1 and j == 2))
                    if ku == KT - 2:
                        last_mm.then_inc(acc_ready, 1)
                if ku != KT - 2:
                    last_mm.then_inc(v_used, 1)

        @block.scalar
        def _(act):
            def square(c, k):
                n = c * KT + k
                if k == 0:
                    act.wait_ge(x_in[c], 16)
                wait_count(act, x_sum, n - 1)
                nc.scalar.activation(xsq[k % 2][:], XF[:, k, cols(c)], ACT.Square).then_inc(x_sq, 1)

            def deviation(c):
                act.wait_ge(x_sum, (c + 1) * KT)
                nc.scalar.activation(rstd[:, cols(c)], sums[0], ACT.Sqrt, bias=epst[:], scale=1.0 / D
                                     ).then_inc(x_sd, 1)

            if src is not None:
                for k in range(KT):
                    square(0, k)
                deviation(0)
            for c in range(NC):
                for k in range(KT):
                    act.wait_ge(x_h, c * KT + k + 1)
                    nc.scalar.activation(XH[:, k, cols(c)], XF[:, k, cols(c)], ACT.Copy).then_inc(x_hi, 1)
                    if src is not None and c + 1 < NC:
                        square(c + 1, k)
                if src is not None and c + 1 < NC:
                    deviation(c + 1)

            for kind, t0, nt, opt in groups:
                scale = opt.get("scale", 1.0)
                if kind == "gate" and nq:
                    act.wait_ge(q_lo, nq)

                def sd(m, slot):
                    act.wait_ge(q_sum, m + 1)
                    wait_count(act, q_done, m - 1)
                    nc.scalar.activation(tsd[slot][:], sums[slot], ACT.Sqrt, bias=epst[:], scale=1.0 / HD
                                         ).then_inc(q_sd, 1)

                def hi(m, c, uses, nhi):
                    act.wait_ge(q_done, m + 1)
                    wait_count(act, stored[c], uses)
                    nc.scalar.activation(sh[c][:].bitcast(F32R), ta[c][:], ACT.Copy).then_inc(hi_ready, 1)

                def pair(i, first, last):
                    for b in range(2):
                        tl = i * 2 + b
                        t = tl + t0
                        for c in range(NC):
                            products = bank[3 * b + c]
                            act.wait_ge(acc_ready, t * 3 + (c + 1))
                            m = tl * 3 + (qk0[t0] + c)
                            if kind == "raw":
                                wait_count(act, stored[c], t * 32)
                                nc.scalar.activation(sh[c][:], products, ACT.Copy).then_inc(acc_read[t0], 1)
                            elif kind == "split":
                                wait_count(act, stored[c], t * 32)
                                nc.scalar.activation(sh[c][:].bitcast(F32R), products, ACT.Copy, scale=scale
                                                     ).then_inc(hi_ready, 1)
                            elif kind == "gate":
                                wait_count(act, g_rcp, tl * 3 + (c - 2))
                                nc.scalar.activation(ta[c][:], products, ACT.Exp, scale=-1.0).then_inc(g_exp, 1)
                            elif kind == "qk":
                                wait_count(act, q_lo, m - 2)
                                nc.scalar.activation(ta[c][:], products, ACT.Copy).then_inc(q_raw, 1)
                                wait_count(act, q_sum, m - 1)
                                nc.scalar.activation(tsq[(3 * b + c) % 2][:], products, ACT.Square
                                                     ).then_inc(acc_read[t0], 1)
                                lag = 3 * b + c
                                if not (first and lag < 1):
                                    sd(m - 1, (lag - 1) % 2)
                                if not (first and lag < 2):
                                    hi(m - 2, (c - 2) % 3, (t if c >= 2 else t - 1) * 32, m - 2)
                    if kind == "qk" and last:
                        mm = qk0[t0] + 3 * nt
                        sd(mm - 1, 1)
                        hi(mm - 2, 1, (t0 + nt - 1) * 32, mm - 2)
                        hi(mm - 1, 2, (t0 + nt - 1) * 32, mm - 1)
                steps(act, nt // 2, pair)
            for i in range(TT):
                W = values["w"].shape[2] // 2
                act.wait_ge(acc_ready, 3 * NT + i + 1)
                act.wait_ge(stored[i % 3], 32 * (NT + i // 3))
                nc.scalar.activation(sh[i % 3][:, 0:W].bitcast(F32R), bank[i % 6][:, 0:W], ACT.Copy
                                     ).then_inc(hi_ready, 1)

        @block.vector
        def _(dve):
            lo_tile = x_split(dve, x_lo_v, nc.vector, 0)
            for c in range(NC):
                if src is not None:
                    dve.wait_ge(x_in[c], 16)
                    dve.wait_ge(x_sd, c + 1)
                    nc.vector.reciprocal(rstd[:, cols(c)], rstd[:, cols(c)]).then_inc(x_rstd, 1)
                    dve.wait_ge(x_rstd, c + 1)
                for k in range(KT):
                    nc.vector.tensor_tensor(XF[:, k, cols(c)], XF[:, k, cols(c)], rstd[:, cols(c)], ALU.mult
                                            ).then_inc(x_h, 1)
                    if k % 2 == 1:
                        lo_tile(c, k - 1)
            if tabs:
                dve.wait_ge(t_in, 16 * (len(tabs) + 2))
                for n, (name, (_, table)) in enumerate(tabs.items()):
                    nc.vector.tensor_scalar(table[:], table[:], hg[:, n:n + 1], HD ** -0.5 if n < 2 else 1.0,
                                            ALU.mult, ALU.mult).then_inc(t_done, 1)

            for kind, t0, nt, opt in groups:
                scale = opt.get("scale", 1.0)

                def norm_rope(m, c, slot):
                    dve.wait_ge(q_sd, m + 1)
                    nc.vector.reciprocal(tsd[slot][:], tsd[slot][:]).then_inc(q_rstd, 1)
                    dve.wait_ge(q_sin, m + 1)
                    dve.wait_ge(q_cos, m + 1)
                    nc.vector.tensor_tensor(ta[c][:], ta[c][:], tb[c][:], ALU.add).then_inc(q_rot, 1)
                    dve.wait_ge(q_rot, m + 1)
                    dve.wait_ge(q_rstd, m + 1)
                    nc.vector.tensor_tensor(ta[c][:], ta[c][:], tsd[slot][:], ALU.mult).then_inc(q_done, 1)

                def lo(m, c):
                    dve.wait_ge(hi_ready, hi0[t0] - qk0[t0] + m + 1)
                    dve.wait_ge(q_done, m + 1)
                    nc.vector.tensor_tensor(sl[c][:].bitcast(F32R), ta[c][:], sh[c][:], ALU.subtract
                                            ).then_inc(q_lo, 1)

                def pair(i, first, last):
                    for b in range(2):
                        tl = i * 2 + b
                        t = tl + t0
                        for c in range(NC):
                            products = bank[3 * b + c]
                            m = tl * 3 + (qk0[t0] + c)
                            if kind == "split":
                                dve.wait_ge(hi_ready, tl * 3 + (hi0[t0] + c + 1))
                                nc.vector.scalar_tensor_tensor(out=sl[c][:].bitcast(F32R), in0=products, scalar=scale,
                                                               in1=sh[c][:], op0=ALU.mult, op1=ALU.subtract
                                                               ).then_inc(acc_read[t0], 1)
                            elif kind == "gate":
                                g = tl * 3 + (c + 1)
                                dve.wait_ge(g_exp, g)
                                nc.vector.tensor_scalar(ta[c][:], ta[c][:], 1.0, None, ALU.add).then_inc(g_one, 1)
                                dve.wait_ge(g_one, g)
                                nc.vector.reciprocal(tb[c][:], ta[c][:]).then_inc(g_rcp, 1)
                                dve.wait_ge(g_rcp, g)
                                wait_count(dve, stored[c], t * 32)
                                nc.vector.tensor_tensor(sh[c][:], products, tb[c][:], ALU.mult).then_inc(acc_read[t0], 1)
                            elif kind == "qk":
                                lag = 3 * b + c
                                wait_apart(dve, q_raw, m + 1, q_seen)
                                nc.vector.stream_shuffle(tb[c][:], ta[c][:], SWAP16).then_inc(q_sw, 1)
                                if not (first and lag < 2):
                                    lo(m - 2, (c - 2) % 3)
                                if not (first and lag < 1):
                                    norm_rope(m - 1, (c - 1) % 3, (lag - 1) % 2)
                    if kind == "qk" and last:
                        mm = qk0[t0] + 3 * nt
                        norm_rope(mm - 1, 2, 1)
                        lo(mm - 2, 1)
                        lo(mm - 1, 2)
                if kind in ("split", "gate", "qk"):
                    steps(dve, nt // 2, pair)
            for i in range(TT):
                W = values["w"].shape[2] // 2
                dve.wait_ge(hi_ready, vhi0 + i + 1)
                nc.vector.tensor_tensor(sl[i % 3][:, 0:W].bitcast(F32R), bank[i % 6][:, 0:W],
                                        sh[i % 3][:, 0:W], ALU.subtract).then_inc(acc_read[NT], 1)


def latent_projections(nc, ar, S, A, ones, epst):
    scale = float(HD + ROPE) ** -0.5
    W3 = [("q", h, c) for h in range(8) for c in range(NC)] + [("k", j, c) for j in range(4) for c in range(NC)] \
        + [("v", i, 0) for i in range(TT)]
    units = [("r", 0, c) for c in range(NC)] + W3
    lat_in = [ar.sem(f"l_in{c}") for c in range(NC)]
    w_in, tab_in = ar.sem("l_w_in"), ar.sem("l_tab_in")
    sq_ready, sum_ready, sd_ready, rstd_ready = (ar.sem(f"l_{x}") for x in ("sq", "sum", "sd", "rstd"))
    n_ready, n_hi, n_lo = ar.sem("l_n"), ar.sem("l_n_hi"), ar.sem("l_n_lo")
    w_mul, w_hi, w_lo = ar.sem("l_w_mul"), ar.sem("l_w_hi"), ar.sem("l_w_lo")
    mm_done, u_raw, u_sw, u_cos, u_sin, u_rot, u_hi, u_lo = (
        ar.sem(f"l_u_{x}") for x in ("mm", "raw", "sw", "cos", "sin", "rot", "hi", "lo"))
    stored = [ar.sem(f"l_stored{i}") for i in range(3)]
    roped = {u: sum(x[0] in "qr" for x in units[:u]) for u in range(len(units) + 1)}
    with ar.scope() as sc:
        L = sc.sb("l_L", [P, 4, T])
        CH_ = sc.sb("l_ch", [P, 3, T], F32R)
        CL_ = sc.sb("l_cl", [P, 3, T], F32R)
        wr = sc.sb("l_wr", [P, 2560])
        wh = sc.sb("l_wh", [P, 2560], F32R)
        wl = sc.sb("l_wl", [P, 2560], F32R)
        g = sc.sb("l_g", [P, 3])
        cos, sin = sc.sb("l_cos", [P, SEQ]), sc.sb("l_sin", [P, SEQ])
        sq = [sc.sb(f"l_sq{i}", [P, CH]) for i in range(2)]
        sd = sc.sb("l_sd", [P, 2, CH])
        nt_ = [sc.sb(f"l_nt{i}", [P, CH]) for i in range(2)]
        ta = [sc.sb(f"l_ta{i}", [P, CH]) for i in range(3)]
        tb = [sc.sb(f"l_tb{i}", [P, CH]) for i in range(3)]
        sh = [sc.sb(f"l_sh{i}", [P, CH]) for i in range(3)]
        sl = [sc.sb(f"l_sl{i}", [P, CH]) for i in range(3)]
        acc = sc.banks("l_acc", 6)
        ssb = sc.banks("l_ssb", 2)
        bank = [acc[:, i * CH:(i + 1) * CH] for i in range(6)]
        sums = [ssb[:, i * CH:(i + 1) * CH] for i in range(2)]
        block = sc.enter_context(nc.Block())

        def cols(c):
            return slice(c * CH, (c + 1) * CH)

        def rows(kind):
            return {"q": slice(0, 96), "k": slice(0, P), "v": slice(0, P), "r": slice(64, 96)}[kind]

        @block.sync
        def _(sp):
            for c in range(NC):
                sp.dma_start(L[:, :, cols(c)], S["latent"].rearrange("(k p) t -> p k t", p=P)[:, :, cols(c)]
                             ).then_inc(lat_in[c], 16)
            sp.dma_start(wr[:, 0:1536].rearrange("p (k n) -> p k n", k=2),
                         A["w_uq"].rearrange("(k p) n -> p k n", p=P)).then_inc(w_in, 16)
            sp.dma_start(wr[:, 1536:2560], A["w_ukv"]).then_inc(w_in, 16)
            sp.dma_start(g[:], A["g_lat"]).then_inc(w_in, 16)
            sp.dma_start(cos[:], A["cosB"]).then_inc(tab_in, 16)
            sp.dma_start(sin[:], A["sinB"]).then_inc(tab_in, 16)
            for u, (kind, j, c) in enumerate(units):
                sp.wait_ge(u_lo, u + 1)
                s = u % 3
                for part, st in (("hi", sh), ("lo", sl)):
                    if kind == "q":
                        dst, src = S["qB", part][j * 96:(j + 1) * 96, cols(c)], st[s][0:96, :]
                    elif kind == "k":
                        dst, src = S["kB", part][j * P:(j + 1) * P, cols(c)], st[s][:]
                    elif kind == "r":
                        dst, src = S["krB", part][:, cols(c)], st[s][64:96, :]
                    else:
                        dst = S["vB", part].rearrange("h p i d -> p h i d")[:, :, j, :]
                        src = st[s][:].rearrange("p (h d) -> p h d", d=HD)
                    sp.dma_start(dst, src).then_inc(stored[s], 16)
            for s in range(3):
                sp.wait_ge(stored[s], 32 * len(range(s, len(units), 3)))

        parts = ((0, 2), (2, 1))

        @block.gpsimd
        def _(pool):
            pool.wait_ge(w_in, 48)
            gb = g[:, 0:2].unsqueeze(2).to_broadcast([P, 2, 768])
            for out in (wh, wr):
                nc.gpsimd.tensor_tensor(out[:, 0:1536].rearrange("p (k n) -> p k n", k=2),
                                        wr[:, 0:1536].rearrange("p (k n) -> p k n", k=2), gb, ALU.mult
                                        ).then_inc(w_mul, 1)
                nc.gpsimd.tensor_tensor(out[:, 1536:2560], wr[:, 1536:2560], g[:, 2:3].to_broadcast([P, 1024]),
                                        ALU.mult).then_inc(w_mul, 1)
            pool.wait_ge(w_mul, 4)
            nc.gpsimd.tensor_tensor(wl[:], wr[:], wh[:].bitcast(F32), ALU.subtract).then_inc(w_lo, 1)
            pool.wait_ge(w_lo, 1)
            pool.wait_ge(tab_in, 32)
            for u, (kind, j, c) in enumerate(units):
                if kind in "qr":
                    s, k = u % 3, roped[u]
                    pc = slice((c * CH) % SEQ, (c * CH) % SEQ + CH)
                    pool.wait_ge(u_sw, k + 1)
                    nc.gpsimd.tensor_tensor(ta[s][64:96, :], ta[s][64:96, :], cos[64:96, pc], ALU.mult
                                            ).then_inc(u_cos, 1)
                    nc.gpsimd.tensor_tensor(tb[s][64:96, :], tb[s][64:96, :], sin[64:96, pc], ALU.mult
                                            ).then_inc(u_sin, 1)

        @block.tensor
        def _(pe):
            n = 0
            for c in range(NC):
                for q, (k0, nk) in enumerate(parts):
                    x = 2 * c + q
                    wait_count(pe, sd_ready, x - 1)
                    for k in range(nk):
                        pe.wait_ge(sq_ready, n + 1)
                        nc.tensor.matmul(sums[q], ones[:], sq[n % 2][:], start=(k == 0), stop=(k == nk - 1)
                                         ).then_inc(sum_ready, 1)
                        n += 1
            pe.wait_ge(w_lo, 1)
            pe.wait_ge(n_lo, 9)
            for w, (kind, j, c) in enumerate(W3):
                u = w + 3
                wait_count(pe, u_raw, u - 5)
                b = bank[w % 6]
                if kind == "q":
                    for k in range(2):
                        ws = slice(k * 768 + j * 96, k * 768 + (j + 1) * 96)
                        for i, (a, x) in enumerate(((wh, CH_), (wh, CL_), (wl, CH_))):
                            mm = nc.tensor.matmul(b[0:96, :], a[:, ws], x[:, k, cols(c)],
                                                  start=(k == 0 and i == 0), stop=(k == 1 and i == 2))
                elif kind == "k":
                    ws = slice(1536 + j * P, 1536 + (j + 1) * P)
                    for i, (a, x) in enumerate(((wh, CH_), (wh, CL_), (wl, CH_))):
                        mm = nc.tensor.matmul(b, a[:, ws], x[:, 2, cols(c)], start=(i == 0), stop=(i == 2))
                else:
                    tok = slice(j * P, (j + 1) * P)
                    for i, (x, a) in enumerate(((CH_, wh), (CL_, wh), (CH_, wl))):
                        mm = nc.tensor.matmul(b, x[:, 2, tok], a[:, 2048:2560], start=(i == 0), stop=(i == 2))
                mm.then_inc(mm_done, 1)

        @block.scalar
        def _(act):
            n = m = 0
            for c in range(NC):
                act.wait_ge(lat_in[c], 16)
                for q, (k0, nk) in enumerate(parts):
                    for k in range(k0, k0 + nk):
                        wait_count(act, sum_ready, n - 1)
                        nc.scalar.activation(sq[n % 2][:], L[:, k, cols(c)], ACT.Square).then_inc(sq_ready, 1)
                        n += 1
                for q, (k0, nk) in enumerate(parts):
                    act.wait_ge(sum_ready, 3 * c + k0 + nk)
                    wait_count(act, n_ready, 3 * c)
                    nc.scalar.activation(sd[:, q, :], sums[q], ACT.Sqrt, bias=epst[:], scale=1.0 / (nk * P)
                                         ).then_inc(sd_ready, 1)
                for k in range(3):
                    act.wait_ge(n_ready, m + 1)
                    nc.scalar.activation(CH_[:, k, cols(c)], nt_[m % 2][:], ACT.Copy).then_inc(n_hi, 1)
                    m += 1

            def hi(u):
                kind, s = units[u][0], u % 3
                if kind in "qr":
                    act.wait_ge(u_rot, roped[u] + 1)
                wait_count(act, stored[s], 32 * (u // 3))
                act.wait_ge(u_raw, u + 1)
                nc.scalar.activation(sh[s][rows(kind), :].bitcast(F32R), ta[s][rows(kind), :], ACT.Copy
                                     ).then_inc(u_hi, 1)

            for u, (kind, j, c) in enumerate(units):
                s = u % 3
                wait_count(act, u_lo, u - 2)
                if kind == "r":
                    nc.scalar.activation(ta[s][64:96, :], L[64:96, 3, cols(c)], ACT.Copy).then_inc(u_raw, 1)
                else:
                    act.wait_ge(mm_done, u - 2)
                    nc.scalar.activation(ta[s][rows(kind), :], bank[(u - 3) % 6][rows(kind), :], ACT.Copy,
                                         scale=scale if kind == "q" else 1.0).then_inc(u_raw, 1)
                if u >= 2:
                    hi(u - 2)
            hi(len(units) - 2)
            hi(len(units) - 1)

        @block.vector
        def _(dve):
            m = 0
            for c in range(NC):
                dve.wait_ge(lat_in[c], 16)
                dve.wait_ge(sd_ready, 2 * c + 2)
                nc.vector.reciprocal(sd[:, 0, :], sd[:, 0, :]).then_inc(rstd_ready, 1)
                nc.vector.reciprocal(sd[:, 1, :], sd[:, 1, :]).then_inc(rstd_ready, 1)
                dve.wait_ge(rstd_ready, 2 * c + 2)
                for k in range(3):
                    wait_count(dve, n_lo, m - 1)
                    nc.vector.tensor_tensor(nt_[m % 2][:], L[:, k, cols(c)], sd[:, k // 2, :], ALU.mult
                                            ).then_inc(n_ready, 1)
                    dve.wait_ge(n_hi, m + 1)
                    dve.wait_ge(n_ready, m + 1)
                    nc.vector.tensor_tensor(CL_[:, k, cols(c)], nt_[m % 2][:], CH_[:, k, cols(c)].bitcast(F32),
                                            ALU.subtract).then_inc(n_lo, 1)
                    m += 1

            def rot(u):
                kind, s = units[u][0], u % 3
                if kind in "qr":
                    dve.wait_ge(u_cos, roped[u] + 1)
                    dve.wait_ge(u_sin, roped[u] + 1)
                    nc.vector.tensor_tensor(ta[s][64:96, :], ta[s][64:96, :], tb[s][64:96, :], ALU.add
                                            ).then_inc(u_rot, 1)

            def lo(u):
                kind, s = units[u][0], u % 3
                dve.wait_ge(u_hi, u + 1)
                if kind in "qr":
                    dve.wait_ge(u_rot, roped[u] + 1)
                r = rows(kind)
                nc.vector.tensor_tensor(sl[s][r, :].bitcast(F32R), ta[s][r, :], sh[s][r, :], ALU.subtract
                                        ).then_inc(u_lo, 1)

            for u, (kind, j, c) in enumerate(units):
                if kind in "qr":
                    dve.wait_ge(u_raw, u + 1)
                    nc.vector.stream_shuffle(tb[u % 3][64:96, :], ta[u % 3][64:96, :], SWAP16).then_inc(u_sw, 1)
                if u >= 1:
                    rot(u - 1)
                if u >= 2:
                    lo(u - 2)
            rot(len(units) - 1)
            lo(len(units) - 2)
            lo(len(units) - 1)



def attention(nc, ar, tag, A, heads, unroll, load_a, load_b, n_a, n_b, KQ, o_head0, S, biased=False):
    stacked = KQ == HD
    KA = KQ + AUG
    NP, NS = SEQ // P, DEC // P
    LAG = 3
    NU = 2 * NP + NS
    MAXES = {3: (0, 1), 4: (2, 3), 5: (4, 5, 6), 6: (7, 8, 9), 7: (10, 11, 12), 8: (13, 14, 15),
             9: (16, 17, 18, 19)}
    HI_V = [0, 1, 2]
    HI_S = [s for s in range(10) if s not in HI_V]
    LO_P = [1, 3, 5, 7, 8, 9]
    LO_V = [s for s in range(10) if s not in LO_P]
    in_a = [ar.sem(f"{tag}_in_a{i}") for i in range(2)]
    in_b = [ar.sem(f"{tag}_in_b{i}") for i in range(2)]
    const_in, const_set = ar.sem(f"{tag}_const_in"), ar.sem(f"{tag}_const_set")
    s_ready = ar.sem(f"{tag}_s_ready")
    e_done = ar.sem(f"{tag}_e_done")
    p_hi_v, p_hi_s = ar.sem(f"{tag}_p_hi_v"), ar.sem(f"{tag}_p_hi_s")
    p_lo_v, p_lo_p = ar.sem(f"{tag}_p_lo_v"), ar.sem(f"{tag}_p_lo_p")
    pv_done = ar.sem(f"{tag}_pv_done")
    m_ready, m_done = ar.sem(f"{tag}_m_ready"), ar.sem(f"{tag}_m_done")
    m_both = ar.sem(f"{tag}_m_both")
    mt_ready, aug_done = ar.sem(f"{tag}_mt"), ar.sem(f"{tag}_aug")
    o_prompt, o_sample = ar.sem(f"{tag}_o_prompt"), ar.sem(f"{tag}_o_sample")
    o_stored = [ar.sem(f"{tag}_o_stored{i}") for i in range(2)]
    if biased:
        b_hi, b_sum, b_lo = ar.sem(f"{tag}_b_hi"), ar.sem(f"{tag}_b_sum"), ar.sem(f"{tag}_b_lo")
        m_seen = ar.sem(f"{tag}_m_seen")
    with ar.scope() as sc:
        KS = P if stacked else KQ
        Q1 = [sc.sb(f"{tag}_Q1{i}", [P, T], F32R) for i in range(2)]
        K2 = [sc.sb(f"{tag}_K2{i}", [P, T], F32R) for i in range(2)]
        Q3 = [sc.sb(f"{tag}_Q3{i}", [P, T], F32R) for i in range(2)]
        K3 = [sc.sb(f"{tag}_K3{i}", [P, T], F32R) for i in range(2)]
        VH = [sc.sb(f"{tag}_VH{i}", [P, TT, HD + 2], F32R) for i in range(2)]
        VL = [sc.sb(f"{tag}_VL{i}", [P, TT, HD + 2], F32R) for i in range(2)]
        PF = [sc.sb(f"{tag}_PF{i}", [P, 2 * CH]) for i in range(4)]
        PH = [sc.sb(f"{tag}_PH{i}", [P, 2 * CH], F32R) for i in range(4)]
        PL = [sc.sb(f"{tag}_PL{i}", [P, 2 * CH], F32R) for i in range(4)]
        OB = [sc.sb(f"{tag}_OB{i}", [HD + 1, T]) for i in range(2)]
        MH = sc.sb(f"{tag}_MH", [P, NP, 2])
        M = sc.sb(f"{tag}_M", [P, 2 * AUG])
        ident = sc.sb(f"{tag}_ident", [P, P])
        negsel = sc.sb(f"{tag}_negsel", [AUG, AUG, P])
        if biased:
            identr = sc.sb(f"{tag}_identr", [P, P], F32R)
            BD, BL_ = sc.sb(f"{tag}_BD", [P, BW]), sc.sb(f"{tag}_BL", [P, BW])
            slope = sc.sb(f"{tag}_slope", [P, 8])
            BF = sc.sb(f"{tag}_BF", [P, BW])
            BS = sc.sb(f"{tag}_BS", [P, 2 * CH])
            Bhi = [sc.sb(f"{tag}_Bhi{i}", [P, BW], F32R) for i in range(2)]
            Blo = [sc.sb(f"{tag}_Blo{i}", [P, BW], F32R) for i in range(2)]
        SA = sc.banks(f"{tag}_SA", 2)
        SM = sc.banks(f"{tag}_SM", 2)
        OP = sc.banks(f"{tag}_OP", 2)
        OS = sc.banks(f"{tag}_OS", 1)
        MT = sc.banks(f"{tag}_MT", 1)
        block = sc.enter_context(nc.Block())
        bufs = [dict(Q1=Q1[i], K2=K2[i], Q3=Q3[i], K3=K3[i], VH=VH[i], VL=VL[i]) for i in range(2)]
        NIT = heads // unroll
        n_const = 5 if biased else 2
        n_set = 8 if biased else 7

        def head_of(i, j):
            return i * unroll + j, j % 2, i * (unroll // 2) + j // 2

        def hi_count(h, s):
            a, sem_ = (HI_V, p_hi_v) if s in HI_V else (HI_S, p_hi_s)
            return sem_, h * len(a) + (a.index(s) + 1)

        def lo_count(h, s):
            a, sem_ = (LO_V, p_lo_v) if s in LO_V else (LO_P, p_lo_p)
            return sem_, h * len(a) + (a.index(s) + 1)

        @block.sync
        def _(sp):
            for dst, src in [(ident[:], A["ident"]), (negsel[:], A["negsel"])] + (
                    [(BD[:], A["bias_dist"]), (BL_[:], A["bias_count"]), (slope[:], A["slopes"])] if biased else []):
                sp.dma_start(dst, src).then_inc(const_in, 16)

            def load(h, b, i, j):
                wait_count(sp, s_ready, h * 10 - 10)
                wait_count(sp, m_done, h * NU - NU)
                for dst, src in load_a(h, i, j, bufs[b]):
                    sp.dma_start(dst.bitcast(F32), src).then_inc(in_a[b], 16)
                wait_count(sp, pv_done, h * 10 - 10)
                for dst, src in load_b(h, i, j, bufs[b]):
                    sp.dma_start(dst.bitcast(F32), src).then_inc(in_b[b], 16)

            load(0, 0, 0, 0)
            load(1, 1, 0, 1)

            def body(i, first, last):
                for j in range(unroll):
                    h, b, _ = head_of(i, j)
                    if not (last and j >= unroll - 2):
                        load(h + 2, b, i + (j + 2) // unroll, (j + 2) % unroll)
                    sp.wait_ge(o_sample, h + 1)
                    sp.dma_start(S["O"][ds(h * HD + o_head0 * HD, HD), :], OB[b][0:HD, :]).then_inc(o_stored[b], 16)
                    sp.dma_start(S["Z"][ds(h + o_head0, 1), :], OB[b][HD:HD + 1, :]).then_inc(o_stored[b], 16)
            steps(sp, NIT, body)
            for b in range(2):
                sp.wait_ge(o_stored[b], 32 * (heads // 2))

        @block.tensor
        def _(pe):
            def max_unit(h, b, fills, u):
                if u == 0:
                    pe.wait_ge(in_a[b], fills * 16 * n_a + 16 * n_a)
                wait_count(pe, m_done, h * NU + (u - 1))
                q, k = (Q1[b][:], K2[b][:]) if stacked else (Q1[b][0:KQ, :], K3[b][0:KQ, :])
                if u < 2 * NP:
                    q0, k0 = (u // 2) * P, (u % 2) * CH
                else:
                    q0, k0 = SEQ + (u - 2 * NP) * P, SEQ
                nc.tensor.matmul(SM[:, (u % 2) * CH:(u % 2 + 1) * CH], q[:, q0:q0 + P], k[:, k0:k0 + CH],
                                 start=True, stop=True).then_inc(m_ready, 1)

            def transpose_max(h, sample):
                if sample:
                    pe.wait_ge(m_done, h * NU + NU)
                else:
                    pe.wait_ge(m_both, h + 1)
                wait_count(pe, aug_done, h * 2 + sample)
                nc.tensor.matmul(MT[0:AUG, 0:P], M[:, sample * AUG:(sample + 1) * AUG], ident[:],
                                 start=True, stop=True).then_inc(mt_ready, 1)

            def scores(h, b, fills, s, g):
                if s == 0:
                    pe.wait_ge(in_b[b], fills * 16 * n_b + 16 * n_b)
                    pe.wait_ge(aug_done, h * 2 + 1)
                    if biased:
                        pe.wait_ge(b_lo, h + 1)
                if s == NP:
                    pe.wait_ge(aug_done, h * 2 + 2)
                wait_count(pe, e_done, g)
                for x in range(2):
                    out = SA[:, x * CH:(x + 1) * CH]
                    if s < NP:
                        q0, k0, base = x * CH, s * P, 0
                    else:
                        q0, k0, base = SEQ, SEQ + (2 * (s - NP) + x) * P, SEQ
                    qs, ks = slice(q0, q0 + CH), slice(k0, k0 + P)
                    mms = [(K2[b][0:KS, ks], Q1[b][0:KS, qs], None), (K3[b][0:KA, ks], Q3[b][0:KA, qs], None)]
                    if not stacked:
                        mms.insert(0, (K3[b][0:KQ, ks], Q1[b][0:KQ, qs], None))
                    if biased:
                        off = q0 - k0 + BW - SEQ
                        mms.insert(1, (identr[:], Bhi[b][:, off:off + CH], None))
                        n0, n1 = max(0, k0 - q0 - 256), min(CH, k0 - q0 + P + 256)
                        if n0 < n1:
                            mms.insert(2, (identr[:], Blo[b][:, off + n0:off + n1], (n0, n1)))
                    for i, (w, y, part) in enumerate(mms):
                        o = out if part is None else out[:, part[0]:part[1]]
                        mm = nc.tensor.matmul(o, w, y, start=(i == 0), stop=(i == len(mms) - 1),
                                              skip_group_check=biased)
                mm.then_inc(s_ready, 1)

            def pv(h, b, s, g, p, between=None):
                if s == 0:
                    wait_count(pe, o_prompt, h)
                if s == NP:
                    wait_count(pe, o_sample, h)
                pe.wait_ge(*hi_count(h, s))
                pe.wait_ge(*lo_count(h, s))
                for x in range(2):
                    pc = slice(x * CH, (x + 1) * CH)
                    if s < NP:
                        kt, out, st, en = s, OP[0:HD + 1, pc], s == 0, s == NP - 1
                    else:
                        kt, out = NP + 2 * (s - NP) + x, OS[0:HD + 1, :]
                        st, en = (s == NP and x == 0), (s == NP + 1 and x == 1)
                    for i, (w, y) in enumerate(((VH, PH), (VL, PH), (VH, PL))):
                        mm = nc.tensor.matmul(out, w[b][:, kt, 0:HD + 1], y[p][:, pc],
                                              start=(st and i == 0), stop=(en and i == 2))
                    if x == 0 and between is not None:
                        max_unit(*between)
                mm.then_inc(pv_done, 1)

            pe.wait_ge(const_in, 16 * n_const)
            pe.wait_ge(const_set, n_set)
            for u in range(NU):
                max_unit(0, 0, 0, u)
            transpose_max(0, 0)

            def body(i, first, last):
                for j in range(unroll):
                    h, b, fills = head_of(i, j)
                    hn, bn, fn = head_of(i, j + 1)
                    final = last and j == unroll - 1
                    for s in range(10):
                        scores(h, b, fills, s, h * 10 + s)
                        if s == 0:
                            transpose_max(h, 1)
                        if s == 9 and not final:
                            transpose_max(hn, 0)
                        units = MAXES.get(s, ()) if not final else ()
                        lead = len(units) - 2
                        for u in units[:max(lead, 0)]:
                            max_unit(hn, bn, fn, u)
                        between = (hn, bn, fn, units[max(lead, 0)]) if units else None
                        if s >= LAG:
                            pv(h, b, s - LAG, h * 10 + s - LAG, (j * 10 + s - LAG) % 4, between)
                        elif not (first and j == 0):
                            pv(h - 1, 1 - b, s + 10 - LAG, h * 10 + s - LAG, (j * 10 + s - LAG) % 4)
                        for u in units[max(lead, 0) + 1:]:
                            max_unit(hn, bn, fn, u)
                if last:
                    for s in range(10 - LAG, 10):
                        pv(h, b, s, h * 10 + s, (j * 10 + s) % 4)
            steps(pe, NIT, body)

        @block.scalar
        def _(act):
            if biased:
                act.wait_ge(const_in, 16 * n_const)
                nc.scalar.activation(identr[:], ident[:], ACT.Copy).then_inc(const_set, 1)

            def evac_prompt(h, b, fills):
                wait_count(act, o_stored[b], fills * 32)
                act.wait_ge(pv_done, h * 10 + NP)
                nc.scalar.activation(OB[b][:, 0:SEQ], OP[0:HD + 1, :], ACT.Copy).then_inc(o_prompt, 1)

            def evac_sample(h, b):
                act.wait_ge(pv_done, h * 10 + 10)
                act.wait_ge(o_prompt, h + 1)
                nc.scalar.activation(OB[b][:, SEQ:T], OS[0:HD + 1, :], ACT.Copy).then_inc(o_sample, 1)

            def body(i, first, last):
                for j in range(unroll):
                    h, b, fills = head_of(i, j)
                    for s in range(10):
                        g, p = h * 10 + s, (j * 10 + s) % 4
                        act.wait_ge(s_ready, g + 1)
                        wait_count(act, pv_done, g - 3)
                        nc.scalar.activation(PF[p][:], SA[:], ACT.Exp).then_inc(e_done, 1)
                        if s in HI_S:
                            act.wait_ge(e_done, g + 1)
                            nc.scalar.activation(PH[p][:], PF[p][:], ACT.Copy).then_inc(p_hi_s, 1)
                        if s == 1 and not (first and j == 0):
                            evac_prompt(h - 1, 1 - b, i * (unroll // 2) + (j - 1) // 2)
                        if s == 3 and not (first and j == 0):
                            evac_sample(h - 1, 1 - b)
                if last:
                    evac_prompt(h, b, fills)
                    evac_sample(h, b)
            steps(act, NIT, body)

        @block.vector
        def _(dve):
            for b in range(2):
                nc.vector.memset(K3[b][KQ:KA, :].bitcast(F32), 1.0).then_inc(const_set, 1)
                nc.vector.memset(VH[b][:, :, HD:HD + 1].bitcast(F32), 1.0).then_inc(const_set, 1)
                nc.vector.memset(VL[b][:, :, HD:HD + 1].bitcast(F32), 0.0).then_inc(const_set, 1)
            nc.vector.memset(M[:], 0.0).then_inc(const_set, 1)
            dve.wait_ge(const_in, 16 * n_const)
            dve.wait_ge(const_set, n_set)

            def bias(h, b):
                wait_count(dve, s_ready, h * 10 - 10)
                sl = slope[:, ds(h, 1)]
                nc.vector.scalar_tensor_tensor(out=Bhi[b][:], in0=BD[:], scalar=sl, in1=BL_[:],
                                               op0=ALU.mult, op1=ALU.add).then_inc(b_hi, 1)
                wait_count(dve, b_lo, h)
                nc.vector.scalar_tensor_tensor(out=BF[:], in0=BD[:], scalar=sl, in1=BL_[:],
                                               op0=ALU.mult, op1=ALU.add).then_inc(b_sum, 1)

            def maximum(h, b, u):
                x = u % 2
                src = SM[:, x * CH:(x + 1) * CH]
                qi = u // 2 if u < 2 * NP else u - 2 * NP
                dst = MH[:, qi, x:x + 1] if u < 2 * NP else M[:, AUG + qi:AUG + qi + 1]
                if not biased:
                    dve.wait_ge(m_ready, h * NU + (u + 1))
                    nc.vector.reduce_max(dst, src, axis=AX_X).then_inc(m_done, 1)
                else:
                    off = BW - SEQ - qi * P + (x * CH if u < 2 * NP else 0)
                    if u == 0:
                        dve.wait_ge(b_hi, h + 1)
                    wait_apart(dve, m_ready, h * NU + (u + 1), m_seen)
                    nc.vector.tensor_tensor_reduce(
                        out=BS[:, x * CH:(x + 1) * CH], in0=src, in1=Bhi[b][:, off:off + CH].bitcast(F32), scale=1.0,
                        scalar=-3.0e38, op0=ALU.add, op1=ALU.max, accum_out=dst).then_inc(m_done, 1)
                if u == 2 * NP - 1:
                    dve.wait_ge(m_done, h * NU + 2 * NP)
                    nc.vector.tensor_tensor(M[:, 0:NP], MH[:, :, 0], MH[:, :, 1], ALU.max).then_inc(m_both, 1)

            def augment(h, b, sample):
                dve.wait_ge(mt_ready, h * 2 + sample + 1)
                wait_count(dve, s_ready, h * 10 - 10)
                nt = NS if sample else NP
                t0 = SEQ if sample else 0
                nc.vector.tensor_tensor(
                    Q3[b][KQ:KA, t0:t0 + nt * P].rearrange("r (i n) -> r i n", n=P),
                    MT[0:AUG, 0:P].unsqueeze(1).to_broadcast([AUG, nt, P]), negsel[:, 0:nt, :], ALU.mult
                ).then_inc(aug_done, 1)

            def low(h, s, g, p):
                dve.wait_ge(*hi_count(h, s))
                nc.vector.tensor_tensor(PL[p][:], PF[p][:], PH[p][:].bitcast(F32), ALU.subtract).then_inc(p_lo_v, 1)

            if biased:
                bias(0, 0)
            for u in range(NU):
                maximum(0, 0, u)
            augment(0, 0, 0)

            def body(i, first, last):
                for j in range(unroll):
                    h, b, fills = head_of(i, j)
                    hn, bn, _ = head_of(i, j + 1)
                    final = last and j == unroll - 1
                    for s in range(10):
                        g, p = h * 10 + s, (j * 10 + s) % 4
                        if s == 0:
                            augment(h, b, 1)
                        if s in HI_V:
                            dve.wait_ge(e_done, g + 1)
                            nc.vector.tensor_copy(PH[p][:], PF[p][:]).then_inc(p_hi_v, 1)
                        if s == 1 and biased and not final:
                            bias(hn, bn)
                        if s == 9 and not final:
                            augment(hn, bn, 0)
                        units = MAXES.get(s, ()) if not final else ()
                        for u in units[0:1]:
                            maximum(hn, bn, u)
                        if s - 1 in LO_V:
                            low(h, s - 1, g - 1, (p - 1) % 4)
                        for u in units[1:]:
                            maximum(hn, bn, u)
            steps(dve, NIT, body)

        @block.gpsimd
        def _(pool):
            def bias_low(h, b):
                pool.wait_ge(b_hi, h + 1)
                pool.wait_ge(b_sum, h + 1)
                nc.gpsimd.tensor_tensor(Blo[b][:], BF[:], Bhi[b][:].bitcast(F32), ALU.subtract).then_inc(b_lo, 1)

            if biased:
                bias_low(0, 0)

            def body(i, first, last):
                for j in range(unroll):
                    h, b, _ = head_of(i, j)
                    hn, bn, _ = head_of(i, j + 1)
                    if biased and not (last and j == unroll - 1):
                        bias_low(hn, bn)
                    for s in LO_P:
                        p = (j * 10 + s) % 4
                        pool.wait_ge(*hi_count(h, s))
                        nc.gpsimd.tensor_tensor(PL[p][:], PF[p][:], PH[p][:].bitcast(F32), ALU.subtract
                                                ).then_inc(p_lo_p, 1)
            steps(pool, NIT, body)



def output_projection(nc, ar, l, S, A, Y, rstd_next, gpost, ones, epst, xin, xout):
    tag = f"o{l}"
    nxt = rstd_next is not None
    row0 = 16 * l
    NB = 5
    N = 16 * T // P
    z_in, z_rcp, z_hi, z_lo, z_out = (ar.sem(f"{tag}_z_{n}") for n in ("in", "rcp", "hi", "lo", "out"))
    rz_in, sel_in, sel_set = ar.sem(f"{tag}_rz_in"), ar.sem(f"{tag}_sel_in"), ar.sem(f"{tag}_sel_set")
    w_in = [ar.sem(f"{tag}_w_in{t}") for t in range(KT)]
    w_hi, w_lo = ar.sem(f"{tag}_w_hi"), ar.sem(f"{tag}_w_lo")
    o_in = [ar.sem(f"{tag}_o_in{n}") for n in ("0a", "0b", "1", "2")]
    g_in = [ar.sem(f"{tag}_g_in{i}") for i in range(2)]
    r_ready = ar.sem(f"{tag}_r_ready")
    o_div, o_gated = ar.sem(f"{tag}_o_div"), ar.sem(f"{tag}_o_gated")
    x_hi, x_lo = ar.sem(f"{tag}_x_hi"), ar.sem(f"{tag}_x_lo")
    acc_ready, y_sq, y_added = ar.sem(f"{tag}_acc_ready"), ar.sem(f"{tag}_y_sq"), ar.sem(f"{tag}_y_added")
    y_raw = ar.sem(f"{tag}_y_raw")
    sum_ready, sd_ready = ar.sem(f"{tag}_sum_ready"), ar.sem(f"{tag}_sd_ready")
    rstd_ready, next_ready = ar.sem(f"{tag}_rstd_ready"), ar.sem(f"{tag}_next_ready")
    res_in = [ar.sem(f"{tag}_res_in{i}") for i in range(2)]
    y_scaled, y_ready, y_out = ar.sem(f"{tag}_y_scaled"), ar.sem(f"{tag}_y_ready"), ar.sem(f"{tag}_y_out")
    n_sq, n_added = ar.sem(f"{tag}_n_sq"), ar.sem(f"{tag}_n_added")
    sums_order = [("y", 0), ("y", 1), ("n", 0), ("y", 2), ("n", 1), ("n", 2)] if nxt else [("y", c) for c in range(NC)]
    YF, YR = Y
    with ar.scope() as sc:
        WH = sc.sb(f"{tag}_WH", [P, KT, D], F32R)
        WF, WL = sc.both(f"{tag}_WL", [P, KT, D])
        XH = [sc.sb(f"{tag}_XH{i}", [P, KT, CH], F32R) for i in range(2)]
        EF, ER = sc.both(f"{tag}_extra", [P, KT, CH])
        G = [sc.sb(f"{tag}_G{i}", [P, CH]) for i in range(2)]
        R = [sc.sb(f"{tag}_res{i}", [P, CH]) for i in range(2)]
        sq = [sc.sb(f"{tag}_sq{i}", [P, CH]) for i in range(2)]
        sq_sum = sc.sb(f"{tag}_sq_sum", [P, CH])
        rstd = sc.sb(f"{tag}_rstd", [P, CH])
        RZ = sc.sb(f"{tag}_RZ", [32, T], F32R)
        sel = sc.sb(f"{tag}_sel", [32, D], F32R)
        z, zh, zl = sc.sb(f"{tag}_z", [P, N]), sc.sb(f"{tag}_zh", [P, N], F32R), sc.sb(f"{tag}_zl", [P, N], F32R)
        if nxt:
            nsq, nsq_sum = sc.sb(f"{tag}_nsq", [P, CH]), sc.sb(f"{tag}_nsq_sum", [P, CH])
        acc = sc.banks(f"{tag}_acc", NB)
        rb = sc.banks(f"{tag}_rb", 2)
        sums = sc.banks(f"{tag}_sums", 1)
        block = sc.enter_context(nc.Block())

        def cols(c):
            return slice(c * CH, (c + 1) * CH)

        def low(c, as_f32r=False):
            if c == NC - 1:
                return (ER if as_f32r else EF)[:]
            return (YR if as_f32r else YF)[:, :, cols(c + 1)]

        def stages():
            for period in range(-1, NC + 2 if nxt else NC + 1):
                g, a, p, x = (c if 0 <= c < NC else None for c in (period + 1, period, period - 1, period - 2))
                for t in range(KT + 2):
                    live = t < KT
                    yield (period, t, g if live else None, a if live else None, p, x if live and nxt else None)

        @block.sync
        def _(sp):
            def flat(x):
                return x[row0:row0 + 16, :].rearrange("h (a n) -> (h a) n", n=N)

            def load_o(i, c, k0, k1):
                sp.dma_start(low(c)[:, k0:k1, :],
                             S["O"][row0 * HD:row0 * HD + D, cols(c)].rearrange("(k p) t -> p k t", p=P)[:, k0:k1, :]
                             ).then_inc(o_in[i], 16)

            def load_gate(n):
                c, k = n // KT, n % KT
                sp.dma_start(G[n % 2][:], S[f"gate{l}"][k * P:(k + 1) * P, cols(c)]).then_inc(g_in[n % 2], 16)

            def load_w(t):
                sp.dma_start(WF[:, t, :], A[f"w_out{l}"][t]).then_inc(w_in[t], 16)

            def load_res(m):
                c, k = m // KT, m % KT
                sp.dma_start(R[m % 2][:], xin[k * P:(k + 1) * P, cols(c)]).then_inc(res_in[m % 2], 16)

            def store(m):
                c, k = m // KT, m % KT
                sp.dma_start(xout[k * P:(k + 2) * P, cols(c)].rearrange("(k p) t -> p k t", p=P),
                             YF[:, k:k + 2, cols(c)]).then_inc(y_out, 16)

            sp.dma_start(z[:], flat(S["Z"])).then_inc(z_in, 16)
            load_o(0, 0, 0, KT // 2)
            sp.dma_start(YF[0:32, 0:2, 0:CH], A["denominator_rows"].rearrange("r (a n) -> r a n", n=CH)
                         ).then_inc(sel_in, 16)
            load_gate(0)
            load_gate(1)
            sp.wait_ge(z_hi, 1)
            sp.dma_start(flat(S["RZ", "hi"]), zh[:].bitcast(F32)).then_inc(z_out, 16)
            sp.wait_ge(z_lo, 1)
            sp.dma_start(flat(S["RZ", "lo"]), zl[:].bitcast(F32)).then_inc(z_out, 16)
            load_o(1, 0, KT // 2, KT)
            load_w(0)
            sp.wait_ge(z_out, 32)
            for i, part in enumerate(("hi", "lo")):
                sp.dma_start(RZ[16 * i:16 * i + 16, :].bitcast(F32), S["RZ", part][row0:row0 + 16, :]
                             ).then_inc(rz_in, 16)
            load_w(1)
            for period, t, g, a, p, x in stages():
                if g is not None:
                    n = g * KT + t
                    sp.wait_ge(o_gated, n + 1)
                    if n + 2 < NC * KT:
                        load_gate(n + 2)
                if period == -1 and t + 2 < KT:
                    load_w(t + 2)
                if period == -1 and t == KT:
                    load_o(2, 1, 0, KT)
                    load_res(0)
                    load_o(3, 2, 0, KT)
                if p is not None and t >= 2:
                    m = p * KT + t - 2
                    wait_count(sp, y_ready, m)
                    if m + 1 < NC * KT:
                        load_res(m + 1)
                    if m % 2 == 0 and m > 0:
                        store(m - 2)
            sp.wait_ge(y_ready, NC * KT)
            store(NC * KT - 2)
            sp.wait_ge(y_out, 16 * NC * KT // 2)

        @block.gpsimd
        def _(pool):
            for t in range(KT):
                pool.wait_ge(w_hi, t + 1)
                nc.gpsimd.tensor_tensor(WL[:, t, :], WF[:, t, :], WH[:, t, :].bitcast(F32), ALU.subtract
                                        ).then_inc(w_lo, 1)
            if nxt:
                for c in range(NC):
                    for k in range(1, KT):
                        pool.wait_ge(n_sq, c * KT + k + 1)
                        wait_count(pool, n_added, c * (KT - 1) + k - 1)
                        nc.gpsimd.tensor_tensor(nsq_sum[:], nsq_sum[:], nsq[:], ALU.add).then_inc(n_added, 1)

        @block.tensor
        def _(pe):
            def square_sum(kind, c):
                i = sums_order.index((kind, c))
                wait_count(pe, sd_ready, i)
                pe.wait_ge(y_added if kind == "y" else n_added, (c + 1) * (KT - 1))
                nc.tensor.matmul(sums[:], ones[:], (sq_sum if kind == "y" else nsq_sum)[:], start=True, stop=True
                                 ).then_inc(sum_ready, 1)

            pe.wait_ge(sel_set, 1)
            pe.wait_ge(rz_in, 32)
            for period, t, g, a, p, x in stages():
                if g is not None:
                    n = g * KT + t
                    wait_count(pe, o_div, n - 1)
                    nc.tensor.matmul(rb[:, cols(n % 2)], sel[:, t * P:(t + 1) * P], RZ[:, cols(g)], start=True,
                                     stop=True).then_inc(r_ready, 1)
                if a is not None:
                    n = a * KT + t
                    if t == 0:
                        pe.wait_ge(x_lo, (a + 1) * KT)
                    if a == 0:
                        pe.wait_ge(w_lo, t + 1)
                    wait_count(pe, y_sq, n - NB + 1)
                    for k in range(KT):
                        ks = slice(k * P, (k + 1) * P)
                        xh, xl = XH[a % 2][:, k, :], low(a, True)[:, k, :]
                        for j, (w, y) in enumerate(((WH, xh), (WH, xl), (WL, xh))):
                            mm = nc.tensor.matmul(acc[:, cols(n % NB)], w[:, t, ks], y, start=(k + j == 0),
                                                  stop=(k == KT - 1 and j == 2))
                    mm.then_inc(acc_ready, 1)
                if t == 0 and p is not None:
                    square_sum("y", p)
                if t == 4 and x is not None:
                    square_sum("n", x)

        @block.scalar
        def _(act):
            def high_weights(t):
                act.wait_ge(w_in[t], 16)
                nc.scalar.activation(WH[:, t, :], WF[:, t, :], ACT.Copy).then_inc(w_hi, 1)

            def deviation(kind, c):
                act.wait_ge(sum_ready, sums_order.index((kind, c)) + 1)
                if kind == "y":
                    wait_count(act, y_ready, c * KT)
                out = rstd[:] if kind == "y" else rstd_next[:, cols(c)]
                nc.scalar.activation(out, sums[:], ACT.Sqrt, bias=epst[:], scale=1.0 / D).then_inc(sd_ready, 1)

            act.wait_ge(z_rcp, 1)
            nc.scalar.activation(zh[:], z[:], ACT.Copy).then_inc(z_hi, 1)
            act.wait_ge(sel_in, 16)
            nc.scalar.activation(sel[:].rearrange("r (a n) -> r a n", n=CH), YF[0:32, 0:2, 0:CH], ACT.Copy
                                 ).then_inc(sel_set, 1)
            for period, t, g, a, p, x in stages():
                if period == 0 and t < KT - 2:
                    high_weights(t + 2)
                if g is not None:
                    act.wait_ge(o_gated, g * KT + t + 1)
                    wait_count(act, acc_ready, (g - 1) * KT)
                    nc.scalar.activation(XH[g % 2][:, t, :], low(g)[:, t, :], ACT.Copy).then_inc(x_hi, 1)
                if period == -1 and t in (KT - 2, KT - 1):
                    high_weights(t - (KT - 2))
                if p is not None and t >= 2 and nxt:
                    k = t - 2
                    act.wait_ge(y_ready, p * KT + k + 1)
                    wait_count(act, n_added, p * (KT - 1) + max(k - 1, 0))
                    if k == 0 and p > 0:
                        act.wait_ge(sum_ready, sums_order.index(("n", p - 1)) + 1)
                    nc.scalar.activation((nsq if k else nsq_sum)[:], YF[:, k, cols(p)], ACT.Square
                                         ).then_inc(n_sq, 1)
                if a is not None:
                    n = a * KT + t
                    act.wait_ge(acc_ready, n + 1)
                    nc.scalar.activation(YF[:, t, cols(a)], acc[:, cols(n % NB)], ACT.Copy).then_inc(y_raw, 1)
                    wait_count(act, y_added, a * (KT - 1) + max(t - 2, 0))
                    if t == 0 and a > 0:
                        act.wait_ge(sum_ready, sums_order.index(("y", a - 1)) + 1)
                    nc.scalar.activation((sq[t % 2] if t else sq_sum)[:], acc[:, cols(n % NB)], ACT.Square
                                         ).then_inc(y_sq, 1)
                if t == 0 and p is not None:
                    deviation("y", p)
                if t == 4 and x is not None:
                    deviation("n", x)

        @block.vector
        def _(dve):
            def low_part(n):
                c, k = n // KT, n % KT
                dve.wait_ge(x_hi, n + 1)
                nc.vector.tensor_tensor(low(c, True)[:, k, :], low(c)[:, k, :], XH[c % 2][:, k, :].bitcast(F32),
                                        ALU.subtract).then_inc(x_lo, 1)

            dve.wait_ge(z_in, 16)
            nc.vector.reciprocal(z[:], z[:]).then_inc(z_rcp, 1)
            dve.wait_ge(z_hi, 1)
            nc.vector.tensor_tensor(zl[:], z[:], zh[:].bitcast(F32), ALU.subtract).then_inc(z_lo, 1)
            for period, t, g, a, p, x in stages():
                if g is not None:
                    n = g * KT + t
                    x_ = low(g)[:, t, :]
                    if t == 0 or n == KT // 2:
                        dve.wait_ge(o_in[(0 if t == 0 else 1) if g == 0 else g + 1], 16)
                    dve.wait_ge(r_ready, n + 1)
                    nc.vector.tensor_tensor(x_, x_, rb[:, cols(n % 2)], ALU.mult).then_inc(o_div, 1)
                    dve.wait_ge(o_div, n + 1)
                    dve.wait_ge(g_in[n % 2], 16 * (n // 2 + 1))
                    nc.vector.tensor_tensor(x_, x_, G[n % 2][:], ALU.mult).then_inc(o_gated, 1)
                    if t > 0:
                        low_part(n - 1)
                    if t == KT - 1:
                        low_part(n)
                if t == 1 and p is not None:
                    dve.wait_ge(sd_ready, sums_order.index(("y", p)) + 1)
                    nc.vector.reciprocal(rstd[:], rstd[:]).then_inc(rstd_ready, 1)
                    dve.wait_ge(rstd_ready, p + 1)
                if p is not None and t >= 2:
                    m = p * KT + t - 2
                    y = YF[:, t - 2, cols(p)]
                    nc.vector.tensor_tensor(y, y, rstd[:], ALU.mult).then_inc(y_scaled, 1)
                    dve.wait_ge(y_scaled, m + 1)
                    dve.wait_ge(res_in[m % 2], 16 * (m // 2 + 1))
                    nc.vector.scalar_tensor_tensor(out=y, in0=y, scalar=gpost[:, t - 2:t - 1], in1=R[m % 2][:],
                                                   op0=ALU.mult, op1=ALU.add).then_inc(y_ready, 1)
                if t == 5 and x is not None:
                    dve.wait_ge(sd_ready, sums_order.index(("n", x)) + 1)
                    nc.vector.reciprocal(rstd_next[:, cols(x)], rstd_next[:, cols(x)]).then_inc(next_ready, 1)
                if a is not None and t > 0:
                    dve.wait_ge(y_sq, a * KT + t + 1)
                    wait_count(dve, y_added, a * (KT - 1) + t - 1)
                    nc.vector.tensor_tensor(sq_sum[:], sq_sum[:], sq[t % 2][:], ALU.add).then_inc(y_added, 1)



def build_trunk(nc, A):
    ar = Arena(nc)

    def scratch(name, shape):
        return nc.dram_tensor(name, shape, F32, kind="Internal").ap()

    S = {"O": scratch("att_out", [32 * HD, T]),
         "Z": scratch("att_den", [32, T]),
         ("RZ", "hi"): scratch("att_rden_hi", [32, T]),
         ("RZ", "lo"): scratch("att_rden_lo", [32, T]),
         "X1": scratch("x_mid", [D, T]),
         "latent": scratch("latent", [4 * P, T]),
         "gate0": scratch("silu_gate0", [D, T]), "gate1": scratch("silu_gate1", [D, T])}
    for part in ("hi", "lo"):
        for name, shape in (("qA", [512, T]), ("kA", [512, T]), ("vA", [8, P, TT, HD]),
                            ("qB", [8 * 96, T]), ("kB", [512, T]), ("krB", [ROPE, T]), ("vB", [8, P, TT, HD]),
                            ("qC", [1024, T]), ("kC", [256, T]), ("vC", [4, P, TT, HD])):
            S[name, part] = scratch(f"{name}_{part}", shape)

    with ar.scope() as sc:
        ones = sc.sb("ones", [P, P])
        epst = sc.sb("epst", [P, 1])
        gpre = [sc.sb(f"gpre{l}", [P, KT]) for l in range(2)]
        gpost = [sc.sb(f"gpost{l}", [P, KT]) for l in range(2)]
        set_up(nc, ar, ones, epst, gpre, gpost, A)

        consts = (ones, epst, A)

        with ar.scope() as s1:
            XH = s1.sb("XH0", [P, KT, T], F32R)
            project(nc, ar, "p0", (XH, *s1.both("XL0", [P, KT, T])), s1.sb("rstd0", [P, T]), A["w_tiles0"], gpre[0],
                    [("split", 0, 4, {"hi": S["qA", "hi"], "lo": S["qA", "lo"], "scale": HD ** -0.5}),
                     ("split", 4, 4, {"hi": S["kA", "hi"], "lo": S["kA", "lo"]}),
                     ("raw", 8, 4, {"out": S["latent"]}),
                     ("gate", 12, 8, {"out": S["gate0"]})],
                    {"w": A["wv0"], "heads": 8, "hi": S["vA", "hi"], "lo": S["vA", "lo"]}, consts, src=A["xT"])
        latent_projections(nc, ar, S, A, ones, epst)

        def per_head(name, part, h, n):
            return S[name, part][ds(h * n, n), :]

        def values_of(name, part, h):
            return S[name, part][ds(h, 1), :, :, :].rearrange("a p i d -> (a p) i d")

        def load_v(name, h, B):
            return [(B["VH"][:, :, 0:HD], values_of(name, "hi", h)), (B["VL"][:, :, 0:HD], values_of(name, "lo", h))]

        attention(nc, ar, "a", A, 8, 2,
                  lambda h, i, j, B: [(B["Q1"][0:HD, :], per_head("qA", "hi", h, HD)),
                                      (B["Q1"][HD:P, :], per_head("qA", "hi", h, HD)),
                                      (B["K2"][0:HD, :], per_head("kA", "hi", h, HD)),
                                      (B["K2"][HD:P, :], per_head("kA", "lo", h, HD))],
                  lambda h, i, j, B: [(B["Q3"][0:HD, :], per_head("qA", "lo", h, HD)),
                                      (B["K3"][0:HD, :], per_head("kA", "hi", h, HD))] + load_v("vA", h, B),
                  4, 4, HD, 0, S, biased=True)
        attention(nc, ar, "b", A, 8, 2,
                  lambda h, i, j, B: [(B["Q1"][0:96, :], per_head("qB", "hi", h, 96)),
                                      (B["K3"][0:HD, :], per_head("kB", "hi", h, HD)),
                                      (B["K3"][HD:96, :], S["krB", "hi"])],
                  lambda h, i, j, B: [(B["K2"][0:HD, :], per_head("kB", "lo", h, HD)),
                                      (B["K2"][HD:96, :], S["krB", "lo"]),
                                      (B["Q3"][0:96, :], per_head("qB", "lo", h, 96))] + load_v("vB", h, B),
                  3, 5, 96, 8, S)

        ar.recycle()

        with ar.scope() as s1:
            Y = s1.both("Y0", [P, KT, T])
            rstd = s1.sb("rstd1", [P, T])
            output_projection(nc, ar, 0, S, A, Y, rstd, gpost[0], ones, epst, A["xT"], S["X1"])
            project(nc, ar, "p1", (s1.sb("XH1", [P, KT, T], F32R), *Y), rstd, A["w_tiles1"], gpre[1],
                    [("qk", 0, 8, {"hi": S["qC", "hi"], "lo": S["qC", "lo"], "cos": "cos_q", "sin": "sin_q"}),
                     ("qk", 8, 2, {"hi": S["kC", "hi"], "lo": S["kC", "lo"], "cos": "cos_k", "sin": "sin_k"}),
                     ("gate", 10, 8, {"out": S["gate1"]})],
                    {"w": A["wv1"], "heads": 4, "hi": S["vC", "hi"], "lo": S["vC", "lo"]}, consts,
                    tabs={"cos_q": ["cosC", None], "sin_q": ["sinC", None],
                          "cos_k": ["cosC", None], "sin_k": ["sinC", None]})
        attention(nc, ar, "c", A, 16, 4,
                  lambda h, i, j, B: [(B["Q1"][0:HD, :], per_head("qC", "hi", h, HD)),
                                      (B["Q1"][HD:P, :], per_head("qC", "hi", h, HD)),
                                      (B["K2"][0:HD, :], per_head("kC", "hi", i, HD)),
                                      (B["K2"][HD:P, :], per_head("kC", "lo", i, HD))],
                  lambda h, i, j, B: [(B["Q3"][0:HD, :], per_head("qC", "lo", h, HD)),
                                      (B["K3"][0:HD, :], per_head("kC", "hi", i, HD))] + load_v("vC", i, B),
                  4, 4, HD, 16, S)
        with ar.scope() as s1:
            output_projection(nc, ar, 1, S, A, s1.both("Y1", [P, KT, T]), None, gpost[1], ones, epst, S["X1"], A["yT"])


def set_up(nc, ar, ones, epst, gpre, gpost, A):
    g_in, c_set = ar.sem("g_in"), ar.sem("c_set")
    with nc.Block() as block:
        @block.sync
        def _(sp):
            for l in range(2):
                sp.dma_start(gpre[l][:], A["gpre"][l]).then_inc(g_in, 16)
                sp.dma_start(gpost[l][:], A["gpost"][l]).then_inc(g_in, 16)
            sp.wait_ge(g_in, 64)

        @block.vector
        def _(dve):
            nc.vector.memset(ones[:], 1.0).then_inc(c_set, 1)
            nc.vector.memset(epst[:], EPS).then_inc(c_set, 1)
            dve.wait_ge(c_set, 2)



def shape_constants():
    import numpy as np
    half = ROPE // 2
    freq = (np.float32(10000.0) ** (-np.arange(half, dtype=np.float32) / np.float32(half))).astype(np.float32)
    r = np.arange(P)
    sign = np.where(r % ROPE < half, -1.0, 1.0).astype(np.float32)[:, None]

    def tables(pos):
        ang = (pos * freq[r % half][:, None]).astype(np.float32)
        return np.cos(ang).astype(np.float32), (np.sin(ang) * sign).astype(np.float32)

    t = np.arange(SEQ, dtype=np.float32)[None, :]
    c = {}
    c["cosB"], c["sinB"] = tables(np.broadcast_to(t, (P, SEQ)))
    axial = np.where((r[:, None] // ROPE) % 2 == 0, np.floor(t / 64), t % 64).astype(np.float32)
    c["cosC"], c["sinC"] = tables(axial)
    c["headsel"] = (r[:, None] // HD == r[None, :] // HD).astype(np.float32)
    c["denominator_rows"] = (np.arange(D)[None, :] // HD == np.arange(32)[:, None] % 16).astype(np.float32)
    c["ident"] = np.eye(P, dtype=np.float32)
    c["negsel"] = np.ascontiguousarray(np.broadcast_to(-np.eye(AUG, dtype=np.float32)[:, :, None], (AUG, AUG, P)))
    off = np.abs(np.arange(BW)[None, :] - (BW - SEQ) - r[:, None])
    held = (off <= 64).astype(int) + ((off % 4 == 0) & (off <= 256)) + ((off % 16 == 0) & (off <= 1024))
    c["bias_dist"] = np.where(held > 0, -off.astype(np.float64), -1e30).astype(np.float32)
    c["bias_count"] = np.where(held > 0, np.log(np.maximum(held, 1).astype(np.float64)), 0.0).astype(np.float32)
    c["slopes"] = np.ascontiguousarray(np.broadcast_to(2.0 ** -np.arange(1, 9, dtype=np.float32), (P, 8)))
    return c


def kernel(x_prompt, x_sample, norm_pre, norm_post, w_in_ab, mla_q_norm, w_uq, mla_kv_norm, w_ukv,
           w_out_ab, w_in_c, c_q_norm, c_k_norm, w_out_c):
    import numpy as np
    import concourse.bacc as bacc
    from concourse.bass_utils import run_bass_kernel_spmd

    def feature_tiles(w):
        return w.reshape(KT, P, -1, P).transpose(2, 1, 0, 3).reshape(-1, P, D)

    def value_units(w):
        return w.reshape(KT // 2, 2, P, -1).transpose(0, 2, 1, 3).reshape(KT // 2, P, -1)

    def columns(g):
        return g.reshape(-1, P).T

    w0, w1 = np.asarray(w_in_ab)[0], np.asarray(w_in_c)[0]
    kr = w0[:, 1920:1952]
    cols0 = np.concatenate([w0[:, 0:1024], w0[:, 1536:1920], kr, kr, kr, kr, w0[:, 1952:2976]], axis=1)
    cols1 = np.concatenate([w1[:, 0:1280], w1[:, 1536:2560]], axis=1)
    wk = np.asarray(w_ukv)[0].reshape(P, 8, 2, HD)
    gq, gk = np.asarray(c_q_norm)[0], np.asarray(c_k_norm)[0]
    swap = np.arange(HD) // 32 * 32 + (np.arange(HD) + 16) % 32
    arrays = {
        "xT": np.concatenate([np.asarray(x_prompt)[0].T, np.asarray(x_sample)[0].T], axis=1),
        "w_tiles0": feature_tiles(cols0), "wv0": value_units(w0[:, 1024:1536]),
        "w_tiles1": feature_tiles(cols1), "wv1": value_units(w1[:, 1280:1536]),
        "w_out0": feature_tiles(np.asarray(w_out_ab)[0]), "w_out1": feature_tiles(np.asarray(w_out_c)[0]),
        "w_uq": np.asarray(w_uq)[0],
        "w_ukv": np.concatenate([wk[:, :, 0].reshape(P, 512), wk[:, :, 1].reshape(P, 512)], axis=1),
        "gpre": np.stack([columns(g) for g in np.asarray(norm_pre)]),
        "gpost": np.stack([columns(g) for g in np.asarray(norm_post)]),
        "g_lat": np.concatenate([columns(np.asarray(mla_q_norm)[0]), columns(np.asarray(mla_kv_norm)[0])], axis=1),
        "g_heads": np.stack([np.concatenate([g, g]) for g in (gq, gq[swap], gk, gk[swap])], axis=1),
    }
    arrays.update(shape_constants())
    arrays = {k: np.ascontiguousarray(v) for k, v in arrays.items()}
    nc = bacc.Bacc("TRN2", target_bir_lowering=False, num_devices=1)
    A = {k: nc.dram_tensor(f"in_{k}", v.shape, mybir.dt.from_np(v.dtype), kind="ExternalInput").ap()
         for k, v in arrays.items()}
    A["yT"] = nc.dram_tensor("yT", (D, T), F32, kind="ExternalOutput").ap()
    build_trunk(nc, A)
    r = run_bass_kernel_spmd(nc, [{f"in_{k}": v for k, v in arrays.items()}], core_ids=[0])
    y = r.results[0]["yT"]
    return (np.ascontiguousarray(y[:, 0:SEQ].T)[None], np.ascontiguousarray(y[:, SEQ:T].T)[None])
```

```python
from contextlib import ExitStack

import concourse.bass as bass
from concourse import mybir

F32 = mybir.dt.float32
F32R = mybir.dt.float32r
ALU = mybir.AluOpType
ACT = mybir.ActivationFunctionType
AX_X = mybir.AxisListType.X

P = 128
D = 1024
KT = D // P
SEQ, DEC = 1024, 512
T = SEQ + DEC
CH = 512
NC = T // CH
TT = T // P
EPS = 1e-6
HD = 64
ROPE = 32
BW = 1920
AUG = 8
SWAP16 = [(i + 16) % 32 for i in range(32)]


def ds(start, size):
    return bass.ds(start, size)


def wait_count(eng, sem, value):
    if isinstance(value, int) and value <= 0:
        return
    eng.wait_ge(sem, value)


def wait_apart(eng, sem, value, seen):
    eng.wait_ge(sem, value)
    eng.sem_inc(seen, 1)


def steps(eng, count, body):
    body(0, True, count == 1)
    if count > 2:
        with eng.Fori(1, count - 1) as i:
            body(i, False, False)
    if count > 1:
        body(count - 1, False, True)


class Arena:

    def __init__(self, nc):
        self.nc, self.sems = nc, []

    def sem(self, name):
        self.sems.append(self.nc.alloc_semaphore(name=name))
        return self.sems[-1]

    def recycle(self):
        self.nc.clear_and_free_semaphores(self.sems)
        self.nc.all_engine_barrier()
        self.sems = []

    def scope(self):
        return Scope(self.nc)


class Scope(ExitStack):
    def __init__(self, nc):
        super().__init__()
        self.nc = nc

    def sb(self, name, shape, dtype=F32):
        return self.enter_context(self.nc.sbuf_tensor(name, shape, dtype))

    def both(self, name, shape):
        offset = (self.nc.sbuf_base + 31) // 32 * 32
        plain = self.sb(name, shape)
        return plain, self.nc.alloc_sbuf_tensor_at(f"{name}_r", shape, F32R, offset=offset)

    def banks(self, name, count):
        return self.enter_context(self.nc.psum_tensor(name, [P, count * CH], F32))



def project(nc, ar, tag, x, rstd, tiles, gain, groups, values, consts, src=None, tabs=None):
    XH, XF, XL = x
    ones, epst, arrays = consts
    x_in = [ar.sem(f"{tag}_x_in{c}") for c in range(NC)]
    x_sq, x_sum, x_sd, x_rstd, x_h, x_hi = (ar.sem(f"{tag}_x_{n}") for n in ("sq", "sum", "sd", "rstd", "h", "hi"))
    x_lo_v, x_lo_p = ar.sem(f"{tag}_x_lo_v"), ar.sem(f"{tag}_x_lo_p")
    NT = sum(g[2] for g in groups)
    raw_in = [ar.sem(f"{tag}_w_in{i}") for i in range(2)]
    w_scaled, w_hi, w_ready = ar.sem(f"{tag}_w_scaled"), ar.sem(f"{tag}_w_hi"), ar.sem(f"{tag}_w_ready")
    acc_ready = ar.sem(f"{tag}_acc_ready")
    acc_read = {g[1]: ar.sem(f"{tag}_acc_read{g[1]}") for g in groups}
    acc_read[NT] = ar.sem(f"{tag}_acc_read_v")
    v_used = ar.sem(f"{tag}_v_used")
    hi_ready = ar.sem(f"{tag}_hi_ready")
    stored = [ar.sem(f"{tag}_stored{i}") for i in range(3)]
    g_exp, g_one, g_rcp = ar.sem(f"{tag}_g_exp"), ar.sem(f"{tag}_g_one"), ar.sem(f"{tag}_g_rcp")
    has_qk = any(g[0] == "qk" for g in groups)
    if has_qk:
        q_raw, q_sum, q_sd, q_rstd = (ar.sem(f"{tag}_q_{x}") for x in ("raw", "sum", "sd", "rstd"))
        q_sw, q_cos, q_sin, q_rot, q_done, q_lo, q_seen = (
            ar.sem(f"{tag}_q_{x}") for x in ("sw", "cos", "sin", "rot", "done", "lo", "seen"))
    hi0, qk0, nh, nq = {}, {}, 0, 0
    for kind, t0, nt, _ in groups:
        hi0[t0], qk0[t0] = nh, nq
        nh += 3 * nt if kind in ("split", "qk") else 0
        nq += 3 * nt if kind == "qk" else 0
    vhi0 = nh
    K = sum(g[2] for g in groups if g[0] == "keep")
    VU = KT

    with ar.scope() as sc:
        raw = [sc.sb(f"{tag}_raw{i}", [P, D]) for i in range(2)]
        wg = sc.sb(f"{tag}_wg", [P, D])
        wh = [sc.sb(f"{tag}_wh{i}", [P, D], F32R) for i in range(2)]
        wl = [sc.sb(f"{tag}_wl{i}", [P, D], F32R) for i in range(2)]
        sh, sl, ta, tb = ([sc.sb(f"{tag}_{n}{i}", [P, CH]) for i in range(3)] for n in ("sh", "sl", "ta", "tb"))
        if src is not None:
            xsq = [sc.sb(f"{tag}_xsq{i}", [P, CH]) for i in range(2)]
        if tabs:
            t_in, t_done = ar.sem(f"{tag}_t_in"), ar.sem(f"{tag}_t_done")
            sel = sc.sb(f"{tag}_headsel", [P, P])
            hg = sc.sb(f"{tag}_head_gain", [P, 4])
            for n in tabs:
                tabs[n][1] = sc.sb(f"{tag}_rope_{n}", [P, SEQ])
        if has_qk:
            tsq = [sc.sb(f"{tag}_tsq{i}", [P, CH]) for i in range(2)]
            tsd = [sc.sb(f"{tag}_tsd{i}", [P, CH]) for i in range(2)]
        acc = sc.banks(f"{tag}_acc", 6)
        ssb = sc.banks(f"{tag}_ssb", 2)
        bank = [acc[:, i * CH:(i + 1) * CH] for i in range(6)]
        sums = [ssb[:, i * CH:(i + 1) * CH] for i in range(2)]
        block = sc.enter_context(nc.Block())

        def cols(c):
            return slice(c * CH, (c + 1) * CH)

        def x_split(eng, done, engine):
            def tile(c, k):
                eng.wait_ge(x_hi, c * KT + k + 1)
                engine.tensor_tensor(XL[:, k, cols(c)], XF[:, k, cols(c)], XH[:, k, cols(c)].bitcast(F32),
                                     ALU.subtract).then_inc(done, 1)
            return tile

        @block.sync
        def _(sp):
            def load(t, b):
                wait_count(sp, w_ready, t - 1)
                sp.dma_start(raw[b][:], tiles[ds(t, 1), :, :].rearrange("a p n -> p (a n)")
                             ).then_inc(raw_in[b], 16)

            load(0, 0)
            if src is not None:
                for c in range(NC):
                    sp.dma_start(XF[:, :, cols(c)], src.rearrange("(k p) t -> p k t", p=P)[:, :, cols(c)]
                                 ).then_inc(x_in[c], 16)
            load(1, 1)
            if tabs:
                sp.dma_start(hg[:], arrays["g_heads"]).then_inc(t_in, 16)
                sp.dma_start(sel[:], arrays["headsel"]).then_inc(t_in, 16)
                for name, (source, table) in tabs.items():
                    sp.dma_start(table[:], arrays[source]).then_inc(t_in, 16)
            for kind, t0, nt, opt in groups:
                final = t0 + nt == NT

                def pair(i, first, last):
                    for b in range(2):
                        tl = i * 2 + b
                        t = tl + t0
                        if not (final and last):
                            load(t + 2, b)
                        for c in range(NC if kind != "keep" else 0):
                            rows = ds(tl * P, P)
                            if kind == "qk":
                                sp.wait_ge(q_lo, tl * 3 + (qk0[t0] + c + 1))
                            else:
                                sp.wait_ge(acc_read[t0], tl * 3 + (c + 1))
                            if kind in ("split", "qk"):
                                sp.dma_start(opt["hi"][rows, cols(c)], sh[c][:]).then_inc(stored[c], 16)
                                sp.dma_start(opt["lo"][rows, cols(c)], sl[c][:]).then_inc(stored[c], 16)
                            else:
                                sp.dma_start(opt["out"][rows, cols(c)], sh[c][:]).then_inc(stored[c], 32)
                steps(sp, nt // 2, pair)
            W = values["w"].shape[2]
            nhd = values["heads"]

            def store_half(half):
                for i in range(6 * half, 6 * half + 6):
                    sp.wait_ge(acc_read[NT], i + 1)
                    for part, stage in (("hi", sh), ("lo", sl)):
                        sp.dma_start(values[part].rearrange("h p i d -> p h i d")[:, :, i, :],
                                     stage[i % 3][:, 0:nhd * HD].rearrange("p (h d) -> p h d", d=HD)
                                     ).then_inc(stored[i % 3], 16)

            for u in range(VU):
                b = (NT + u) % 2
                sp.wait_ge(w_ready, NT + u - 1)
                sp.dma_start(raw[b][:, 0:W], values["w"][u % (VU // 2)]).then_inc(raw_in[b], 16)
                if u == VU // 2 + 1:
                    store_half(0)
            store_half(1)
            for c in range(3):
                sp.wait_ge(stored[c], 32 * (NT - K + TT // 3))

        @block.gpsimd
        def _(pool):
            def split(t, b, w, g, counts, free_sem=acc_ready):
                def v(x):
                    return x[:, 0:w].rearrange("p (k n) -> p k n", k=g.shape[1])
                gb = g.unsqueeze(2).to_broadcast([P, g.shape[1], w // g.shape[1]])
                pool.wait_ge(raw_in[b], counts[1])
                wait_count(pool, free_sem, counts[0])
                nc.gpsimd.tensor_tensor(v(wh[b]), v(raw[b]), gb, ALU.mult).then_inc(w_hi, 1)
                wait_count(pool, w_ready, t)
                nc.gpsimd.tensor_tensor(v(wg), v(raw[b]), gb, ALU.mult).then_inc(w_scaled, 1)
                pool.wait_ge(w_hi, t + 1)
                pool.wait_ge(w_scaled, t + 1)
                nc.gpsimd.tensor_tensor(wl[b][:, 0:w], wg[:, 0:w], wh[b][:, 0:w].bitcast(F32), ALU.subtract
                                        ).then_inc(w_ready, 1)

            split(0, 0, D, gain[:, 0:KT], (0, 16))
            lo = x_split(pool, x_lo_p, nc.gpsimd)
            for c in range(NC):
                for k in range(1, KT, 2):
                    lo(c, k)
            for kind, t0, nt, opt in groups:
                final = t0 + nt == NT

                def pair(i, first, last):
                    for b in range(2):
                        tl = i * 2 + b
                        if not (final and last and b == 1):
                            split(tl + (t0 + 1), 1 - b, D, gain[:, 0:KT],
                                  (tl * 3 + 3 * t0, i * 16 + (16 * (t0 // 2 + b) + 16)))
                        if kind == "qk" and t0 == 0 and first and b == 0:
                            pool.wait_ge(t_done, 4)
                        for c in range(NC if kind == "qk" else 0):
                            m = tl * 3 + (qk0[t0] + c)
                            pc = slice((c * CH) % SEQ, (c * CH) % SEQ + CH)
                            pool.wait_ge(q_sw, m + 1)
                            nc.gpsimd.tensor_tensor(ta[c][:], ta[c][:], tabs[opt["cos"]][1][:, pc], ALU.mult
                                                    ).then_inc(q_cos, 1)
                            nc.gpsimd.tensor_tensor(tb[c][:], tb[c][:], tabs[opt["sin"]][1][:, pc], ALU.mult
                                                    ).then_inc(q_sin, 1)
                steps(pool, nt // 2, pair)
            for u in range(VU):
                W = values["w"].shape[2]
                if u < 2:
                    free = (acc_ready, 3 * (NT + u) - 3)
                elif (u - 2) % (VU // 2) == VU // 2 - 1:
                    free = (acc_ready, 3 * NT + 6 * ((u - 2) // (VU // 2) + 1))
                else:
                    free = (v_used, u - 1 - (u - 2) // (VU // 2))
                ku = 2 * (u % (VU // 2))
                split(NT + u, (NT + u) % 2, W, gain[:, ku:ku + 2], (free[1], 16 * ((NT + u) // 2) + 16), free[0])

        @block.tensor
        def _(pe):
            def bank_free(t0, n):
                if isinstance(n, int) and n < 6:
                    before = [g for g in groups if g[1] < t0]
                    if before:
                        pe.wait_ge(acc_read[before[-1][1]], 3 * before[-1][2] + n - 5)
                else:
                    pe.wait_ge(acc_read[t0], n - 5)

            def square_sum(c):
                wait_count(pe, x_sd, c)
                for k in range(KT):
                    pe.wait_ge(x_sq, c * KT + k + 1)
                    nc.tensor.matmul(sums[0], ones[:], xsq[k % 2][:], start=(k == 0), stop=(k == KT - 1)
                                     ).then_inc(x_sum, 1)

            def chunk_split(c):
                if src is not None:
                    for cc in range(2) if c == 0 else range(c + 1, min(c + 2, NC)):
                        square_sum(cc)
                pe.wait_ge(x_lo_v, (c + 1) * (KT // 2))
                pe.wait_ge(x_lo_p, (c + 1) * (KT // 2))

            def head_sums(m, slot, t0, n_read):
                if isinstance(m, int) and m == 0:
                    pe.wait_ge(t_done, 4)
                pe.wait_ge(acc_read[t0], n_read)
                wait_count(pe, q_sd, m - 1)
                nc.tensor.matmul(sums[slot], sel[:], tsq[slot][:], start=True, stop=True).then_inc(q_sum, 1)

            for kind, t0, nt, opt in groups:
                def pair(i, first, last):
                    for b in range(2):
                        tl = i * 2 + b
                        t = tl + t0
                        pe.wait_ge(w_ready, t + 1)
                        for c in range(NC):
                            if t0 == 0 and first and b == 0:
                                chunk_split(c)
                            bank_free(t0, tl * 3 + c)
                            out = bank[3 * b + c]
                            for k in range(KT):
                                ks = slice(k * P, (k + 1) * P)
                                for j, (w, x) in enumerate(((wh[b], XH), (wh[b], XL), (wl[b], XH))):
                                    last_mm = nc.tensor.matmul(out, w[:, ks], x[:, k, cols(c)],
                                                               start=(k == 0 and j == 0),
                                                               stop=(k == KT - 1 and j == 2))
                            last_mm.then_inc(acc_ready, 1)
                            if kind == "qk" and not (first and b == 0 and c == 0):
                                head_sums(tl * 3 + (qk0[t0] + c - 1), (3 * b + c - 1) % 2, t0, tl * 3 + c)
                    if kind == "qk" and last:
                        head_sums(qk0[t0] + 3 * nt - 1, 1, t0, 3 * nt)
                assert t0 % 2 == 0 and nt % 2 == 0
                steps(pe, nt // 2, pair)
            W = values["w"].shape[2] // 2
            for u in range(VU):
                half, ku = u // (VU // 2), 2 * (u % (VU // 2))
                b = (NT + u) % 2
                pe.wait_ge(w_ready, NT + u + 1)
                for i in range(6):
                    if ku == 0:
                        bank_free(NT, 6 * half + i)
                    tok = slice((6 * half + i) * P, (6 * half + i + 1) * P)
                    for kk in range(2):
                        ws = slice(kk * W, (kk + 1) * W)
                        for j, (x, w) in enumerate(((XH, wh[b]), (XL, wh[b]), (XH, wl[b]))):
                            last_mm = nc.tensor.matmul(bank[i][:, 0:W], x[:, ku + kk, tok], w[:, ws],
                                                       start=(ku + kk + j == 0),
                                                       stop=(ku + kk == KT - 1 and j == 2))
                    if ku == KT - 2:
                        last_mm.then_inc(acc_ready, 1)
                if ku != KT - 2:
                    last_mm.then_inc(v_used, 1)

        @block.scalar
        def _(act):
            def square(c, k):
                n = c * KT + k
                if k == 0:
                    act.wait_ge(x_in[c], 16)
                wait_count(act, x_sum, n - 1)
                nc.scalar.activation(xsq[k % 2][:], XF[:, k, cols(c)], ACT.Square).then_inc(x_sq, 1)

            def deviation(c):
                act.wait_ge(x_sum, (c + 1) * KT)
                nc.scalar.activation(rstd[:, cols(c)], sums[0], ACT.Sqrt, bias=epst[:], scale=1.0 / D
                                     ).then_inc(x_sd, 1)

            if src is not None:
                for k in range(KT):
                    square(0, k)
                deviation(0)
            for c in range(NC):
                for k in range(KT):
                    act.wait_ge(x_h, c * KT + k + 1)
                    nc.scalar.activation(XH[:, k, cols(c)], XF[:, k, cols(c)], ACT.Copy).then_inc(x_hi, 1)
                    if src is not None and c + 1 < NC:
                        square(c + 1, k)
                if src is not None and c + 1 < NC:
                    deviation(c + 1)

            for kind, t0, nt, opt in groups:
                scale = opt.get("scale", 1.0)
                if kind == "gate" and nq:
                    act.wait_ge(q_lo, nq)

                def sd(m, slot):
                    act.wait_ge(q_sum, m + 1)
                    wait_count(act, q_done, m - 1)
                    nc.scalar.activation(tsd[slot][:], sums[slot], ACT.Sqrt, bias=epst[:], scale=1.0 / HD
                                         ).then_inc(q_sd, 1)

                def hi(m, c, uses, nhi):
                    act.wait_ge(q_done, m + 1)
                    wait_count(act, stored[c], uses)
                    nc.scalar.activation(sh[c][:].bitcast(F32R), ta[c][:], ACT.Copy).then_inc(hi_ready, 1)

                def pair(i, first, last):
                    for b in range(2):
                        tl = i * 2 + b
                        t = tl + t0
                        for c in range(NC):
                            products = bank[3 * b + c]
                            act.wait_ge(acc_ready, t * 3 + (c + 1))
                            m = tl * 3 + (qk0[t0] + c)
                            if kind == "keep":
                                nc.scalar.activation(opt["out"][:, ds(tl, 1), cols(c)].rearrange("p a n -> p (a n)"),
                                                     products, ACT.Copy).then_inc(acc_read[t0], 1)
                            elif kind == "split":
                                wait_count(act, stored[c], (t - K) * 32)
                                nc.scalar.activation(sh[c][:].bitcast(F32R), products, ACT.Copy, scale=scale
                                                     ).then_inc(hi_ready, 1)
                            elif kind == "gate":
                                wait_count(act, g_rcp, tl * 3 + (c - 2))
                                nc.scalar.activation(ta[c][:], products, ACT.Exp, scale=-1.0).then_inc(g_exp, 1)
                            elif kind == "qk":
                                wait_count(act, q_lo, m - 2)
                                nc.scalar.activation(ta[c][:], products, ACT.Copy).then_inc(q_raw, 1)
                                wait_count(act, q_sum, m - 1)
                                nc.scalar.activation(tsq[(3 * b + c) % 2][:], products, ACT.Square
                                                     ).then_inc(acc_read[t0], 1)
                                lag = 3 * b + c
                                if not (first and lag < 1):
                                    sd(m - 1, (lag - 1) % 2)
                                if not (first and lag < 2):
                                    hi(m - 2, (c - 2) % 3, (t if c >= 2 else t - 1) * 32, m - 2)
                    if kind == "qk" and last:
                        mm = qk0[t0] + 3 * nt
                        sd(mm - 1, 1)
                        hi(mm - 2, 1, (t0 + nt - 1) * 32, mm - 2)
                        hi(mm - 1, 2, (t0 + nt - 1) * 32, mm - 1)
                steps(act, nt // 2, pair)
            for i in range(TT):
                W = values["w"].shape[2] // 2
                act.wait_ge(acc_ready, 3 * NT + i + 1)
                act.wait_ge(stored[i % 3], 32 * (NT - K + i // 3))
                nc.scalar.activation(sh[i % 3][:, 0:W].bitcast(F32R), bank[i % 6][:, 0:W], ACT.Copy
                                     ).then_inc(hi_ready, 1)

        @block.vector
        def _(dve):
            lo_tile = x_split(dve, x_lo_v, nc.vector)
            for c in range(NC):
                if src is not None:
                    dve.wait_ge(x_in[c], 16)
                    dve.wait_ge(x_sd, c + 1)
                    nc.vector.reciprocal(rstd[:, cols(c)], rstd[:, cols(c)]).then_inc(x_rstd, 1)
                    dve.wait_ge(x_rstd, c + 1)
                for k in range(KT):
                    nc.vector.tensor_tensor(XF[:, k, cols(c)], XF[:, k, cols(c)], rstd[:, cols(c)], ALU.mult
                                            ).then_inc(x_h, 1)
                    if k % 2 == 1:
                        lo_tile(c, k - 1)
            if tabs:
                dve.wait_ge(t_in, 16 * (len(tabs) + 2))
                for n, (name, (_, table)) in enumerate(tabs.items()):
                    nc.vector.tensor_scalar(table[:], table[:], hg[:, n:n + 1], HD ** -0.5 if n < 2 else 1.0,
                                            ALU.mult, ALU.mult).then_inc(t_done, 1)

            for kind, t0, nt, opt in groups:
                scale = opt.get("scale", 1.0)

                def norm_rope(m, c, slot):
                    dve.wait_ge(q_sd, m + 1)
                    nc.vector.reciprocal(tsd[slot][:], tsd[slot][:]).then_inc(q_rstd, 1)
                    dve.wait_ge(q_sin, m + 1)
                    dve.wait_ge(q_cos, m + 1)
                    nc.vector.tensor_tensor(ta[c][:], ta[c][:], tb[c][:], ALU.add).then_inc(q_rot, 1)
                    dve.wait_ge(q_rot, m + 1)
                    dve.wait_ge(q_rstd, m + 1)
                    nc.vector.tensor_tensor(ta[c][:], ta[c][:], tsd[slot][:], ALU.mult).then_inc(q_done, 1)

                def lo(m, c):
                    dve.wait_ge(hi_ready, hi0[t0] - qk0[t0] + m + 1)
                    dve.wait_ge(q_done, m + 1)
                    nc.vector.tensor_tensor(sl[c][:].bitcast(F32R), ta[c][:], sh[c][:], ALU.subtract
                                            ).then_inc(q_lo, 1)

                def pair(i, first, last):
                    for b in range(2):
                        tl = i * 2 + b
                        t = tl + t0
                        for c in range(NC):
                            products = bank[3 * b + c]
                            m = tl * 3 + (qk0[t0] + c)
                            if kind == "split":
                                dve.wait_ge(hi_ready, tl * 3 + (hi0[t0] + c + 1))
                                nc.vector.scalar_tensor_tensor(out=sl[c][:].bitcast(F32R), in0=products, scalar=scale,
                                                               in1=sh[c][:], op0=ALU.mult, op1=ALU.subtract
                                                               ).then_inc(acc_read[t0], 1)
                            elif kind == "gate":
                                g = tl * 3 + (c + 1)
                                dve.wait_ge(g_exp, g)
                                nc.vector.tensor_scalar(ta[c][:], ta[c][:], 1.0, None, ALU.add).then_inc(g_one, 1)
                                dve.wait_ge(g_one, g)
                                nc.vector.reciprocal(tb[c][:], ta[c][:]).then_inc(g_rcp, 1)
                                dve.wait_ge(g_rcp, g)
                                wait_count(dve, stored[c], (t - K) * 32)
                                nc.vector.tensor_tensor(sh[c][:], products, tb[c][:], ALU.mult).then_inc(acc_read[t0], 1)
                            elif kind == "qk":
                                lag = 3 * b + c
                                wait_apart(dve, q_raw, m + 1, q_seen)
                                nc.vector.stream_shuffle(tb[c][:], ta[c][:], SWAP16).then_inc(q_sw, 1)
                                if not (first and lag < 2):
                                    lo(m - 2, (c - 2) % 3)
                                if not (first and lag < 1):
                                    norm_rope(m - 1, (c - 1) % 3, (lag - 1) % 2)
                    if kind == "qk" and last:
                        mm = qk0[t0] + 3 * nt
                        norm_rope(mm - 1, 2, 1)
                        lo(mm - 2, 1)
                        lo(mm - 1, 2)
                if kind in ("split", "gate", "qk"):
                    steps(dve, nt // 2, pair)
            for i in range(TT):
                W = values["w"].shape[2] // 2
                dve.wait_ge(hi_ready, vhi0 + i + 1)
                nc.vector.tensor_tensor(sl[i % 3][:, 0:W].bitcast(F32R), bank[i % 6][:, 0:W],
                                        sh[i % 3][:, 0:W], ALU.subtract).then_inc(acc_read[NT], 1)


def latent_projections(nc, ar, S, A, latent, ones, epst):
    scale = float(HD + ROPE) ** -0.5
    chunk_units = [[("r", 0, c), ("q", 0, c), ("R", 0, c), ("q", 1, c), ("R", 1, c), ("q", 2, c), ("q", 3, c)]
                   + [("k", j, c) for j in range(4)] + [("v", 4 * c + j, c) for j in range(4)] for c in range(NC)]
    units = sum(chunk_units, [])
    n_units = len(units)
    products = [u for u in range(n_units) if units[u][0] != "r"]
    ropes = [u for u in range(n_units) if units[u][0] in "rR"]
    finish_order, LAG = [], 4
    for u in range(n_units):
        if u not in ropes:
            finish_order.append(u)
        if u - LAG in ropes:
            finish_order.append(u - LAG)
    place = {u: i for i, u in enumerate(finish_order)}
    NST = 8

    w_in, tab_in = ar.sem("l_w_in"), ar.sem("l_tab_in")
    sq_ready, sum_ready, sd_ready, rstd_ready = (ar.sem(f"l_{x}") for x in ("sq", "sum", "sd", "rstd"))
    n_ready, n_hi, n_lo = ar.sem("l_n"), ar.sem("l_n_hi"), ar.sem("l_n_lo")
    w_mul, w_lo = ar.sem("l_w_mul"), ar.sem("l_w_lo")
    mm_done, u_raw, u_sw, u_cos, u_sin, u_rot, u_hi, u_lo = (
        ar.sem(f"l_u_{x}") for x in ("mm", "raw", "sw", "cos", "sin", "rot", "hi", "lo"))
    stored = [ar.sem(f"l_stored{i}") for i in range(NST)]
    LF, LR = latent
    with ar.scope() as sc:
        LH = sc.sb("l_high", [P, 3, T], F32R)
        wr = sc.sb("l_wr", [P, 2560])
        wh = sc.sb("l_wh", [P, 2560], F32R)
        wl = sc.sb("l_wl", [P, 2560], F32R)
        g = sc.sb("l_g", [P, 3])
        cos, sin = sc.sb("l_cos", [P, SEQ]), sc.sb("l_sin", [P, SEQ])
        sq = [sc.sb(f"l_sq{i}", [P, CH]) for i in range(2)]
        sd = [sc.sb(f"l_sd{c}", [P, 2, CH]) for c in range(NC)]
        ta = [sc.sb(f"l_ta{i}", [P, CH]) for i in range(3)]
        tb = [sc.sb(f"l_tb{i}", [P, CH]) for i in range(3)]
        sh = [sc.sb(f"l_sh{i}", [P, CH]) for i in range(NST)]
        sl = [sc.sb(f"l_sl{i}", [P, CH]) for i in range(NST)]
        acc = sc.banks("l_acc", 6)
        ssb = sc.banks("l_ssb", 2)
        bank = [acc[:, i * CH:(i + 1) * CH] for i in range(6)]
        sums = [ssb[:, i * CH:(i + 1) * CH] for i in range(2)]
        block = sc.enter_context(nc.Block())

        def cols(c):
            return slice(c * CH, (c + 1) * CH)

        def rows(u):
            return slice(0, ROPE if units[u][0] == "r" else P)

        def bank_of(u):
            return bank[products.index(u) % 6]

        parts = ((0, 2), (2, 1))

        @block.sync
        def _(sp):
            sp.dma_start(wr[:, 0:1536].rearrange("p (k n) -> p k n", k=2),
                         A["w_uq"].rearrange("(k p) n -> p k n", p=P)).then_inc(w_in, 16)
            sp.dma_start(wr[:, 1536:2560], A["w_ukv"]).then_inc(w_in, 16)
            sp.dma_start(g[:], A["g_lat"]).then_inc(w_in, 16)
            sp.dma_start(cos[:], A["cosB"]).then_inc(tab_in, 16)
            sp.dma_start(sin[:], A["sinB"]).then_inc(tab_in, 16)
            for i, u in enumerate(finish_order):
                kind, j, c = units[u]
                sp.wait_ge(u_lo, i + 1)
                s = i % NST
                for part, st in (("hi", sh), ("lo", sl)):
                    src = st[s][rows(u), :]
                    if kind == "v":
                        dst = S["vB", part].rearrange("h p i d -> p h i d")[:, :, j, :]
                        src = src.rearrange("p (h d) -> p h d", d=HD)
                    else:
                        n = ROPE if kind == "r" else P
                        name = {"q": "qB", "R": "qrB", "k": "kB", "r": "krB"}[kind]
                        dst = S[name, part][j * n:(j + 1) * n, cols(c)]
                    sp.dma_start(dst, src).then_inc(stored[s], 16)
            for s in range(NST):
                sp.wait_ge(stored[s], 32 * len(range(s, n_units, NST)))

        @block.gpsimd
        def _(pool):
            def weights(c0, c1, gb, shape, done):
                def v(x):
                    return x[:, c0:c1].rearrange("p (k n) -> p k n", k=shape)
                for i, out in enumerate((wh, wr)):
                    nc.gpsimd.tensor_tensor(v(out), v(wr), gb, ALU.mult).then_inc(w_mul, 1)
                pool.wait_ge(w_mul, 2 * done)
                nc.gpsimd.tensor_tensor(wl[:, c0:c1], wr[:, c0:c1], wh[:, c0:c1].bitcast(F32), ALU.subtract
                                        ).then_inc(w_lo, 1)

            def low_parts(c):
                for k in range(3):
                    pool.wait_ge(n_hi, 3 * c + k + 1)
                    nc.gpsimd.tensor_tensor(LR[:, k, cols(c)], LF[:, k, cols(c)], LH[:, k, cols(c)].bitcast(F32),
                                            ALU.subtract).then_inc(n_lo, 1)
                pool.wait_ge(n_lo, 3 * c + 3)

            def rope(c):
                for u in ropes:
                    if units[u][2] != c:
                        continue
                    i, r = ropes.index(u), rows(u)
                    s, pc = i % 3, slice((c * CH) % SEQ, (c * CH) % SEQ + CH)
                    pool.wait_ge(u_sw, i + 1)
                    wait_count(pool, u_sin, i)
                    nc.gpsimd.tensor_tensor(ta[s][r, :], ta[s][r, :], cos[r, pc], ALU.mult).then_inc(u_cos, 1)
                    nc.gpsimd.tensor_tensor(tb[s][r, :], tb[s][r, :], sin[r, pc], ALU.mult).then_inc(u_sin, 1)
                pool.wait_ge(u_sin, 3 * c + 3)

            pool.wait_ge(w_in, 48)
            weights(0, 1536, g[:, 0:2].unsqueeze(2).to_broadcast([P, 2, 768]), 2, 1)
            low_parts(0)
            weights(1536, 2560, g[:, 2:3].unsqueeze(2).to_broadcast([P, 1, 1024]), 1, 2)
            pool.wait_ge(w_lo, 2)
            low_parts(1)
            pool.wait_ge(tab_in, 32)
            rope(0)
            low_parts(2)
            rope(1)
            rope(2)

        @block.tensor
        def _(pe):
            def statistics(c):
                n = 3 * c
                for q, (k0, nk) in enumerate(parts):
                    wait_count(pe, sd_ready, 2 * c + q - 1)
                    for k in range(nk):
                        pe.wait_ge(sq_ready, n + 1)
                        nc.tensor.matmul(sums[q], ones[:], sq[n % 2][:], start=(k == 0), stop=(k == nk - 1)
                                         ).then_inc(sum_ready, 1)
                        n += 1

            def unit(u):
                kind, j, c = units[u]
                w = products.index(u)
                if w >= 6:
                    before = products[w - 6]
                    if before in ropes:
                        pe.wait_ge(u_raw, ropes.index(before) + 1)
                    else:
                        pe.wait_ge(u_lo, place[before] + 1)
                out = bank_of(u)
                if kind in "qR":
                    for k in range(2):
                        o = k * 768 + (512 if kind == "R" else 0) + j * P
                        for i, (a, x) in enumerate(((wh, LH), (wh, LR), (wl, LH))):
                            mm = nc.tensor.matmul(out, a[:, o:o + P], x[:, k, cols(c)],
                                                  start=(k == 0 and i == 0), stop=(k == 1 and i == 2))
                elif kind == "k":
                    ws = slice(1536 + j * P, 1536 + (j + 1) * P)
                    for i, (a, x) in enumerate(((wh, LH), (wh, LR), (wl, LH))):
                        mm = nc.tensor.matmul(out, a[:, ws], x[:, 2, cols(c)], start=(i == 0), stop=(i == 2))
                else:
                    tok = slice(j * P, (j + 1) * P)
                    for i, (x, a) in enumerate(((LH, wh), (LR, wh), (LH, wl))):
                        mm = nc.tensor.matmul(out, x[:, 2, tok], a[:, 2048:2560], start=(i == 0), stop=(i == 2))
                mm.then_inc(mm_done, 1)

            def chunk(c):
                if c == 0:
                    pe.wait_ge(w_lo, 1)
                pe.wait_ge(n_lo, 3 * c + 3)
                for u in range(n_units):
                    if units[u][2] == c and units[u][0] != "r":
                        if units[u] == ("k", 0, 0):
                            pe.wait_ge(w_lo, 2)
                        unit(u)

            for c in range(NC):
                statistics(c)
            chunk(0)
            chunk(1)
            chunk(2)

        @block.scalar
        def _(act):
            def statistics(c):
                for k in range(3):
                    n = 3 * c + k
                    wait_count(act, sum_ready, n - 1)
                    nc.scalar.activation(sq[n % 2][:], LF[:, k, cols(c)], ACT.Square).then_inc(sq_ready, 1)
                for q, (k0, nk) in enumerate(parts):
                    act.wait_ge(sum_ready, 3 * c + k0 + nk)
                    nc.scalar.activation(sd[c][:, q, :], sums[q], ACT.Sqrt, bias=epst[:], scale=1.0 / (nk * P)
                                         ).then_inc(sd_ready, 1)

            def high_parts(c):
                for k in range(3):
                    act.wait_ge(n_ready, 3 * c + k + 1)
                    nc.scalar.activation(LH[:, k, cols(c)], LF[:, k, cols(c)], ACT.Copy).then_inc(n_hi, 1)

            def finish(u):
                i = place[u]
                wait_count(act, stored[i % NST], 32 * (i // NST))
                if u in ropes:
                    act.wait_ge(u_rot, ropes.index(u) + 1)
                    src = ta[ropes.index(u) % 3][rows(u), :]
                else:
                    act.wait_ge(mm_done, products.index(u) + 1)
                    src = bank_of(u)
                nc.scalar.activation(sh[i % NST][rows(u), :].bitcast(F32R), src, ACT.Copy,
                                     scale=scale if units[u][0] == "q" else 1.0).then_inc(u_hi, 1)

            def chunk(c):
                for u in range(n_units):
                    if units[u][2] == c:
                        if u in ropes:
                            i = ropes.index(u)
                            if i >= 3:
                                act.wait_ge(u_lo, place[ropes[i - 3]] + 1)
                            if units[u][0] == "r":
                                nc.scalar.activation(ta[i % 3][0:ROPE, :], LF[0:ROPE, 3, cols(c)], ACT.Copy
                                                     ).then_inc(u_raw, 1)
                            else:
                                act.wait_ge(mm_done, products.index(u) + 1)
                                nc.scalar.activation(ta[i % 3][:], bank_of(u), ACT.Copy, scale=scale
                                                     ).then_inc(u_raw, 1)
                        else:
                            finish(u)
                        if u - LAG in ropes:
                            finish(u - LAG)

            for c in range(NC):
                statistics(c)
            high_parts(0)
            high_parts(1)
            chunk(0)
            high_parts(2)
            chunk(1)
            chunk(2)

        @block.vector
        def _(dve):
            def normalise(c):
                dve.wait_ge(sd_ready, 2 * c + 2)
                s = sd[c]
                nc.vector.reciprocal(s[:, 0, :], s[:, 0, :]).then_inc(rstd_ready, 1)
                nc.vector.reciprocal(s[:, 1, :], s[:, 1, :]).then_inc(rstd_ready, 1)
                dve.wait_ge(rstd_ready, 2 * c + 2)
                for k in range(3):
                    nc.vector.tensor_tensor(LF[:, k, cols(c)], LF[:, k, cols(c)], s[:, k // 2, :], ALU.mult
                                            ).then_inc(n_ready, 1)

            def rotate(u):
                i = ropes.index(u)
                r, s = rows(u), i % 3
                dve.wait_ge(u_cos, i + 1)
                dve.wait_ge(u_sin, i + 1)
                nc.vector.tensor_tensor(ta[s][r, :], ta[s][r, :], tb[s][r, :], ALU.add).then_inc(u_rot, 1)

            def finish(u):
                i, r = place[u], rows(u)
                dve.wait_ge(u_hi, i + 1)
                out, hi = sl[i % NST][r, :].bitcast(F32R), sh[i % NST][r, :]
                if u in ropes:
                    dve.wait_ge(u_rot, ropes.index(u) + 1)
                    nc.vector.tensor_tensor(out, ta[ropes.index(u) % 3][r, :], hi, ALU.subtract).then_inc(u_lo, 1)
                else:
                    nc.vector.scalar_tensor_tensor(out=out, in0=bank_of(u), in1=hi, op0=ALU.mult, op1=ALU.subtract,
                                                   scalar=scale if units[u][0] == "q" else 1.0).then_inc(u_lo, 1)

            def chunk(c):
                for u in range(n_units):
                    if units[u][2] == c:
                        if u in ropes:
                            i = ropes.index(u)
                            r = rows(u)
                            dve.wait_ge(u_raw, i + 1)
                            nc.vector.stream_shuffle(tb[i % 3][r, :], ta[i % 3][r, :], SWAP16).then_inc(u_sw, 1)
                        if u - (LAG - 1) in ropes:
                            rotate(u - (LAG - 1))
                        if u not in ropes:
                            finish(u)
                        if u - LAG in ropes:
                            finish(u - LAG)

            normalise(0)
            normalise(1)
            chunk(0)
            normalise(2)
            chunk(1)
            chunk(2)



def attention(nc, ar, tag, A, heads, unroll, load_a, load_b, n_a, n_b, KQ, o_head0, S, biased=False):
    stacked = KQ == HD
    KA = KQ + AUG
    NP, NS = SEQ // P, DEC // P
    LAG = 3
    NU = 2 * NP + NS
    MAXES = {3: (0, 1), 4: (2, 3), 5: (4, 5, 6), 6: (7, 8, 9), 7: (10, 11, 12), 8: (13, 14, 15),
             9: (16, 17, 18, 19)}
    HI_V = [0] if biased else [0, 1, 2]
    HI_S = [s for s in range(10) if s not in HI_V]
    LO_P = [1, 3, 5, 6, 7, 8, 9]
    LO_V = [s for s in range(10) if s not in LO_P]
    in_a = [ar.sem(f"{tag}_in_a{i}") for i in range(2)]
    in_b = [ar.sem(f"{tag}_in_b{i}") for i in range(2)]
    const_in, const_set = ar.sem(f"{tag}_const_in"), ar.sem(f"{tag}_const_set")
    s_ready = ar.sem(f"{tag}_s_ready")
    e_done = ar.sem(f"{tag}_e_done")
    p_hi_v, p_hi_s = ar.sem(f"{tag}_p_hi_v"), ar.sem(f"{tag}_p_hi_s")
    p_lo_v, p_lo_p = ar.sem(f"{tag}_p_lo_v"), ar.sem(f"{tag}_p_lo_p")
    pv_done = ar.sem(f"{tag}_pv_done")
    m_ready, m_done = ar.sem(f"{tag}_m_ready"), ar.sem(f"{tag}_m_done")
    m_both = ar.sem(f"{tag}_m_both")
    mt_ready, aug_done = ar.sem(f"{tag}_mt"), ar.sem(f"{tag}_aug")
    o_prompt, o_sample = ar.sem(f"{tag}_o_prompt"), ar.sem(f"{tag}_o_sample")
    o_stored = [ar.sem(f"{tag}_o_stored{i}") for i in range(2)]
    if biased:
        b_hi, b_sum, b_lo = ar.sem(f"{tag}_b_hi"), ar.sem(f"{tag}_b_sum"), ar.sem(f"{tag}_b_lo")
        m_seen = ar.sem(f"{tag}_m_seen")
    with ar.scope() as sc:
        KS = P if stacked else KQ
        Q1 = [sc.sb(f"{tag}_Q1{i}", [P, T], F32R) for i in range(2)]
        K2 = [sc.sb(f"{tag}_K2{i}", [P, T], F32R) for i in range(2)]
        Q3 = [sc.sb(f"{tag}_Q3{i}", [P, T], F32R) for i in range(2)]
        K3 = [sc.sb(f"{tag}_K3{i}", [P, T], F32R) for i in range(2)]
        VH = [sc.sb(f"{tag}_VH{i}", [P, TT, HD + 2], F32R) for i in range(2)]
        VL = [sc.sb(f"{tag}_VL{i}", [P, TT, HD + 2], F32R) for i in range(2)]
        PF = [sc.sb(f"{tag}_PF{i}", [P, 2 * CH]) for i in range(4)]
        PH = [sc.sb(f"{tag}_PH{i}", [P, 2 * CH], F32R) for i in range(4)]
        PL = [sc.sb(f"{tag}_PL{i}", [P, 2 * CH], F32R) for i in range(4)]
        OB = [sc.sb(f"{tag}_OB{i}", [HD + 1, T]) for i in range(2)]
        MH = sc.sb(f"{tag}_MH", [P, NP, 2])
        M = sc.sb(f"{tag}_M", [P, 2 * AUG])
        ident = sc.sb(f"{tag}_ident", [P, P])
        negsel = sc.sb(f"{tag}_negsel", [AUG, AUG, P])
        if biased:
            identr = sc.sb(f"{tag}_identr", [P, P], F32R)
            BD, BL_ = sc.sb(f"{tag}_BD", [P, BW]), sc.sb(f"{tag}_BL", [P, BW])
            slope = sc.sb(f"{tag}_slope", [P, 8])
            BF = sc.sb(f"{tag}_BF", [P, BW])
            BS = sc.sb(f"{tag}_BS", [P, 2 * CH])
            Bhi = [sc.sb(f"{tag}_Bhi{i}", [P, BW], F32R) for i in range(2)]
            Blo = [sc.sb(f"{tag}_Blo{i}", [P, BW], F32R) for i in range(2)]
        SA = sc.banks(f"{tag}_SA", 2)
        SM = sc.banks(f"{tag}_SM", 2)
        OP = sc.banks(f"{tag}_OP", 2)
        OS = sc.banks(f"{tag}_OS", 1)
        MT = sc.banks(f"{tag}_MT", 1)
        block = sc.enter_context(nc.Block())
        bufs = [dict(Q1=Q1[i], K2=K2[i], Q3=Q3[i], K3=K3[i], VH=VH[i], VL=VL[i]) for i in range(2)]
        NIT = heads // unroll
        n_const = 5 if biased else 2
        n_set = 8 if biased else 7

        def head_of(i, j):
            return i * unroll + j, j % 2, i * (unroll // 2) + j // 2

        def hi_count(h, s):
            a, sem_ = (HI_V, p_hi_v) if s in HI_V else (HI_S, p_hi_s)
            return sem_, h * len(a) + (a.index(s) + 1)

        def lo_count(h, s):
            a, sem_ = (LO_V, p_lo_v) if s in LO_V else (LO_P, p_lo_p)
            return sem_, h * len(a) + (a.index(s) + 1)

        @block.sync
        def _(sp):
            for dst, src in [(ident[:], A["ident"]), (negsel[:], A["negsel"])] + (
                    [(BD[:], A["bias_dist"]), (BL_[:], A["bias_count"]), (slope[:], A["slopes"])] if biased else []):
                sp.dma_start(dst, src).then_inc(const_in, 16)

            def load(h, b, i, j):
                wait_count(sp, s_ready, h * 10 - 10)
                wait_count(sp, m_done, h * NU - NU)
                for dst, src in load_a(h, i, j, bufs[b]):
                    sp.dma_start(dst.bitcast(F32), src).then_inc(in_a[b], 16)
                wait_count(sp, pv_done, h * 10 - 10)
                for dst, src in load_b(h, i, j, bufs[b]):
                    sp.dma_start(dst.bitcast(F32), src).then_inc(in_b[b], 16)

            load(0, 0, 0, 0)
            load(1, 1, 0, 1)

            def body(i, first, last):
                for j in range(unroll):
                    h, b, _ = head_of(i, j)
                    if not (last and j >= unroll - 2):
                        load(h + 2, b, i + (j + 2) // unroll, (j + 2) % unroll)
                    sp.wait_ge(o_sample, h + 1)
                    sp.dma_start(S["O"][ds(h * HD + o_head0 * HD, HD), :], OB[b][0:HD, :]).then_inc(o_stored[b], 16)
                    sp.dma_start(S["Z"][ds(h + o_head0, 1), :], OB[b][HD:HD + 1, :]).then_inc(o_stored[b], 16)
            steps(sp, NIT, body)
            for b in range(2):
                sp.wait_ge(o_stored[b], 32 * (heads // 2))

        @block.tensor
        def _(pe):
            def max_unit(h, b, fills, u):
                if u == 0:
                    pe.wait_ge(in_a[b], fills * 16 * n_a + 16 * n_a)
                wait_count(pe, m_done, h * NU + (u - 1))
                q, k = (Q1[b][:], K2[b][:]) if stacked else (Q1[b][0:KQ, :], K3[b][0:KQ, :])
                if u < 2 * NP:
                    q0, k0 = (u // 2) * P, (u % 2) * CH
                else:
                    q0, k0 = SEQ + (u - 2 * NP) * P, SEQ
                nc.tensor.matmul(SM[:, (u % 2) * CH:(u % 2 + 1) * CH], q[:, q0:q0 + P], k[:, k0:k0 + CH],
                                 start=True, stop=True).then_inc(m_ready, 1)

            def transpose_max(h, sample):
                if sample:
                    pe.wait_ge(m_done, h * NU + NU)
                else:
                    pe.wait_ge(m_both, h + 1)
                wait_count(pe, aug_done, h * 2 + sample)
                nc.tensor.matmul(MT[0:AUG, 0:P], M[:, sample * AUG:(sample + 1) * AUG], ident[:],
                                 start=True, stop=True).then_inc(mt_ready, 1)

            def scores(h, b, fills, s, g):
                if s == 0:
                    pe.wait_ge(in_b[b], fills * 16 * n_b + 16 * n_b)
                    pe.wait_ge(aug_done, h * 2 + 1)
                    if biased:
                        pe.wait_ge(b_lo, h + 1)
                if s == NP:
                    pe.wait_ge(aug_done, h * 2 + 2)
                wait_count(pe, e_done, g)
                for x in range(2):
                    out = SA[:, x * CH:(x + 1) * CH]
                    if s < NP:
                        q0, k0, base = x * CH, s * P, 0
                    else:
                        q0, k0, base = SEQ, SEQ + (2 * (s - NP) + x) * P, SEQ
                    qs, ks = slice(q0, q0 + CH), slice(k0, k0 + P)
                    mms = [(K2[b][0:KS, ks], Q1[b][0:KS, qs], None), (K3[b][0:KA, ks], Q3[b][0:KA, qs], None)]
                    if not stacked:
                        mms.insert(0, (K3[b][0:KQ, ks], Q1[b][0:KQ, qs], None))
                    if biased:
                        off = q0 - k0 + BW - SEQ
                        mms.insert(1, (identr[:], Bhi[b][:, off:off + CH], None))
                        n0, n1 = max(0, k0 - q0 - 256), min(CH, k0 - q0 + P + 256)
                        if n0 < n1:
                            mms.insert(2, (identr[:], Blo[b][:, off + n0:off + n1], (n0, n1)))
                    for i, (w, y, part) in enumerate(mms):
                        o = out if part is None else out[:, part[0]:part[1]]
                        mm = nc.tensor.matmul(o, w, y, start=(i == 0), stop=(i == len(mms) - 1),
                                              skip_group_check=biased)
                mm.then_inc(s_ready, 1)

            def pv(h, b, s, g, p, between=None):
                if s == 0:
                    wait_count(pe, o_prompt, h)
                if s == NP:
                    wait_count(pe, o_sample, h)
                pe.wait_ge(*hi_count(h, s))
                pe.wait_ge(*lo_count(h, s))
                for x in range(2):
                    pc = slice(x * CH, (x + 1) * CH)
                    if s < NP:
                        kt, out, st, en = s, OP[0:HD + 1, pc], s == 0, s == NP - 1
                    else:
                        kt, out = NP + 2 * (s - NP) + x, OS[0:HD + 1, :]
                        st, en = (s == NP and x == 0), (s == NP + 1 and x == 1)
                    for i, (w, y) in enumerate(((VH, PH), (VL, PH), (VH, PL))):
                        mm = nc.tensor.matmul(out, w[b][:, kt, 0:HD + 1], y[p][:, pc],
                                              start=(st and i == 0), stop=(en and i == 2))
                    if x == 0 and between is not None:
                        max_unit(*between)
                mm.then_inc(pv_done, 1)

            pe.wait_ge(const_in, 16 * n_const)
            pe.wait_ge(const_set, n_set)
            for u in range(NU):
                max_unit(0, 0, 0, u)
            transpose_max(0, 0)

            def body(i, first, last):
                for j in range(unroll):
                    h, b, fills = head_of(i, j)
                    hn, bn, fn = head_of(i, j + 1)
                    final = last and j == unroll - 1
                    for s in range(10):
                        scores(h, b, fills, s, h * 10 + s)
                        if s == 0:
                            transpose_max(h, 1)
                        if s == 9 and not final:
                            transpose_max(hn, 0)
                        units = MAXES.get(s, ()) if not final else ()
                        lead = len(units) - 2
                        for u in units[:max(lead, 0)]:
                            max_unit(hn, bn, fn, u)
                        between = (hn, bn, fn, units[max(lead, 0)]) if units else None
                        if s >= LAG:
                            pv(h, b, s - LAG, h * 10 + s - LAG, (j * 10 + s - LAG) % 4, between)
                        elif not (first and j == 0):
                            pv(h - 1, 1 - b, s + 10 - LAG, h * 10 + s - LAG, (j * 10 + s - LAG) % 4)
                        for u in units[max(lead, 0) + 1:]:
                            max_unit(hn, bn, fn, u)
                if last:
                    for s in range(10 - LAG, 10):
                        pv(h, b, s, h * 10 + s, (j * 10 + s) % 4)
            steps(pe, NIT, body)

        @block.scalar
        def _(act):
            if biased:
                act.wait_ge(const_in, 16 * n_const)
                nc.scalar.activation(identr[:], ident[:], ACT.Copy).then_inc(const_set, 1)

            def evac_prompt(h, b, fills):
                wait_count(act, o_stored[b], fills * 32)
                act.wait_ge(pv_done, h * 10 + NP)
                nc.scalar.activation(OB[b][:, 0:SEQ], OP[0:HD + 1, :], ACT.Copy).then_inc(o_prompt, 1)

            def evac_sample(h, b):
                act.wait_ge(pv_done, h * 10 + 10)
                act.wait_ge(o_prompt, h + 1)
                nc.scalar.activation(OB[b][:, SEQ:T], OS[0:HD + 1, :], ACT.Copy).then_inc(o_sample, 1)

            def body(i, first, last):
                for j in range(unroll):
                    h, b, fills = head_of(i, j)
                    for s in range(10):
                        g, p = h * 10 + s, (j * 10 + s) % 4
                        act.wait_ge(s_ready, g + 1)
                        wait_count(act, pv_done, g - 3)
                        nc.scalar.activation(PF[p][:], SA[:], ACT.Exp).then_inc(e_done, 1)
                        if s in HI_S:
                            act.wait_ge(e_done, g + 1)
                            nc.scalar.activation(PH[p][:], PF[p][:], ACT.Copy).then_inc(p_hi_s, 1)
                        if s == 1 and not (first and j == 0):
                            evac_prompt(h - 1, 1 - b, i * (unroll // 2) + (j - 1) // 2)
                        if s == 3 and not (first and j == 0):
                            evac_sample(h - 1, 1 - b)
                if last:
                    evac_prompt(h, b, fills)
                    evac_sample(h, b)
            steps(act, NIT, body)

        @block.vector
        def _(dve):
            for b in range(2):
                nc.vector.memset(K3[b][KQ:KA, :].bitcast(F32), 1.0).then_inc(const_set, 1)
                nc.vector.memset(VH[b][:, :, HD:HD + 1].bitcast(F32), 1.0).then_inc(const_set, 1)
                nc.vector.memset(VL[b][:, :, HD:HD + 1].bitcast(F32), 0.0).then_inc(const_set, 1)
            nc.vector.memset(M[:], 0.0).then_inc(const_set, 1)
            dve.wait_ge(const_in, 16 * n_const)
            dve.wait_ge(const_set, n_set)

            def bias(h, b):
                wait_count(dve, s_ready, h * 10 - 10)
                nc.vector.scalar_tensor_tensor(out=Bhi[b][:], in0=BD[:], scalar=slope[:, ds(h, 1)], in1=BL_[:],
                                               op0=ALU.mult, op1=ALU.add).then_inc(b_hi, 1)

            def bias_full(h):
                wait_count(dve, b_lo, h)
                nc.vector.scalar_tensor_tensor(out=BF[:], in0=BD[:], scalar=slope[:, ds(h, 1)], in1=BL_[:],
                                               op0=ALU.mult, op1=ALU.add).then_inc(b_sum, 1)

            def maximum(h, b, u):
                x = u % 2
                src = SM[:, x * CH:(x + 1) * CH]
                qi = u // 2 if u < 2 * NP else u - 2 * NP
                dst = MH[:, qi, x:x + 1] if u < 2 * NP else M[:, AUG + qi:AUG + qi + 1]
                if not biased:
                    dve.wait_ge(m_ready, h * NU + (u + 1))
                    nc.vector.reduce_max(dst, src, axis=AX_X).then_inc(m_done, 1)
                else:
                    off = BW - SEQ - qi * P + (x * CH if u < 2 * NP else 0)
                    if u == 0:
                        dve.wait_ge(b_hi, h + 1)
                    wait_apart(dve, m_ready, h * NU + (u + 1), m_seen)
                    nc.vector.tensor_tensor_reduce(
                        out=BS[:, x * CH:(x + 1) * CH], in0=src, in1=Bhi[b][:, off:off + CH].bitcast(F32), scale=1.0,
                        scalar=-3.0e38, op0=ALU.add, op1=ALU.max, accum_out=dst).then_inc(m_done, 1)
                if u == 2 * NP - 1:
                    dve.wait_ge(m_done, h * NU + 2 * NP)
                    nc.vector.tensor_tensor(M[:, 0:NP], MH[:, :, 0], MH[:, :, 1], ALU.max).then_inc(m_both, 1)

            def augment(h, b, sample):
                dve.wait_ge(mt_ready, h * 2 + sample + 1)
                wait_count(dve, s_ready, h * 10 - 10)
                nt = NS if sample else NP
                t0 = SEQ if sample else 0
                nc.vector.tensor_tensor(
                    Q3[b][KQ:KA, t0:t0 + nt * P].rearrange("r (i n) -> r i n", n=P),
                    MT[0:AUG, 0:P].unsqueeze(1).to_broadcast([AUG, nt, P]), negsel[:, 0:nt, :], ALU.mult
                ).then_inc(aug_done, 1)

            def low(h, s, g, p):
                dve.wait_ge(*hi_count(h, s))
                nc.vector.tensor_tensor(PL[p][:], PF[p][:], PH[p][:].bitcast(F32), ALU.subtract).then_inc(p_lo_v, 1)

            if biased:
                bias(0, 0)
                bias_full(0)
            for u in range(NU):
                maximum(0, 0, u)
            augment(0, 0, 0)

            def body(i, first, last):
                for j in range(unroll):
                    h, b, fills = head_of(i, j)
                    hn, bn, _ = head_of(i, j + 1)
                    final = last and j == unroll - 1
                    for s in range(10):
                        g, p = h * 10 + s, (j * 10 + s) % 4
                        if s == 0:
                            augment(h, b, 1)
                        if s in HI_V:
                            dve.wait_ge(e_done, g + 1)
                            nc.vector.tensor_copy(PH[p][:], PF[p][:]).then_inc(p_hi_v, 1)
                        if s == 9 and not final:
                            augment(hn, bn, 0)
                        units = MAXES.get(s, ()) if not final else ()
                        for u in units[0:1]:
                            maximum(hn, bn, u)
                        if s - 1 in LO_V:
                            low(h, s - 1, g - 1, (p - 1) % 4)
                        if s == 1 and biased and not final:
                            bias(hn, bn)
                        if s == 2 and biased and not final:
                            bias_full(hn)
                        for u in units[1:]:
                            maximum(hn, bn, u)
            steps(dve, NIT, body)

        @block.gpsimd
        def _(pool):
            def bias_low(h, b):
                pool.wait_ge(b_hi, h + 1)
                pool.wait_ge(b_sum, h + 1)
                nc.gpsimd.tensor_tensor(Blo[b][:], BF[:], Bhi[b][:].bitcast(F32), ALU.subtract).then_inc(b_lo, 1)

            if biased:
                bias_low(0, 0)

            def body(i, first, last):
                for j in range(unroll):
                    h, b, _ = head_of(i, j)
                    hn, bn, _ = head_of(i, j + 1)
                    if biased and not (last and j == unroll - 1):
                        bias_low(hn, bn)
                    for s in LO_P:
                        p = (j * 10 + s) % 4
                        pool.wait_ge(*hi_count(h, s))
                        nc.gpsimd.tensor_tensor(PL[p][:], PF[p][:], PH[p][:].bitcast(F32), ALU.subtract
                                                ).then_inc(p_lo_p, 1)
            steps(pool, NIT, body)



def output_projection(nc, ar, l, S, A, Y, rstd_next, gpost, ones, epst, xin, xout):
    tag = f"o{l}"
    nxt = rstd_next is not None
    row0 = 16 * l
    NB = 5
    N = 16 * T // P
    z_in, z_rcp, z_hi, z_lo, z_out = (ar.sem(f"{tag}_z_{n}") for n in ("in", "rcp", "hi", "lo", "out"))
    rz_in, sel_in, sel_set = ar.sem(f"{tag}_rz_in"), ar.sem(f"{tag}_sel_in"), ar.sem(f"{tag}_sel_set")
    w_in = [ar.sem(f"{tag}_w_in{t}") for t in range(KT)]
    w_hi, w_lo = ar.sem(f"{tag}_w_hi"), ar.sem(f"{tag}_w_lo")
    o_in = [ar.sem(f"{tag}_o_in{n}") for n in ("0a", "0b", "1", "2")]
    g_in = [ar.sem(f"{tag}_g_in{i}") for i in range(2)]
    r_ready = ar.sem(f"{tag}_r_ready")
    o_div, o_gated = ar.sem(f"{tag}_o_div"), ar.sem(f"{tag}_o_gated")
    x_hi, x_lo = ar.sem(f"{tag}_x_hi"), ar.sem(f"{tag}_x_lo")
    acc_ready, y_sq, y_added = ar.sem(f"{tag}_acc_ready"), ar.sem(f"{tag}_y_sq"), ar.sem(f"{tag}_y_added")
    y_raw = ar.sem(f"{tag}_y_raw")
    sum_ready, sd_ready = ar.sem(f"{tag}_sum_ready"), ar.sem(f"{tag}_sd_ready")
    rstd_ready, next_ready = ar.sem(f"{tag}_rstd_ready"), ar.sem(f"{tag}_next_ready")
    res_in = [ar.sem(f"{tag}_res_in{i}") for i in range(2)]
    y_scaled, y_ready, y_out = ar.sem(f"{tag}_y_scaled"), ar.sem(f"{tag}_y_ready"), ar.sem(f"{tag}_y_out")
    n_sq, n_added = ar.sem(f"{tag}_n_sq"), ar.sem(f"{tag}_n_added")
    sums_order = [("y", 0), ("y", 1), ("n", 0), ("y", 2), ("n", 1), ("n", 2)] if nxt else [("y", c) for c in range(NC)]
    YF, YR = Y
    with ar.scope() as sc:
        WH = sc.sb(f"{tag}_WH", [P, KT, D], F32R)
        WF, WL = sc.both(f"{tag}_WL", [P, KT, D])
        XH = [sc.sb(f"{tag}_XH{i}", [P, KT, CH], F32R) for i in range(2)]
        EF, ER = sc.both(f"{tag}_extra", [P, KT, CH])
        G = [sc.sb(f"{tag}_G{i}", [P, CH]) for i in range(2)]
        R = [sc.sb(f"{tag}_res{i}", [P, CH]) for i in range(2)]
        sq = [sc.sb(f"{tag}_sq{i}", [P, CH]) for i in range(2)]
        sq_sum = sc.sb(f"{tag}_sq_sum", [P, CH])
        rstd = sc.sb(f"{tag}_rstd", [P, CH])
        RZ = sc.sb(f"{tag}_RZ", [32, T], F32R)
        sel = sc.sb(f"{tag}_sel", [32, D], F32R)
        z, zh, zl = sc.sb(f"{tag}_z", [P, N]), sc.sb(f"{tag}_zh", [P, N], F32R), sc.sb(f"{tag}_zl", [P, N], F32R)
        if nxt:
            nsq, nsq_sum = sc.sb(f"{tag}_nsq", [P, CH]), sc.sb(f"{tag}_nsq_sum", [P, CH])
        acc = sc.banks(f"{tag}_acc", NB)
        rb = sc.banks(f"{tag}_rb", 2)
        sums = sc.banks(f"{tag}_sums", 1)
        block = sc.enter_context(nc.Block())

        def cols(c):
            return slice(c * CH, (c + 1) * CH)

        def low(c, as_f32r=False):
            if c == NC - 1:
                return (ER if as_f32r else EF)[:]
            return (YR if as_f32r else YF)[:, :, cols(c + 1)]

        def stages():
            for period in range(-1, NC + 2 if nxt else NC + 1):
                g, a, p, x = (c if 0 <= c < NC else None for c in (period + 1, period, period - 1, period - 2))
                for t in range(KT + 2):
                    live = t < KT
                    yield (period, t, g if live else None, a if live else None, p, x if live and nxt else None)

        @block.sync
        def _(sp):
            def flat(x):
                return x[row0:row0 + 16, :].rearrange("h (a n) -> (h a) n", n=N)

            def load_o(i, c, k0, k1):
                sp.dma_start(low(c)[:, k0:k1, :],
                             S["O"][row0 * HD:row0 * HD + D, cols(c)].rearrange("(k p) t -> p k t", p=P)[:, k0:k1, :]
                             ).then_inc(o_in[i], 16)

            def load_gate(n):
                c, k = n // KT, n % KT
                sp.dma_start(G[n % 2][:], S[f"gate{l}"][k * P:(k + 1) * P, cols(c)]).then_inc(g_in[n % 2], 16)

            def load_w(t):
                sp.dma_start(WF[:, t, :], A[f"w_out{l}"][t]).then_inc(w_in[t], 16)

            def load_res(m):
                c, k = m // KT, m % KT
                sp.dma_start(R[m % 2][:], xin[k * P:(k + 1) * P, cols(c)]).then_inc(res_in[m % 2], 16)

            def store(m):
                c, k = m // KT, m % KT
                sp.dma_start(xout[k * P:(k + 2) * P, cols(c)].rearrange("(k p) t -> p k t", p=P),
                             YF[:, k:k + 2, cols(c)]).then_inc(y_out, 16)

            sp.dma_start(z[:], flat(S["Z"])).then_inc(z_in, 16)
            load_o(0, 0, 0, KT // 2)
            sp.dma_start(YF[0:32, 0:2, 0:CH], A["denominator_rows"].rearrange("r (a n) -> r a n", n=CH)
                         ).then_inc(sel_in, 16)
            load_gate(0)
            load_gate(1)
            sp.wait_ge(z_hi, 1)
            sp.dma_start(flat(S["RZ", "hi"]), zh[:].bitcast(F32)).then_inc(z_out, 16)
            sp.wait_ge(z_lo, 1)
            sp.dma_start(flat(S["RZ", "lo"]), zl[:].bitcast(F32)).then_inc(z_out, 16)
            load_o(1, 0, KT // 2, KT)
            load_w(0)
            sp.wait_ge(z_out, 32)
            for i, part in enumerate(("hi", "lo")):
                sp.dma_start(RZ[16 * i:16 * i + 16, :].bitcast(F32), S["RZ", part][row0:row0 + 16, :]
                             ).then_inc(rz_in, 16)
            load_w(1)
            for period, t, g, a, p, x in stages():
                if g is not None:
                    n = g * KT + t
                    sp.wait_ge(o_gated, n + 1)
                    if n + 2 < NC * KT:
                        load_gate(n + 2)
                if period == -1 and t + 2 < KT:
                    load_w(t + 2)
                if period == -1 and t == KT:
                    load_o(2, 1, 0, KT)
                    load_res(0)
                    load_o(3, 2, 0, KT)
                if p is not None and t >= 2:
                    m = p * KT + t - 2
                    wait_count(sp, y_ready, m)
                    if m + 1 < NC * KT:
                        load_res(m + 1)
                    if m % 2 == 0 and m > 0:
                        store(m - 2)
            sp.wait_ge(y_ready, NC * KT)
            store(NC * KT - 2)
            sp.wait_ge(y_out, 16 * NC * KT // 2)

        @block.gpsimd
        def _(pool):
            for t in range(KT):
                pool.wait_ge(w_hi, t + 1)
                nc.gpsimd.tensor_tensor(WL[:, t, :], WF[:, t, :], WH[:, t, :].bitcast(F32), ALU.subtract
                                        ).then_inc(w_lo, 1)
            if nxt:
                for c in range(NC):
                    for k in range(1, KT):
                        pool.wait_ge(n_sq, c * KT + k + 1)
                        wait_count(pool, n_added, c * (KT - 1) + k - 1)
                        nc.gpsimd.tensor_tensor(nsq_sum[:], nsq_sum[:], nsq[:], ALU.add).then_inc(n_added, 1)

        @block.tensor
        def _(pe):
            def square_sum(kind, c):
                i = sums_order.index((kind, c))
                wait_count(pe, sd_ready, i)
                pe.wait_ge(y_added if kind == "y" else n_added, (c + 1) * (KT - 1))
                nc.tensor.matmul(sums[:], ones[:], (sq_sum if kind == "y" else nsq_sum)[:], start=True, stop=True
                                 ).then_inc(sum_ready, 1)

            pe.wait_ge(sel_set, 1)
            pe.wait_ge(rz_in, 32)
            for period, t, g, a, p, x in stages():
                if g is not None:
                    n = g * KT + t
                    wait_count(pe, o_div, n - 1)
                    nc.tensor.matmul(rb[:, cols(n % 2)], sel[:, t * P:(t + 1) * P], RZ[:, cols(g)], start=True,
                                     stop=True).then_inc(r_ready, 1)
                if a is not None:
                    n = a * KT + t
                    if t == 0:
                        pe.wait_ge(x_lo, (a + 1) * KT)
                    if a == 0:
                        pe.wait_ge(w_lo, t + 1)
                    wait_count(pe, y_sq, n - NB + 1)
                    for k in range(KT):
                        ks = slice(k * P, (k + 1) * P)
                        xh, xl = XH[a % 2][:, k, :], low(a, True)[:, k, :]
                        for j, (w, y) in enumerate(((WH, xh), (WH, xl), (WL, xh))):
                            mm = nc.tensor.matmul(acc[:, cols(n % NB)], w[:, t, ks], y, start=(k + j == 0),
                                                  stop=(k == KT - 1 and j == 2))
                    mm.then_inc(acc_ready, 1)
                if t == 0 and p is not None:
                    square_sum("y", p)
                if t == 4 and x is not None:
                    square_sum("n", x)

        @block.scalar
        def _(act):
            def high_weights(t):
                act.wait_ge(w_in[t], 16)
                nc.scalar.activation(WH[:, t, :], WF[:, t, :], ACT.Copy).then_inc(w_hi, 1)

            def deviation(kind, c):
                act.wait_ge(sum_ready, sums_order.index((kind, c)) + 1)
                if kind == "y":
                    wait_count(act, y_ready, c * KT)
                out = rstd[:] if kind == "y" else rstd_next[:, cols(c)]
                nc.scalar.activation(out, sums[:], ACT.Sqrt, bias=epst[:], scale=1.0 / D).then_inc(sd_ready, 1)

            act.wait_ge(z_rcp, 1)
            nc.scalar.activation(zh[:], z[:], ACT.Copy).then_inc(z_hi, 1)
            act.wait_ge(sel_in, 16)
            nc.scalar.activation(sel[:].rearrange("r (a n) -> r a n", n=CH), YF[0:32, 0:2, 0:CH], ACT.Copy
                                 ).then_inc(sel_set, 1)
            for period, t, g, a, p, x in stages():
                if period == 0 and t < KT - 2:
                    high_weights(t + 2)
                if g is not None:
                    act.wait_ge(o_gated, g * KT + t + 1)
                    wait_count(act, acc_ready, (g - 1) * KT)
                    nc.scalar.activation(XH[g % 2][:, t, :], low(g)[:, t, :], ACT.Copy).then_inc(x_hi, 1)
                if period == -1 and t in (KT - 2, KT - 1):
                    high_weights(t - (KT - 2))
                if p is not None and t >= 2 and nxt:
                    k = t - 2
                    act.wait_ge(y_ready, p * KT + k + 1)
                    wait_count(act, n_added, p * (KT - 1) + max(k - 1, 0))
                    if k == 0 and p > 0:
                        act.wait_ge(sum_ready, sums_order.index(("n", p - 1)) + 1)
                    nc.scalar.activation((nsq if k else nsq_sum)[:], YF[:, k, cols(p)], ACT.Square
                                         ).then_inc(n_sq, 1)
                if a is not None:
                    n = a * KT + t
                    act.wait_ge(acc_ready, n + 1)
                    nc.scalar.activation(YF[:, t, cols(a)], acc[:, cols(n % NB)], ACT.Copy).then_inc(y_raw, 1)
                    wait_count(act, y_added, a * (KT - 1) + max(t - 2, 0))
                    if t == 0 and a > 0:
                        act.wait_ge(sum_ready, sums_order.index(("y", a - 1)) + 1)
                    nc.scalar.activation((sq[t % 2] if t else sq_sum)[:], acc[:, cols(n % NB)], ACT.Square
                                         ).then_inc(y_sq, 1)
                if t == 0 and p is not None:
                    deviation("y", p)
                if t == 4 and x is not None:
                    deviation("n", x)

        @block.vector
        def _(dve):
            def low_part(n):
                c, k = n // KT, n % KT
                dve.wait_ge(x_hi, n + 1)
                nc.vector.tensor_tensor(low(c, True)[:, k, :], low(c)[:, k, :], XH[c % 2][:, k, :].bitcast(F32),
                                        ALU.subtract).then_inc(x_lo, 1)

            dve.wait_ge(z_in, 16)
            nc.vector.reciprocal(z[:], z[:]).then_inc(z_rcp, 1)
            dve.wait_ge(z_hi, 1)
            nc.vector.tensor_tensor(zl[:], z[:], zh[:].bitcast(F32), ALU.subtract).then_inc(z_lo, 1)
            for period, t, g, a, p, x in stages():
                if g is not None:
                    n = g * KT + t
                    x_ = low(g)[:, t, :]
                    if t == 0 or n == KT // 2:
                        dve.wait_ge(o_in[(0 if t == 0 else 1) if g == 0 else g + 1], 16)
                    dve.wait_ge(r_ready, n + 1)
                    nc.vector.tensor_tensor(x_, x_, rb[:, cols(n % 2)], ALU.mult).then_inc(o_div, 1)
                    dve.wait_ge(o_div, n + 1)
                    dve.wait_ge(g_in[n % 2], 16 * (n // 2 + 1))
                    nc.vector.tensor_tensor(x_, x_, G[n % 2][:], ALU.mult).then_inc(o_gated, 1)
                    if t > 0:
                        low_part(n - 1)
                    if t == KT - 1:
                        low_part(n)
                if t == 1 and p is not None:
                    dve.wait_ge(sd_ready, sums_order.index(("y", p)) + 1)
                    nc.vector.reciprocal(rstd[:], rstd[:]).then_inc(rstd_ready, 1)
                    dve.wait_ge(rstd_ready, p + 1)
                if p is not None and t >= 2:
                    m = p * KT + t - 2
                    y = YF[:, t - 2, cols(p)]
                    nc.vector.tensor_tensor(y, y, rstd[:], ALU.mult).then_inc(y_scaled, 1)
                    dve.wait_ge(y_scaled, m + 1)
                    dve.wait_ge(res_in[m % 2], 16 * (m // 2 + 1))
                    nc.vector.scalar_tensor_tensor(out=y, in0=y, scalar=gpost[:, t - 2:t - 1], in1=R[m % 2][:],
                                                   op0=ALU.mult, op1=ALU.add).then_inc(y_ready, 1)
                if t == 5 and x is not None:
                    dve.wait_ge(sd_ready, sums_order.index(("n", x)) + 1)
                    nc.vector.reciprocal(rstd_next[:, cols(x)], rstd_next[:, cols(x)]).then_inc(next_ready, 1)
                if a is not None and t > 0:
                    dve.wait_ge(y_sq, a * KT + t + 1)
                    wait_count(dve, y_added, a * (KT - 1) + t - 1)
                    nc.vector.tensor_tensor(sq_sum[:], sq_sum[:], sq[t % 2][:], ALU.add).then_inc(y_added, 1)



def build_trunk(nc, A):
    ar = Arena(nc)

    def scratch(name, shape):
        return nc.dram_tensor(name, shape, F32, kind="Internal").ap()

    S = {"O": scratch("att_out", [32 * HD, T]),
         "Z": scratch("att_den", [32, T]),
         ("RZ", "hi"): scratch("att_rden_hi", [32, T]),
         ("RZ", "lo"): scratch("att_rden_lo", [32, T]),
         "X1": scratch("x_mid", [D, T]),
         "gate0": scratch("silu_gate0", [D, T]), "gate1": scratch("silu_gate1", [D, T])}
    for part in ("hi", "lo"):
        for name, shape in (("qA", [512, T]), ("kA", [512, T]), ("vA", [8, P, TT, HD]),
                            ("qB", [512, T]), ("qrB", [256, T]), ("kB", [512, T]), ("krB", [ROPE, T]), ("vB", [8, P, TT, HD]),
                            ("qC", [1024, T]), ("kC", [256, T]), ("vC", [4, P, TT, HD])):
            S[name, part] = scratch(f"{name}_{part}", shape)

    with ar.scope() as sc:
        ones = sc.sb("ones", [P, P])
        epst = sc.sb("epst", [P, 1])
        gpre = [sc.sb(f"gpre{l}", [P, KT]) for l in range(2)]
        gpost = [sc.sb(f"gpost{l}", [P, KT]) for l in range(2)]
        set_up(nc, ar, ones, epst, gpre, gpost, A)

        consts = (ones, epst, A)

        with ar.scope() as s1:
            latent = s1.both("latent", [P, 4, T])
            with ar.scope() as s2:
                XH = s2.sb("XH0", [P, KT, T], F32R)
                project(nc, ar, "p0", (XH, *s2.both("XL0", [P, KT, T])), s2.sb("rstd0", [P, T]), A["w_tiles0"],
                        gpre[0],
                        [("keep", 0, 4, {"out": latent[0]}),
                         ("split", 4, 4, {"hi": S["qA", "hi"], "lo": S["qA", "lo"], "scale": HD ** -0.5}),
                         ("split", 8, 4, {"hi": S["kA", "hi"], "lo": S["kA", "lo"]}),
                         ("gate", 12, 8, {"out": S["gate0"]})],
                        {"w": A["wv0"], "heads": 8, "hi": S["vA", "hi"], "lo": S["vA", "lo"]}, consts, src=A["xT"])
            latent_projections(nc, ar, S, A, latent, ones, epst)

        def per_head(name, part, h, n):
            return S[name, part][ds(h * n, n), :]

        def values_of(name, part, h):
            return S[name, part][ds(h, 1), :, :, :].rearrange("a p i d -> (a p) i d")

        def load_v(name, h, B):
            return [(B["VH"][:, :, 0:HD], values_of(name, "hi", h)), (B["VL"][:, :, 0:HD], values_of(name, "lo", h))]

        attention(nc, ar, "a", A, 8, 2,
                  lambda h, i, j, B: [(B["Q1"][0:HD, :], per_head("qA", "hi", h, HD)),
                                      (B["Q1"][HD:P, :], per_head("qA", "hi", h, HD)),
                                      (B["K2"][0:HD, :], per_head("kA", "hi", h, HD)),
                                      (B["K2"][HD:P, :], per_head("kA", "lo", h, HD))],
                  lambda h, i, j, B: [(B["Q3"][0:HD, :], per_head("qA", "lo", h, HD)),
                                      (B["K3"][0:HD, :], per_head("kA", "hi", h, HD))] + load_v("vA", h, B),
                  4, 4, HD, 0, S, biased=True)
        attention(nc, ar, "b", A, 8, 2,
                  lambda h, i, j, B: [(B["Q1"][0:HD, :], per_head("qB", "hi", h, HD)),
                                      (B["Q1"][HD:96, :], per_head("qrB", "hi", h, ROPE)),
                                      (B["K3"][0:HD, :], per_head("kB", "hi", h, HD)),
                                      (B["K3"][HD:96, :], S["krB", "hi"])],
                  lambda h, i, j, B: [(B["K2"][0:HD, :], per_head("kB", "lo", h, HD)),
                                      (B["K2"][HD:96, :], S["krB", "lo"]),
                                      (B["Q3"][0:HD, :], per_head("qB", "lo", h, HD)),
                                      (B["Q3"][HD:96, :], per_head("qrB", "lo", h, ROPE))] + load_v("vB", h, B),
                  4, 6, 96, 8, S)

        ar.recycle()

        with ar.scope() as s1:
            Y = s1.both("Y0", [P, KT, T])
            rstd = s1.sb("rstd1", [P, T])
            output_projection(nc, ar, 0, S, A, Y, rstd, gpost[0], ones, epst, A["xT"], S["X1"])
            project(nc, ar, "p1", (s1.sb("XH1", [P, KT, T], F32R), *Y), rstd, A["w_tiles1"], gpre[1],
                    [("qk", 0, 8, {"hi": S["qC", "hi"], "lo": S["qC", "lo"], "cos": "cos_q", "sin": "sin_q"}),
                     ("qk", 8, 2, {"hi": S["kC", "hi"], "lo": S["kC", "lo"], "cos": "cos_k", "sin": "sin_k"}),
                     ("gate", 10, 8, {"out": S["gate1"]})],
                    {"w": A["wv1"], "heads": 4, "hi": S["vC", "hi"], "lo": S["vC", "lo"]}, consts,
                    tabs={"cos_q": ["cosC", None], "sin_q": ["sinC", None],
                          "cos_k": ["cosC", None], "sin_k": ["sinC", None]})
        attention(nc, ar, "c", A, 16, 4,
                  lambda h, i, j, B: [(B["Q1"][0:HD, :], per_head("qC", "hi", h, HD)),
                                      (B["Q1"][HD:P, :], per_head("qC", "hi", h, HD)),
                                      (B["K2"][0:HD, :], per_head("kC", "hi", i, HD)),
                                      (B["K2"][HD:P, :], per_head("kC", "lo", i, HD))],
                  lambda h, i, j, B: [(B["Q3"][0:HD, :], per_head("qC", "lo", h, HD)),
                                      (B["K3"][0:HD, :], per_head("kC", "hi", i, HD))] + load_v("vC", i, B),
                  4, 4, HD, 16, S)
        with ar.scope() as s1:
            output_projection(nc, ar, 1, S, A, s1.both("Y1", [P, KT, T]), None, gpost[1], ones, epst, S["X1"], A["yT"])


def set_up(nc, ar, ones, epst, gpre, gpost, A):
    g_in, c_set = ar.sem("g_in"), ar.sem("c_set")
    with nc.Block() as block:
        @block.sync
        def _(sp):
            for l in range(2):
                sp.dma_start(gpre[l][:], A["gpre"][l]).then_inc(g_in, 16)
                sp.dma_start(gpost[l][:], A["gpost"][l]).then_inc(g_in, 16)
            sp.wait_ge(g_in, 64)

        @block.vector
        def _(dve):
            nc.vector.memset(ones[:], 1.0).then_inc(c_set, 1)
            nc.vector.memset(epst[:], EPS).then_inc(c_set, 1)
            dve.wait_ge(c_set, 2)



def shape_constants():
    import numpy as np
    half = ROPE // 2
    freq = (np.float32(10000.0) ** (-np.arange(half, dtype=np.float32) / np.float32(half))).astype(np.float32)
    r = np.arange(P)
    sign = np.where(r % ROPE < half, -1.0, 1.0).astype(np.float32)[:, None]

    def tables(pos):
        ang = (pos * freq[r % half][:, None]).astype(np.float32)
        return np.cos(ang).astype(np.float32), (np.sin(ang) * sign).astype(np.float32)

    t = np.arange(SEQ, dtype=np.float32)[None, :]
    c = {}
    c["cosB"], c["sinB"] = tables(np.broadcast_to(t, (P, SEQ)))
    axial = np.where((r[:, None] // ROPE) % 2 == 0, np.floor(t / 64), t % 64).astype(np.float32)
    c["cosC"], c["sinC"] = tables(axial)
    c["headsel"] = (r[:, None] // HD == r[None, :] // HD).astype(np.float32)
    c["denominator_rows"] = (np.arange(D)[None, :] // HD == np.arange(32)[:, None] % 16).astype(np.float32)
    c["ident"] = np.eye(P, dtype=np.float32)
    c["negsel"] = np.ascontiguousarray(np.broadcast_to(-np.eye(AUG, dtype=np.float32)[:, :, None], (AUG, AUG, P)))
    off = np.abs(np.arange(BW)[None, :] - (BW - SEQ) - r[:, None])
    held = (off <= 64).astype(int) + ((off % 4 == 0) & (off <= 256)) + ((off % 16 == 0) & (off <= 1024))
    c["bias_dist"] = np.where(held > 0, -off.astype(np.float64), -1e30).astype(np.float32)
    c["bias_count"] = np.where(held > 0, np.log(np.maximum(held, 1).astype(np.float64)), 0.0).astype(np.float32)
    c["slopes"] = np.ascontiguousarray(np.broadcast_to(2.0 ** -np.arange(1, 9, dtype=np.float32), (P, 8)))
    return c


def kernel(x_prompt, x_sample, norm_pre, norm_post, w_in_ab, mla_q_norm, w_uq, mla_kv_norm, w_ukv,
           w_out_ab, w_in_c, c_q_norm, c_k_norm, w_out_c):
    import numpy as np
    import concourse.bacc as bacc
    from concourse.bass_utils import run_bass_kernel_spmd

    def feature_tiles(w):
        return w.reshape(KT, P, -1, P).transpose(2, 1, 0, 3).reshape(-1, P, D)

    def value_units(w):
        return w.reshape(KT // 2, 2, P, -1).transpose(0, 2, 1, 3).reshape(KT // 2, P, -1)

    def columns(g):
        return g.reshape(-1, P).T

    w0, w1 = np.asarray(w_in_ab)[0], np.asarray(w_in_c)[0]
    kr = w0[:, 1920:1952]
    cols0 = np.concatenate([w0[:, 1536:1920], kr, kr, kr, kr, w0[:, 0:1024], w0[:, 1952:2976]], axis=1)
    cols1 = np.concatenate([w1[:, 0:1280], w1[:, 1536:2560]], axis=1)
    wq = np.asarray(w_uq)[0].reshape(2 * P, 8, HD + ROPE)
    wk = np.asarray(w_ukv)[0].reshape(P, 8, 2, HD)
    gq, gk = np.asarray(c_q_norm)[0], np.asarray(c_k_norm)[0]
    swap = np.arange(HD) // 32 * 32 + (np.arange(HD) + 16) % 32
    arrays = {
        "xT": np.concatenate([np.asarray(x_prompt)[0].T, np.asarray(x_sample)[0].T], axis=1),
        "w_tiles0": feature_tiles(cols0), "wv0": value_units(w0[:, 1024:1536]),
        "w_tiles1": feature_tiles(cols1), "wv1": value_units(w1[:, 1280:1536]),
        "w_out0": feature_tiles(np.asarray(w_out_ab)[0]), "w_out1": feature_tiles(np.asarray(w_out_c)[0]),
        "w_uq": np.concatenate([wq[:, :, 0:HD].reshape(2 * P, 512), wq[:, :, HD:].reshape(2 * P, 256)], axis=1),
        "w_ukv": np.concatenate([wk[:, :, 0].reshape(P, 512), wk[:, :, 1].reshape(P, 512)], axis=1),
        "gpre": np.stack([columns(g) for g in np.asarray(norm_pre)]),
        "gpost": np.stack([columns(g) for g in np.asarray(norm_post)]),
        "g_lat": np.concatenate([columns(np.asarray(mla_q_norm)[0]), columns(np.asarray(mla_kv_norm)[0])], axis=1),
        "g_heads": np.stack([np.concatenate([g, g]) for g in (gq, gq[swap], gk, gk[swap])], axis=1),
    }
    arrays.update(shape_constants())
    arrays = {k: np.ascontiguousarray(v) for k, v in arrays.items()}
    nc = bacc.Bacc("TRN2", target_bir_lowering=False, num_devices=1)
    A = {k: nc.dram_tensor(f"in_{k}", v.shape, mybir.dt.from_np(v.dtype), kind="ExternalInput").ap()
         for k, v in arrays.items()}
    A["yT"] = nc.dram_tensor("yT", (D, T), F32, kind="ExternalOutput").ap()
    build_trunk(nc, A)
    r = run_bass_kernel_spmd(nc, [{f"in_{k}": v for k, v in arrays.items()}], core_ids=[0])
    y = r.results[0]["yT"]
    return (np.ascontiguousarray(y[:, 0:SEQ].T)[None], np.ascontiguousarray(y[:, SEQ:T].T)[None])
```
